# Optimizing a Trainium2 kernel written in Bass

```python
import math
import jax, jax.numpy as jnp
from jax import lax
import numpy as np

D_MODEL = 1024
BATCH = 1
SEQ = 1024
DEPTH = 1
DEC_BATCH = 1
DEC_SEQ = 64
PAST_LEN = 2048

CHUNK = 64
Q_BLOCK = 128
MIX_WIDTH = D_MODEL
DIFF_WIDTH = MIX_WIDTH // 2
SB_WIDTH = MIX_WIDTH - DIFF_WIDTH
DIFF_HEADS = 4
DIFF_QK_DIM = 64
DIFF_V_DIM = DIFF_WIDTH // DIFF_HEADS
DIFF_QK_WIDTH = DIFF_HEADS * 2 * DIFF_QK_DIM
SB_HEADS = 8
SB_HEAD_DIM = SB_WIDTH // SB_HEADS
IN_WIDTH = 2 * DIFF_QK_WIDTH + DIFF_WIDTH + 3 * SB_WIDTH
D_FF = -(-8 * D_MODEL // (3 * 256)) * 256
RMS_EPS = 1e-6
NEG_INF = -1e30

kernel_name = 'hymba_diff_stickbreak_stream_step'

def _rms_norm(x, g):
    xf = x.astype(jnp.float32)
    y = xf * lax.rsqrt(jnp.mean(xf * xf, axis=-1, keepdims=True) + RMS_EPS)
    return (y * g.astype(jnp.float32)).astype(x.dtype)

def _alibi_slopes():
    return jnp.exp2(-8.0 / DIFF_HEADS * jnp.arange(1, DIFF_HEADS + 1, dtype=jnp.float32))

def _lambda_init(layer):
    return 0.8 - 0.6 * math.exp(-0.3 * layer)

def _project(n, w_in):
    B, T, _ = n.shape
    qkv = n @ w_in.astype(n.dtype)
    o1 = DIFF_QK_WIDTH
    o2 = o1 + DIFF_QK_WIDTH
    o3 = o2 + DIFF_WIDTH
    o4 = o3 + SB_WIDTH
    o5 = o4 + SB_WIDTH
    qd = qkv[..., :o1].reshape(B, T, DIFF_HEADS, 2 * DIFF_QK_DIM)
    kd = qkv[..., o1:o2].reshape(B, T, DIFF_HEADS, 2 * DIFF_QK_DIM)
    vd = qkv[..., o2:o3].reshape(B, T, DIFF_HEADS, DIFF_V_DIM)
    qs = qkv[..., o3:o4].reshape(B, T, SB_HEADS, SB_HEAD_DIM)
    ks = qkv[..., o4:o5].reshape(B, T, SB_HEADS, SB_HEAD_DIM)
    vs = qkv[..., o5:].reshape(B, T, SB_HEADS, SB_HEAD_DIM)
    return qd, kd, vd, qs, ks, vs

def _diff_attention(q, k, v, q_pos, k_pos, lam, lam_init, subln_g):
    B, Tq = q.shape[0], q.shape[1]
    Tk = k.shape[1]
    qf = q.astype(jnp.float32).reshape(B, Tq, DIFF_HEADS, 2, DIFF_QK_DIM)
    kf = k.astype(jnp.float32).reshape(B, Tk, DIFF_HEADS, 2, DIFF_QK_DIM)
    s = jnp.einsum('bqhmd,bkhmd->bhmqk', qf, kf) * (DIFF_QK_DIM ** -0.5)
    dist = jnp.abs(q_pos[:, None] - k_pos[None, :]).astype(jnp.float32)
    bias = -_alibi_slopes()[:, None, None] * dist
    visible = (k_pos[None, :] // CHUNK) <= (q_pos[:, None] // CHUNK)
    s = jnp.where(visible, s + bias[None, :, None], NEG_INF)
    p = jax.nn.softmax(s, axis=-1)
    a = p[:, :, 0] - lam * p[:, :, 1]
    o = jnp.einsum('bhqk,bkhd->bqhd', a, v.astype(jnp.float32))
    o = o * lax.rsqrt(jnp.mean(o * o, axis=-1, keepdims=True) + RMS_EPS)
    o = o * subln_g.astype(jnp.float32) * (1.0 - lam_init)
    return o.reshape(B, Tq, DIFF_WIDTH)

def _stick_breaking(q, k, v, q_pos, k_pos):
    B, Tq = q.shape[0], q.shape[1]
    z = jnp.einsum('bqhd,bkhd->bhqk', q.astype(jnp.float32), k.astype(jnp.float32)) * (SB_HEAD_DIM ** -0.5)
    causal = k_pos[None, :] < q_pos[:, None]
    log_keep = jnp.where(causal, jax.nn.log_sigmoid(-z), 0.0)
    after = lax.cumsum(log_keep, axis=3, reverse=True) - log_keep
    a = jnp.where(causal, jnp.exp(jax.nn.log_sigmoid(z) + after), 0.0)
    o = jnp.einsum('bhqk,bkhd->bqhd', a, v.astype(jnp.float32))
    return o.reshape(B, Tq, SB_WIDTH)

def _swiglu(h, g, w_gate, w_up, w_down):
    n = _rms_norm(h, g)
    dt = n.dtype
    return (jax.nn.silu(n @ w_gate.astype(dt)) * (n @ w_up.astype(dt))) @ w_down.astype(dt)

def setup_inputs(seed: int = 0) -> dict:
    key = jax.random.key(seed)
    ks = jax.random.split(key, 20)
    f32 = jnp.float32
    nrm = lambda k, shape, scale: jax.random.normal(k, shape, f32) * scale
    return {
        'x_prompt': nrm(ks[0], (BATCH, SEQ, D_MODEL), 1.0),
        'x_sample': nrm(ks[1], (DEC_BATCH, DEC_SEQ, D_MODEL), 1.0),
        'cache_diff_k': nrm(ks[2], (DEPTH, DEC_BATCH, PAST_LEN, DIFF_HEADS, 2 * DIFF_QK_DIM), 1.0),
        'cache_diff_v': nrm(ks[3], (DEPTH, DEC_BATCH, PAST_LEN, DIFF_HEADS, DIFF_V_DIM), 1.0),
        'cache_sb_k': nrm(ks[4], (DEPTH, DEC_BATCH, PAST_LEN, SB_HEADS, SB_HEAD_DIM), 1.0),
        'cache_sb_v': nrm(ks[5], (DEPTH, DEC_BATCH, PAST_LEN, SB_HEADS, SB_HEAD_DIM), 1.0),
        'norm_attn_g': 1.0 + nrm(ks[6], (DEPTH, D_MODEL), 0.02),
        'w_in': nrm(ks[7], (DEPTH, D_MODEL, IN_WIDTH), D_MODEL ** -0.5),
        'lambda_q1': nrm(ks[8], (DEPTH, DIFF_QK_DIM), 0.1),
        'lambda_k1': nrm(ks[9], (DEPTH, DIFF_QK_DIM), 0.1),
        'lambda_q2': nrm(ks[10], (DEPTH, DIFF_QK_DIM), 0.1),
        'lambda_k2': nrm(ks[11], (DEPTH, DIFF_QK_DIM), 0.1),
        'diff_subln_g': 1.0 + nrm(ks[12], (DEPTH, DIFF_V_DIM), 0.02),
        'w_out': nrm(ks[13], (DEPTH, MIX_WIDTH, D_MODEL), MIX_WIDTH ** -0.5),
        'norm_ffn_g': 1.0 + nrm(ks[14], (DEPTH, D_MODEL), 0.02),
        'w_gate': nrm(ks[15], (DEPTH, D_MODEL, D_FF), D_MODEL ** -0.5),
        'w_up': nrm(ks[16], (DEPTH, D_MODEL, D_FF), D_MODEL ** -0.5),
        'w_down': nrm(ks[17], (DEPTH, D_FF, D_MODEL), D_FF ** -0.5),
        'norm_final_g': 1.0 + nrm(ks[18], (D_MODEL,), 0.02),
    }

def reference(x_prompt, x_sample, cache_diff_k, cache_diff_v, cache_sb_k, cache_sb_v,
              norm_attn_g, w_in, lambda_q1, lambda_k1, lambda_q2, lambda_k2, diff_subln_g,
              w_out, norm_ffn_g, w_gate, w_up, w_down, norm_final_g):
    xp = x_prompt
    xs = x_sample
    pos_prompt = jnp.arange(SEQ, dtype=jnp.int32)
    dec_seq = x_sample.shape[1]
    pos_sample_q = PAST_LEN + jnp.arange(dec_seq, dtype=jnp.int32)
    pos_sample_k = jnp.arange(PAST_LEN + dec_seq, dtype=jnp.int32)
    p_dk, p_dv, p_sk, p_sv = [], [], [], []
    s_dk, s_dv, s_sk, s_sv = [], [], [], []
    for l in range(DEPTH):
        lam_init = _lambda_init(l)
        lam = (jnp.exp(jnp.sum(lambda_q1[l].astype(jnp.float32) * lambda_k1[l].astype(jnp.float32)))
               - jnp.exp(jnp.sum(lambda_q2[l].astype(jnp.float32) * lambda_k2[l].astype(jnp.float32)))
               + lam_init)

        n = _rms_norm(xp, norm_attn_g[l])
        qd, kd, vd, qs, ks_, vs = _project(n, w_in[l])

        def prompt_block(b):
            start = b * Q_BLOCK
            qpos = start + jnp.arange(Q_BLOCK, dtype=jnp.int32)
            qd_b = lax.dynamic_slice_in_dim(qd, start, Q_BLOCK, axis=1)
            qs_b = lax.dynamic_slice_in_dim(qs, start, Q_BLOCK, axis=1)
            od = _diff_attention(qd_b, kd, vd, qpos, pos_prompt, lam, lam_init, diff_subln_g[l])
            osb = _stick_breaking(qs_b, ks_, vs, qpos, pos_prompt)
            return jnp.concatenate([od, osb], axis=-1)

        blocks = lax.map(prompt_block, jnp.arange(SEQ // Q_BLOCK, dtype=jnp.int32))
        mixed = jnp.transpose(blocks, (1, 0, 2, 3)).reshape(xp.shape[0], SEQ, MIX_WIDTH).astype(xp.dtype)
        hp = xp + mixed @ w_out[l].astype(xp.dtype)
        xp = hp + _swiglu(hp, norm_ffn_g[l], w_gate[l], w_up[l], w_down[l])
        p_dk.append(kd); p_dv.append(vd); p_sk.append(ks_); p_sv.append(vs)

        n = _rms_norm(xs, norm_attn_g[l])
        qd2, kd2, vd2, qs2, ks2, vs2 = _project(n, w_in[l])
        kd_all = jnp.concatenate([cache_diff_k[l].astype(kd2.dtype), kd2], axis=1)
        vd_all = jnp.concatenate([cache_diff_v[l].astype(vd2.dtype), vd2], axis=1)
        ks_all = jnp.concatenate([cache_sb_k[l].astype(ks2.dtype), ks2], axis=1)
        vs_all = jnp.concatenate([cache_sb_v[l].astype(vs2.dtype), vs2], axis=1)
        od = _diff_attention(qd2, kd_all, vd_all, pos_sample_q, pos_sample_k, lam, lam_init, diff_subln_g[l])
        osb = _stick_breaking(qs2, ks_all, vs_all, pos_sample_q, pos_sample_k)
        mixed_s = jnp.concatenate([od, osb], axis=-1).astype(xs.dtype)
        hs = xs + mixed_s @ w_out[l].astype(xs.dtype)
        xs = hs + _swiglu(hs, norm_ffn_g[l], w_gate[l], w_up[l], w_down[l])
        s_dk.append(kd2); s_dv.append(vd2); s_sk.append(ks2); s_sv.append(vs2)

    y_prompt = _rms_norm(xp, norm_final_g)
    y_sample = _rms_norm(xs, norm_final_g)
    prompt_diff_k = jnp.stack(p_dk)
    prompt_diff_v = jnp.stack(p_dv)
    prompt_sb_k = jnp.stack(p_sk)
    prompt_sb_v = jnp.stack(p_sv)
    sample_diff_k = jnp.stack(s_dk)
    sample_diff_v = jnp.stack(s_dv)
    sample_sb_k = jnp.stack(s_sk)
    sample_sb_v = jnp.stack(s_sv)
    return (y_prompt, y_sample, prompt_diff_k, prompt_diff_v, prompt_sb_k, prompt_sb_v,
            sample_diff_k, sample_diff_v, sample_sb_k, sample_sb_v)


_drawn_inputs = setup_inputs


def setup_inputs(seed=0):
    import zlib

    import numpy as np

    out = dict(_drawn_inputs(seed))
    spreads = {}
    factors = {'norm_attn_g': 2.734,
     'lambda_k1': 8.0,
     'lambda_q2': 8.0,
     'diff_subln_g': 6.046,
     'norm_ffn_g': 4.566,
     'norm_final_g': 8.402,
     'cache_diff_k': 8.0,
     'cache_diff_v': 8.0}
    for name, (base, spread) in spreads.items():
        noise = np.random.default_rng([zlib.crc32(name.encode()), seed]).standard_normal(out[name].shape)
        drawn = base * np.exp(spread * noise) if base else spread * noise
        out[name] = __import__('jax').numpy.asarray(drawn.astype(out[name].dtype))
    for name, factor in factors.items():
        out[name] = (out[name] * factor).astype(out[name].dtype)
    return out
```

```python
import math
from contextlib import ExitStack

import concourse.bass as bass
from concourse import mybir

F32 = mybir.dt.float32
F32R = mybir.dt.float32r
ALU = mybir.AluOpType
ACT = mybir.ActivationFunctionType
AX = mybir.AxisListType

P = 128
CHUNK = 64
EPS = 1e-6
NEG_INF = -1e30
LAM_INIT = 0.8 - 0.6 * math.exp(-0.3 * 0)
BANK = 512
SOFTPLUS_LINEAR = 40.0


def token_tiles(seq, dec):
    return [(i * P, P) for i in range(seq // P)] + [(seq, dec)]


def split_rows(tiles, prompt, sample, i):
    t0, n = tiles[i]
    return prompt[t0:t0 + n, :] if i < len(tiles) - 1 else sample[0:n, :]


def norm_rows_act(nc, act, src, junk, sumsq, done, count):
    if count:
        act.wait_ge(done, count)
    nc.scalar.activation(junk, src, ACT.Square, accum_out=sumsq).then_inc(done, 1)


def rstd_pool(nc, pool, ms, sumsq, rstd, neg_half, width, done, count):
    nc.gpsimd.tensor_scalar(ms, sumsq, 1.0 / width, EPS, ALU.mult, ALU.add).then_inc(done, 1)
    pool.wait_ge(done, 2 * count + 1)
    nc.gpsimd.tensor_tensor(rstd, ms, neg_half, ALU.pow).then_inc(done, 1)


def project(nc, t):
    tiles = token_tiles(t["seq"], t["dec"])
    NT, T = len(tiles), t["seq"] + t["dec"]
    D = t["x_prompt"].shape[1]
    KD = D // P
    NG = t["w_in"].shape[1] // BANK
    w_in = t["w_in"].rearrange("(k p) n -> p k n", p=P)
    with ExitStack() as ctx:
        def sbuf(name, shape, dtype=F32):
            return ctx.enter_context(nc.sbuf_tensor(name, shape, dtype))

        def psum(name, shape):
            return ctx.enter_context(nc.psum_tensor(name, shape, F32))

        def sem(name):
            return ctx.enter_context(nc.semaphore(name))

        x_sb = sbuf("x_sb", [P, 3, D])
        xn = sbuf("xn", [P, 2, D])
        squares = sbuf("squares", [P, D])
        g_sb = sbuf("g_sb", [P, D])
        sumsq = sbuf("sumsq", [P, NT])
        ms = sbuf("ms", [P, NT])
        rstd = sbuf("rstd", [P, NT])
        nT_hi = sbuf("nT_hi", [P, KD, T], F32R)
        nT_lo = sbuf("nT_lo", [P, KD, T], F32R)
        w_raw = sbuf("w_raw", [P, 2, KD, BANK])
        w_hi = [sbuf(f"w_hi{b}", [P, KD, BANK], F32R) for b in range(2)]
        w_lo = [sbuf(f"w_lo{b}", [P, KD, BANK], F32R) for b in range(2)]
        out_sb = sbuf("out_sb", [P, 4, BANK])
        ps_turn = psum("ps_turn", [P, 4, 4, P])
        ps_proj = psum("ps_proj", [P, 4, BANK])
        x_loaded = [sem(f"x_loaded{i}") for i in range(3)]
        w_loaded = [sem(f"w_loaded{i}") for i in range(2)]
        g_loaded = sem("g_loaded")
        squared = sem("squared")
        rstd_done = sem("rstd_done")
        normed = sem("normed")
        turned = sem("turned")
        n_hi = sem("n_hi")
        n_lo = sem("n_lo")
        w_hi_done = sem("w_hi_done")
        w_lo_done = sem("w_lo_done")
        projected = sem("projected")
        evacuated = sem("evacuated")
        stored = [sem(f"stored{i}") for i in range(4)]
        block = ctx.enter_context(nc.Block())

        @block.sync
        def _(sp):
            def load_w(g):
                if g >= 2:
                    sp.wait_ge(w_lo_done, KD * (g - 1))
                sp.dma_start(w_raw[:, g % 2], w_in[:, :, g * BANK:(g + 1) * BANK]).then_inc(w_loaded[g % 2], 16)

            for i in range(NT):
                n = tiles[i][1]
                if i >= 3:
                    sp.wait_ge(normed, i - 2)
                sp.dma_start(x_sb[0:n, i % 3], split_rows(tiles, t["x_prompt"], t["x_sample"], i)) \
                    .then_inc(x_loaded[i % 3], 16)
                if i == 0:
                    sp.dma_start(g_sb[:], t["norm_attn_g"].partition_broadcast(P)).then_inc(g_loaded, 16)
                if i in (0, 2):
                    load_w(i // 2)
            for g in range(2, NG):
                load_w(g)

        @block.gpsimd
        def _(pool):
            def split_w(g):
                for k in range(KD):
                    pool.wait_ge(w_hi_done, KD * g + k + 1)
                    if g >= 2 and k == 0:
                        pool.wait_ge(projected, NT * (g - 1))
                    nc.gpsimd.tensor_tensor(w_lo[g % 2][:, k], w_raw[:, g % 2, k],
                                            w_hi[g % 2][:, k].bitcast(F32), ALU.subtract).then_inc(w_lo_done, 1)

            for i in range(NT):
                n = tiles[i][1]
                pool.wait_ge(squared, i + 1)
                rstd_pool(nc, pool, ms[0:n, i:i + 1], sumsq[0:n, i:i + 1], rstd[0:n, i:i + 1],
                          t["neg_half"][0:n, 0:1], D, rstd_done, i)
                if i == 0:
                    split_w(0)
            for g in range(1, NG):
                split_w(g)

        @block.scalar
        def _(act):
            def square(i):
                n = tiles[i][1]
                act.wait_ge(x_loaded[i % 3], 16 * (i // 3 + 1))
                norm_rows_act(nc, act, x_sb[0:n, i % 3], squares[0:n], sumsq[0:n, i:i + 1], squared, i)

            def store(m):
                g, i = divmod(m, NT)
                n = tiles[i][1]
                act.wait_ge(evacuated, m + 1)
                dst = split_rows(tiles, *t["proj_out"][g], i)
                act.dma_start(dst, out_sb[0:n, m % 4]).then_inc(stored[m % 4], 16)

            def evacuate(m):
                n = tiles[m % NT][1]
                act.wait_ge(projected, m + 1)
                if m >= 4:
                    act.wait_ge(stored[m % 4], 16 * (m // 4))
                nc.scalar.copy(out_sb[0:n, m % 4], ps_proj[0:n, m % 4]).then_inc(evacuated, 1)
                if m >= 1:
                    store(m - 1)

            square(0)
            for i in range(NT):
                t0, n = tiles[i]
                if i + 1 < NT:
                    square(i + 1)
                for j in range(2):
                    q = 2 * i + j
                    act.wait_ge(turned, q + 1)
                    nc.scalar.copy(nT_hi[:, 4 * j:4 * j + 4, t0:t0 + n], ps_turn[:, q % 4, :, 0:n]).then_inc(n_hi, 1)
                if i >= 1:
                    evacuate(i - 1)
            for m in range(NT - 1, NG * NT):
                evacuate(m)
            store(NG * NT - 1)
            for s in range(4):
                act.wait_ge(stored[s], 16 * len(range(s, NG * NT, 4)))

        @block.vector
        def _(dve):
            def split_w(g):
                dve.wait_ge(w_loaded[g % 2], 16 * (g // 2 + 1))
                if g >= 2:
                    dve.wait_ge(projected, NT * (g - 1))
                for k in range(KD):
                    nc.vector.tensor_copy(w_hi[g % 2][:, k], w_raw[:, g % 2, k]).then_inc(w_hi_done, 1)

            def norm(i):
                n = tiles[i][1]
                dve.wait_ge(rstd_done, 2 * (i + 1))
                if i == 0:
                    dve.wait_ge(g_loaded, 16)
                if i >= 2:
                    dve.wait_ge(turned, 2 * (i - 1))
                nc.vector.scalar_tensor_tensor(xn[0:n, i % 2], x_sb[0:n, i % 3], rstd[0:n, i:i + 1], g_sb[0:n],
                                               ALU.mult, ALU.mult).then_inc(normed, 1)

            norm(0)
            split_w(0)
            for i in range(NT):
                t0, n = tiles[i]
                if i + 1 < NT:
                    norm(i + 1)
                for j in range(2):
                    q = 2 * i + j
                    dve.wait_ge(n_hi, q + 1)
                    nc.vector.tensor_tensor(nT_lo[:, 4 * j:4 * j + 4, t0:t0 + n], ps_turn[:, q % 4, :, 0:n],
                                            nT_hi[:, 4 * j:4 * j + 4, t0:t0 + n].bitcast(F32),
                                            ALU.subtract).then_inc(n_lo, 1)
            for g in range(1, NG):
                split_w(g)

        @block.tensor
        def _(pe):
            def turn(i):
                n = tiles[i][1]
                pe.wait_ge(normed, i + 1)
                for j in range(2):
                    q = 2 * i + j
                    if q >= 4:
                        pe.wait_ge(n_lo, q - 3)
                    for k in range(4):
                        c = (4 * j + k) * P
                        last = nc.tensor.transpose(ps_turn[:, q % 4, k, 0:n], xn[0:n, i % 2, c:c + P],
                                                   t["ident"][0:n, 0:n])
                    last.then_inc(turned, 1)

            turn(0)
            for g in range(NG):
                for i in range(NT):
                    if g == 0 and i + 1 < NT:
                        turn(i + 1)
                    t0, n = tiles[i]
                    m = g * NT + i
                    if g == 0:
                        pe.wait_ge(n_lo, 2 * (i + 1))
                    if m >= 4:
                        pe.wait_ge(evacuated, m - 3)
                    for k in range(KD):
                        if i == 0:
                            pe.wait_ge(w_lo_done, KD * g + k + 1)
                        a_hi, a_lo = nT_hi[:, k, t0:t0 + n], nT_lo[:, k, t0:t0 + n]
                        b_hi, b_lo = w_hi[g % 2][:, k], w_lo[g % 2][:, k]
                        out = ps_proj[0:n, m % 4]
                        nc.tensor.matmul(out, a_hi, b_hi, start=(k == 0), stop=False)
                        nc.tensor.matmul(out, a_hi, b_lo, start=False, stop=False)
                        last = nc.tensor.matmul(out, a_lo, b_hi, start=False, stop=(k == KD - 1))
                    last.then_inc(projected, 1)


def attend(nc, t):
    seq, dec, past = t["seq"], t["dec"], t["past"]
    NC = seq // CHUNK + 1
    NU, ND = 8, 4
    LIVE = past + dec
    NTASK = NU * NC
    VT = seq // P + -(-LIVE // P)
    QSCALE = 64 ** -0.5

    def keys(c):
        return CHUNK * (c + 1) if c < NC - 1 else LIVE

    def blocks(c):
        return [(b, min(P, keys(c) - b)) for b in range(0, keys(c), P)]

    def segments(c):
        return [(s, min(BANK, keys(c) - s)) for s in range(0, keys(c), BANK)]

    PP = 4 * P
    pieces = []
    for r in range(0, seq, PP):
        pieces += [("q", "new", r, PP, r // CHUNK), ("k", "new", r, PP, r), ("v", "new", r, PP, r // P)]
    pieces += [("q", "sample", 0, dec, NC - 1), ("k", "sample", 0, dec, seq + past),
               ("v", "sample", 0, dec, (seq + past) // P)]
    for r in range(0, past, PP):
        pieces += [("k", "cache", r, PP, seq + r), ("v", "cache", r, PP, (seq + r) // P)]
    NP = len(pieces)
    assert NP <= NC
    piece_of = {}
    turns = {}
    for u in range(NU):
        for j in range(NP):
            n = len(piece_of)
            piece_of[(u, j)] = n
            if pieces[j][0] != "v":
                turns[n] = len(turns)
    v_order = {n: s for s, n in enumerate(n for n in range(NU * NP) if n not in turns)}
    seg0, grp0 = [0], [0]
    for s in range(NTASK):
        seg0.append(seg0[-1] + len(segments(s % NC)))
        grp0.append(grp0[-1] + -(-len(blocks(s % NC)) // 4))
    RAW = 6
    TABLES = 13

    def source(u, kind, where):
        side = "d" if u < ND else "s"
        return t[f"{where}_{side}{kind}"][:, (u % ND) * P:(u % ND + 1) * P]

    with ExitStack() as ctx:
        def sbuf(name, shape, dtype=F32):
            return ctx.enter_context(nc.sbuf_tensor(name, shape, dtype))

        def psum(name, shape):
            return ctx.enter_context(nc.psum_tensor(name, shape, F32))

        def sem(name):
            return ctx.enter_context(nc.semaphore(name))

        kT_hi = [sbuf(f"kT_hi{b}", [P, seq + LIVE], F32R) for b in range(2)]
        kT_lo = [sbuf(f"kT_lo{b}", [P, seq + LIVE], F32R) for b in range(2)]
        v = [sbuf(f"v{b}", [P, VT, 2, P], F32R) for b in range(2)]
        qT_hi = [sbuf(f"qT_hi{b}", [P, NC, P], F32R) for b in range(2)]
        qT_lo = [sbuf(f"qT_lo{b}", [P, NC, P], F32R) for b in range(2)]
        raw = sbuf("raw", [P, RAW, 4, P])
        z = sbuf("z", [P, 2, LIVE])
        w = sbuf("w", [P, LIVE])
        aT_hi = sbuf("aT_hi", [P, 3, 4, P], F32R)
        aT_lo = sbuf("aT_lo", [P, 3, 4, P], F32R)
        bias = sbuf("bias", [P, LIVE])
        mask = sbuf("mask", [P, CHUNK])
        seg_max = sbuf("seg_max", [P, 2, 8])
        row_max = sbuf("row_max", [P, 2])
        neg_max = sbuf("neg_max", [P, 2])
        row_sum = sbuf("row_sum", [P, 2])
        inv_sum = sbuf("inv_sum", [P, 2])
        o_sb = sbuf("o_sb", [P, 4, P])
        ps_prep = psum("ps_prep", [P, 2, 4, P])
        ps_z = psum("ps_z", [P, 2, BANK])
        ps_aT = psum("ps_aT", [P, 2, 4, P])
        ps_o = psum("ps_o", [P, 2, BANK])
        raw_loaded = [sem(f"raw_loaded{i}") for i in range(6)]
        tables = sem("tables")
        bias_done = sem("bias_done")
        prep_turned = sem("prep_turned")
        prep_hi = sem("prep_hi")
        prep_lo = sem("prep_lo")
        v_hi = sem("v_hi")
        v_lo = sem("v_lo")
        scored = sem("scored")
        z_bulk = sem("z_bulk")
        z_diag = sem("z_diag")
        z_seg = sem("z_seg")
        front = sem("front")
        exp_done = sem("exp_done")
        kept = sem("kept")
        weights = sem("weights")
        chain = sem("chain")
        inv_done = sem("inv_done")
        a_turned = sem("a_turned")
        a_hi = sem("a_hi")
        a_lo = sem("a_lo")
        a_used = sem("a_used")
        max_done = sem("max_done")
        o_half = sem("o_half")
        o_done = sem("o_done")
        o_stored = [sem(f"o_stored{i}") for i in range(4)]
        block = ctx.enter_context(nc.Block())

        def kbase(c):
            return 0 if c < NC - 1 else seq

        def is_diff(s):
            return s // NC < ND

        def steps():
            for s in range(-NC, NTASK):
                u, j = divmod(s + NC, NC)
                yield s, (piece_of[(u, j)] if u < NU and j < NP else None)

        SB0 = ND * NC
        sb_seg0 = [max(0, seg0[s] - seg0[SB0]) if s >= SB0 else 0 for s in range(NTASK + 1)]

        def bulk_segments(c):
            return [(a, min(n, keys(c) - CHUNK - a)) for a, n in segments(c) if keys(c) - CHUNK > a]

        bulk0 = [0]
        for s in range(NTASK):
            bulk0.append(bulk0[-1] + (len(bulk_segments(s % NC)) if s >= SB0 else 0))

        @block.sync
        def _(sp):
            def load(n):
                u, j = divmod(n, NP)
                kind, where, r, rows, _ = pieces[j]
                if n >= RAW:
                    m = n - RAW
                    if m in turns:
                        sp.wait_ge(prep_turned, turns[m] + 1)
                    else:
                        sp.wait_ge(v_lo, v_order[m] + 1)
                src = source(u, kind, where)[r:r + rows, :]
                if rows >= P:
                    src = src.rearrange("(i p) n -> p i n", p=P)
                    sp.dma_start(raw[:, n % RAW, 0:rows // P], src).then_inc(raw_loaded[n % RAW], 16)
                else:
                    sp.dma_start(raw[0:rows, n % RAW, 0], src).then_inc(raw_loaded[n % RAW], 16)

            def store(s):
                u, c = divmod(s, NC)
                tok = c * CHUNK
                sp.wait_ge(o_done, s + 1)
                o = o_sb[:, s % 4]
                if u < ND:
                    sp.dma_start(t["mixed"][tok:tok + CHUNK, u * P:(u + 1) * P], o[0:CHUNK]) \
                        .then_inc(o_stored[s % 4], 16)
                    sp.dma_start(t["mixed1"][tok:tok + CHUNK, u * P:(u + 1) * P], o[CHUNK:P]) \
                        .then_inc(o_stored[s % 4], 16)
                else:
                    col = u * P
                    for h in range(2):
                        a = h * CHUNK
                        sp.dma_start(t["mixed"][tok:tok + CHUNK, col + a:col + a + CHUNK],
                                     o[a:a + CHUNK, a:a + CHUNK]).then_inc(o_stored[s % 4], 16)

            for n in range(RAW - 1):
                load(n)
            loaded = RAW - 1
            for s, piece in steps():
                if piece is not None and loaded < NU * NP:
                    load(loaded)
                    loaded += 1
                if s >= 1:
                    store(s - 1)
            store(NTASK - 1)
            for s in range(4):
                sp.wait_ge(o_stored[s], 32 * len(range(s, NTASK, 4)))

        @block.gpsimd
        def _(pool):
            made = 0
            for q in (qT_hi[0], qT_lo[0], qT_hi[1], qT_lo[1]):
                for a in (0, CHUNK):
                    off = q[a:a + CHUNK, :, CHUNK - a:P - a].bitcast(mybir.dt.uint32)
                    if made:
                        pool.wait_ge(tables, made)
                    nc.gpsimd.memset(off, 0).then_inc(tables, 1)
                    made += 1
            for a in (0, CHUNK):
                pool.wait_ge(tables, made)
                nc.gpsimd.iota(w[a:a + CHUNK], [[-1, LIVE]], base=past, channel_multiplier=1,
                               allow_small_or_imprecise_dtypes=True).then_inc(tables, 1)
                made += 1
            pool.wait_ge(tables, made)
            nc.gpsimd.memset(mask[:], 0.0).then_inc(tables, 1)
            made += 1
            for a in (0, CHUNK):
                pool.wait_ge(tables, made)
                nc.gpsimd.affine_select(out=mask[a:a + CHUNK], in_=mask[a:a + CHUNK], compare_op=ALU.is_gt,
                                        fill=NEG_INF, base=0, pattern=[[-1, CHUNK]],
                                        channel_multiplier=1).then_inc(tables, 1)
                made += 1
            assert made == TABLES
            pool.wait_ge(tables, made)
            for s, n in steps():
                if n is not None and n not in turns:
                    u, j = divmod(n, NP)
                    _, _, _, rows, place = pieces[j]
                    k, m = max(1, rows // P), min(P, rows)
                    pool.wait_ge(v_hi, v_order[n] + 1)
                    nc.gpsimd.tensor_tensor(v[u % 2][0:m, place:place + k, 1, :], raw[0:m, n % RAW, 0:k],
                                            v[u % 2][0:m, place:place + k, 0, :].bitcast(F32),
                                            ALU.subtract).then_inc(v_lo, 1)

        @block.scalar
        def _(act):
            def prep(s, n):
                u, j = divmod(n, NP)
                kind, _, _, rows, place = pieces[j]
                k, m = max(1, rows // P), min(P, rows)
                if u >= 2:
                    act.wait_ge(a_used, grp0[NC * (u - 1)])
                if kind == "v":
                    act.wait_ge(raw_loaded[n % RAW], 16 * (n // RAW + 1))
                    nc.scalar.copy(v[u % 2][0:m, place:place + k, 0, :], raw[0:m, n % RAW, 0:k]).then_inc(v_hi, 1)
                    return
                e = turns[n]
                act.wait_ge(prep_turned, e + 1)
                src = ps_prep[:, e % 2].rearrange("p a b -> p (a b)")
                if kind == "k":
                    nc.scalar.copy(kT_hi[u % 2][:, place:place + rows], src[:, 0:rows]).then_inc(prep_hi, 1)
                else:
                    ch = rows // CHUNK
                    srcq = src[:, 0:rows].rearrange("p (c q) -> p c q", q=CHUNK)
                    for a in (0, CHUNK):
                        last = nc.scalar.activation(qT_hi[u % 2][a:a + CHUNK, place:place + ch, a:a + CHUNK],
                                                    srcq[a:a + CHUNK], ACT.Copy, scale=QSCALE)
                    last.then_inc(prep_hi, 1)

            def copy_scores(s):
                for b, (a, n) in enumerate(bulk_segments(s % NC)):
                    act.wait_ge(scored, seg0[s] + b + 1)
                    if b == 0:
                        act.wait_ge(a_turned, grp0[s - 1])
                    nc.scalar.copy(z[:, s % 2, a:a + n], ps_z[:, (seg0[s] + b) % 2, 0:n]).then_inc(z_bulk, 1)

            def exponent(s):
                n = keys(s % NC)
                act.wait_ge(front, s + 1)
                if is_diff(s):
                    if s >= 2:
                        act.wait_ge(inv_done, s - 1)
                    nc.scalar.activation(z[:, s % 2, 0:n], z[:, s % 2, 0:n], ACT.Exp, bias=neg_max[:, s % 2:s % 2 + 1],
                                         accum_out=row_sum[:, s % 2:s % 2 + 1]).then_inc(weights, 1)
                else:
                    nc.scalar.activation(w[:, 0:n], w[:, 0:n], ACT.Exp).then_inc(exp_done, 1)
                    act.wait_ge(exp_done, s - SB0 + 1)
                    nc.scalar.activation(w[:, 0:n], w[:, 0:n], ACT.Ln, bias=1.0).then_inc(kept, 1)

            def weigh(s):
                n = keys(s % NC)
                act.wait_ge(chain, 3 * (s - SB0 + 1))
                nc.scalar.activation(z[:, s % 2, 0:n], z[:, s % 2, 0:n], ACT.Exp).then_inc(weights, 1)

            def evacuate(s):
                bl = blocks(s % NC)
                for g in range(0, len(bl), 4):
                    e = grp0[s] + g // 4
                    act.wait_ge(a_turned, e + 1)
                    if e >= 3:
                        act.wait_ge(a_used, e - 2)
                    full = [b for b in bl[g:g + 4] if b[1] == P]
                    part = [b for b in bl[g:g + 4] if b[1] < P]
                    f = len(full)
                    if f:
                        last = nc.scalar.copy(aT_hi[:, e % 3, 0:f], ps_aT[:, e % 2, 0:f])
                    if part:
                        m = part[0][1]
                        last = nc.scalar.copy(aT_hi[0:m, e % 3, f], ps_aT[0:m, e % 2, f])
                    last.then_inc(a_hi, 1)

            def left(s):
                act.wait_ge(a_used, grp0[s + 1])
                if s >= 4:
                    act.wait_ge(o_stored[s % 4], 32 * (s // 4))
                if is_diff(s):
                    act.wait_ge(inv_done, s + 1)
                    nc.scalar.activation(o_sb[:, s % 4], ps_o[:, s % 2, 0:P], ACT.Copy,
                                         scale=inv_sum[:, s % 2:s % 2 + 1]).then_inc(o_half, 1)
                else:
                    nc.scalar.copy(o_sb[:, s % 4], ps_o[:, s % 2, 0:P]).then_inc(o_half, 1)

            nc.scalar.preload_act_table_set("natural_log_exp_and_others")
            act.wait_ge(tables, TABLES)
            for s, n in steps():
                if n is not None:
                    prep(s, n)
                if s + 1 >= SB0 and s + 1 < NTASK:
                    copy_scores(s + 1)
                if s >= SB0:
                    weigh(s)
                if 0 <= s + 1 < NTASK:
                    exponent(s + 1)
                if s >= 1:
                    left(s - 1)
                if s >= 0:
                    evacuate(s)
            left(NTASK - 1)

        @block.vector
        def _(dve):
            def prep(s, n):
                if n not in turns:
                    return
                u, j = divmod(n, NP)
                kind, _, _, rows, place = pieces[j]
                e = turns[n]
                dve.wait_ge(prep_hi, e + 1)
                src = ps_prep[:, e % 2].rearrange("p a b -> p (a b)")
                if kind == "k":
                    nc.vector.tensor_tensor(kT_lo[u % 2][:, place:place + rows], src[:, 0:rows],
                                            kT_hi[u % 2][:, place:place + rows].bitcast(F32),
                                            ALU.subtract).then_inc(prep_lo, 1)
                else:
                    ch = rows // CHUNK
                    srcq = src[:, 0:rows].rearrange("p (c q) -> p c q", q=CHUNK)
                    for a in (0, CHUNK):
                        part = (slice(a, a + CHUNK), slice(place, place + ch), slice(a, a + CHUNK))
                        last = nc.vector.scalar_tensor_tensor(qT_lo[u % 2][part], srcq[a:a + CHUNK], QSCALE,
                                                              qT_hi[u % 2][part].bitcast(F32), ALU.mult,
                                                              ALU.subtract)
                    last.then_inc(prep_lo, 1)

            def keep(s):
                n = keys(s % NC)
                q = 3 * (s - SB0)
                zs, ws = z[:, s % 2, 0:n], w[:, 0:n]
                dve.wait_ge(kept, s - SB0 + 1)
                nc.vector.tensor_tensor(ws, zs, ws, ALU.max).then_inc(chain, 1)
                dve.wait_ge(chain, q + 1)
                nc.vector.tensor_tensor_scan(w[:, 0:n][:, ::-1], w[:, 0:n][:, ::-1], w[:, 0:n][:, ::-1], 0.0,
                                             ALU.add, ALU.bypass).then_inc(chain, 1)
                dve.wait_ge(chain, q + 2)
                nc.vector.tensor_tensor(zs, zs, ws, ALU.subtract).then_inc(chain, 1)

            def front_of(s):
                u, c = divmod(s, NC)
                n = keys(c)
                if is_diff(s):
                    if c == 0:
                        if u == 0:
                            dve.wait_ge(tables, TABLES)
                            nc.vector.scalar_tensor_tensor(bias[:], w[:], -1.0, w[:], ALU.mult,
                                                           ALU.min).then_inc(bias_done, 1)
                            dve.wait_ge(bias_done, 1)
                        nc.vector.tensor_scalar(bias[:], bias[:], 0.25, None, ALU.mult).then_inc(bias_done, 1)
                        dve.wait_ge(bias_done, u + 2)
                    if s >= 2:
                        dve.wait_ge(a_turned, grp0[s - 1])
                    if s >= 2:
                        dve.wait_ge(weights, s - 1)
                    for b, (a, m) in enumerate(segments(c)):
                        dve.wait_ge(scored, seg0[s] + b + 1)
                        off = LIVE - n + a
                        nc.vector.tensor_tensor_reduce(z[:, s % 2, a:a + m], ps_z[:, (seg0[s] + b) % 2, 0:m],
                                                       bias[:, off:off + m], 1.0, -3e38, ALU.add, ALU.max,
                                                       seg_max[:, s % 2, b:b + 1]).then_inc(z_seg, 1)
                    dve.wait_ge(z_seg, seg0[s + 1])
                    nc.vector.tensor_reduce(row_max[:, s % 2:s % 2 + 1], seg_max[:, s % 2, 0:len(segments(c))],
                                            AX.X, ALU.max).then_inc(max_done, 1)
                    dve.wait_ge(max_done, s + 1)
                    nc.vector.tensor_scalar(neg_max[:, s % 2:s % 2 + 1], row_max[:, s % 2:s % 2 + 1], -1.0, None,
                                            ALU.mult).then_inc(front, 1)
                else:
                    a, m = n - CHUNK, CHUNK
                    b = len(segments(c)) - 1
                    dve.wait_ge(scored, seg0[s + 1])
                    dve.wait_ge(a_turned, grp0[s - 1])
                    dve.wait_ge(z_bulk, bulk0[s + 1])
                    a0 = a - b * BANK
                    nc.vector.tensor_tensor(z[:, s % 2, a:n], ps_z[:, (seg0[s] + b) % 2, a0:a0 + m], mask[:],
                                            ALU.add).then_inc(z_diag, 1)
                    dve.wait_ge(z_diag, s - SB0 + 1)
                    nc.vector.tensor_scalar(w[:, 0:n], z[:, s % 2, 0:n], SOFTPLUS_LINEAR, None,
                                            ALU.min).then_inc(front, 1)

            def evacuate(s):
                bl = blocks(s % NC)
                if is_diff(s):
                    dve.wait_ge(weights, s + 1)
                    nc.vector.reciprocal(inv_sum[:, s % 2:s % 2 + 1], row_sum[:, s % 2:s % 2 + 1]).then_inc(inv_done, 1)
                for g in range(0, len(bl), 4):
                    e = grp0[s] + g // 4
                    dve.wait_ge(a_hi, e + 1)
                    full = [b for b in bl[g:g + 4] if b[1] == P]
                    part = [b for b in bl[g:g + 4] if b[1] < P]
                    f = len(full)
                    if f:
                        last = nc.vector.tensor_tensor(aT_lo[:, e % 3, 0:f], ps_aT[:, e % 2, 0:f],
                                                       aT_hi[:, e % 3, 0:f].bitcast(F32), ALU.subtract)
                    if part:
                        m = part[0][1]
                        last = nc.vector.tensor_tensor(aT_lo[0:m, e % 3, f], ps_aT[0:m, e % 2, f],
                                                       aT_hi[0:m, e % 3, f].bitcast(F32), ALU.subtract)
                    last.then_inc(a_lo, 1)

            def right(s):
                dve.wait_ge(o_half, s + 1)
                if is_diff(s):
                    nc.vector.scalar_tensor_tensor(o_sb[:, s % 4], ps_o[:, s % 2, P:2 * P],
                                                   inv_sum[:, s % 2:s % 2 + 1], o_sb[:, s % 4],
                                                   ALU.mult, ALU.add).then_inc(o_done, 1)
                else:
                    nc.vector.tensor_tensor(o_sb[:, s % 4], ps_o[:, s % 2, P:2 * P], o_sb[:, s % 4],
                                            ALU.add).then_inc(o_done, 1)

            for s, n in steps():
                if n is not None:
                    prep(s, n)
                if s >= SB0:
                    keep(s)
                if 0 <= s + 1 < NTASK:
                    front_of(s + 1)
                if s >= 1:
                    right(s - 1)
                if s >= 0:
                    evacuate(s)
            right(NTASK - 1)

        @block.tensor
        def _(pe):
            def prep(n):
                if n not in turns:
                    return
                u, j = divmod(n, NP)
                _, _, _, rows, _ = pieces[j]
                e = turns[n]
                pe.wait_ge(raw_loaded[n % RAW], 16 * (n // RAW + 1))
                if e >= 2:
                    pe.wait_ge(prep_lo, e - 1)
                for i in range(max(1, rows // P)):
                    m = min(P, rows)
                    last = nc.tensor.transpose(ps_prep[:, e % 2, i, 0:m], raw[0:m, n % RAW, i], t["ident"][0:m, 0:m])
                last.then_inc(prep_turned, 1)

            def score(s):
                u, c = divmod(s, NC)
                if c == 0:
                    pe.wait_ge(prep_lo, 1 + max(turns[n] for n in turns if n < NP * (u + 1)))
                    pe.wait_ge(v_lo, 1 + max(v_order[n] for n in v_order if n < NP * (u + 1)))
                q_hi, q_lo = qT_hi[u % 2][:, c], qT_lo[u % 2][:, c]
                for b, (a, m) in enumerate(segments(c)):
                    e = seg0[s] + b
                    if e >= 2:
                        r = next(x for x in range(s + 1) if seg0[x + 1] > e - 2)
                        rb = e - 2 - seg0[r]
                        if is_diff(r):
                            pe.wait_ge(z_seg, e - 1)
                        else:
                            nb = len(bulk_segments(r % NC))
                            if nb:
                                pe.wait_ge(z_bulk, bulk0[r] + min(rb + 1, nb))
                            if rb == len(segments(r % NC)) - 1:
                                pe.wait_ge(z_diag, r - SB0 + 1)
                    out = ps_z[:, e % 2, 0:m]
                    k0 = kbase(c) + a
                    k_hi, k_lo = kT_hi[u % 2][:, k0:k0 + m], kT_lo[u % 2][:, k0:k0 + m]
                    nc.tensor.matmul(out, q_hi, k_hi, start=True, stop=False)
                    nc.tensor.matmul(out, q_hi, k_lo, start=False, stop=False)
                    nc.tensor.matmul(out, q_lo, k_hi, start=False, stop=True).then_inc(scored, 1)

            def values(s, g):
                u, c = divmod(s, NC)
                bl = blocks(c)
                e = grp0[s] + g
                pe.wait_ge(a_lo, e + 1)
                for i, (b, m) in enumerate(bl[4 * g:4 * g + 4]):
                    tile = (kbase(c) + b) // P
                    rhs = v[u % 2][0:m, tile].rearrange("p a n -> p (a n)")
                    nc.tensor.matmul(ps_o[:, s % 2, 0:2 * P], aT_hi[0:m, e % 3, i], rhs, start=(b == 0), stop=False)
                    last = nc.tensor.matmul(ps_o[:, s % 2, 0:2 * P], aT_lo[0:m, e % 3, i], rhs,
                                            start=False, stop=(b == bl[-1][0]))
                last.then_inc(a_used, 1)

            def turn_and_use(s):
                bl = blocks(s % NC)
                G = -(-len(bl) // 4)
                pe.wait_ge(weights, s + 1)
                for g in range(G):
                    e = grp0[s] + g
                    if e >= 2:
                        pe.wait_ge(a_lo, e - 1)
                    for i, (b, m) in enumerate(bl[4 * g:4 * g + 4]):
                        last = nc.tensor.transpose(ps_aT[0:m, e % 2, i], z[:, s % 2, b:b + m], t["ident"][:, :])
                    last.then_inc(a_turned, 1)
                    if g >= 1:
                        values(s, g - 1)
                    if g == 0 and s >= 2:
                        pe.wait_ge(o_done, s - 1)
                values(s, G - 1)

            for s, n in steps():
                if n is not None:
                    prep(n)
                if 0 <= s + 1 < NTASK:
                    score(s + 1)
                if s >= 0:
                    turn_and_use(s)


def mix(nc, t, h_all):
    tiles = token_tiles(t["seq"], t["dec"])
    NT = len(tiles)
    D = t["x_prompt"].shape[1]
    KD = D // P
    DW = t["mixed1"].shape[1]
    NH = DW // P
    w_out = t["w_out"].rearrange("(k p) n -> p k n", p=P)
    with ExitStack() as ctx:
        def sbuf(name, shape, dtype=F32):
            return ctx.enter_context(nc.sbuf_tensor(name, shape, dtype))

        def psum(name, shape):
            return ctx.enter_context(nc.psum_tensor(name, shape, F32))

        def sem(name):
            return ctx.enter_context(nc.semaphore(name))

        m0 = sbuf("m0", [P, 2, D])
        m1 = sbuf("m1", [P, 2, DW])
        squares = sbuf("squares3", [P, DW])
        lambdas = sbuf("lambdas", [P, 4, 64])
        lam_prod = sbuf("lam_prod", [P, 2, 64])
        lam = sbuf("lam", [P, 8])
        subln = sbuf("subln", [P, P])
        head_sq = sbuf("head_sq", [P, NT, NH])
        head_ms = sbuf("head_ms", [P, NT, NH])
        head_rstd = sbuf("head_rstd", [P, NT, NH])
        wo_raw = sbuf("wo_raw", [P, KD, D])
        wo_hi = sbuf("wo_hi", [P, KD, D], F32R)
        wo_lo = sbuf("wo_lo", [P, KD, D], F32R)
        mT_hi = sbuf("mT_hi", [P, 2, KD, P], F32R)
        mT_lo = sbuf("mT_lo", [P, 2, KD, P], F32R)
        ps_turn = psum("ps_turn3", [P, 4, 4, P])
        ps_h = psum("ps_h", [P, 4, BANK])
        m_loaded = [sem(f"m_loaded{i}") for i in range(2)]
        h_loaded = sem("h_loaded")
        wo_loaded = sem("wo_loaded")
        small_loaded = sem("small_loaded")
        lam_dve = sem("lam_dve")
        lam_act = sem("lam_act")
        combined = sem("combined")
        head_rstd_done = sem("head_rstd_done")
        wo_hi_done = sem("wo_hi_done")
        wo_lo_done = sem("wo_lo_done")
        turned = sem("turned3")
        m_hi = sem("m_hi")
        m_lo = sem("m_lo")
        multiplied = sem("multiplied")
        h_added = sem("h_added")
        block = ctx.enter_context(nc.Block())

        @block.sync
        def _(sp):
            for j, name in enumerate(("lambda_q1", "lambda_k1", "lambda_q2", "lambda_k2")):
                sp.dma_start(lambdas[:, j], t[name].partition_broadcast(P)).then_inc(small_loaded, 16)
            sp.dma_start(subln[:], t["diff_subln_g"].partition_broadcast(P)).then_inc(small_loaded, 16)
            for i in range(NT):
                t0, n = tiles[i]
                if i >= 2:
                    sp.wait_ge(turned, 2 * (i - 1))
                sp.dma_start(m0[0:n, i % 2], t["mixed"][t0:t0 + n, :]).then_inc(m_loaded[i % 2], 16)
                sp.dma_start(m1[0:n, i % 2], t["mixed1"][t0:t0 + n, :]).then_inc(m_loaded[i % 2], 16)
                if i == 0:
                    for k in range(KD):
                        sp.dma_start(wo_raw[:, k], w_out[:, k]).then_inc(wo_loaded, 16)
                    for j in range(NT):
                        m = tiles[j][1]
                        sp.dma_start(h_all[0:m, j], split_rows(tiles, t["x_prompt"], t["x_sample"], j)) \
                            .then_inc(h_loaded, 16)

        @block.gpsimd
        def _(pool):
            def rstd(i):
                n = tiles[i][1]
                pool.wait_ge(combined, 6 * i + 3)
                rstd_pool(nc, pool, head_ms[0:n, i], head_sq[0:n, i], head_rstd[0:n, i],
                          t["neg_half"][0:n, 0:NH], P, head_rstd_done, i)

            rstd(0)
            for k in range(KD):
                pool.wait_ge(wo_hi_done, k + 1)
                nc.gpsimd.tensor_tensor(wo_lo[:, k], wo_raw[:, k], wo_hi[:, k].bitcast(F32),
                                        ALU.subtract).then_inc(wo_lo_done, 1)
                if k == 0:
                    rstd(1)
            for i in range(2, NT):
                rstd(i)

        @block.scalar
        def _(act):
            act.wait_ge(lam_dve, 2)
            nc.scalar.activation(lam[:, 2:4], lam[:, 0:2], ACT.Exp).then_inc(lam_act, 1)
            for i in range(NT):
                n = tiles[i][1]
                for j in range(2):
                    q = 2 * i + j
                    act.wait_ge(turned, q + 1)
                    if i >= 2:
                        act.wait_ge(multiplied, 2 * (i - 1))
                    nc.scalar.copy(mT_hi[:, i % 2, 4 * j:4 * j + 4, 0:n], ps_turn[:, q % 4, :, 0:n]).then_inc(m_hi, 1)

        @block.vector
        def _(dve):
            dve.wait_ge(small_loaded, 80)
            for j in range(2):
                nc.vector.tensor_tensor_reduce(lam_prod[:, j], lambdas[:, 2 * j], lambdas[:, 2 * j + 1], 1.0, 0.0,
                                               ALU.mult, ALU.add, lam[:, j:j + 1]).then_inc(lam_dve, 1)
            dve.wait_ge(lam_act, 1)
            nc.vector.tensor_tensor(lam[:, 4:5], lam[:, 3:4], lam[:, 2:3], ALU.subtract).then_inc(lam_dve, 1)
            dve.wait_ge(lam_dve, 3)
            nc.vector.tensor_scalar(lam[:, 5:6], lam[:, 4:5], -LAM_INIT, None, ALU.add).then_inc(lam_dve, 1)
            nc.vector.tensor_scalar(subln[:], subln[:], 1.0 - LAM_INIT, None, ALU.mult).then_inc(lam_dve, 1)
            dve.wait_ge(lam_dve, 5)

            def combine(i):
                n = tiles[i][1]
                d = m0[0:n, i % 2, 0:DW]
                dh = d.rearrange("p (h v) -> p h v", h=NH)
                dve.wait_ge(m_loaded[i % 2], 32 * (i // 2 + 1))
                nc.vector.scalar_tensor_tensor(d, m1[0:n, i % 2], lam[0:n, 5:6], d, ALU.mult,
                                               ALU.add).then_inc(combined, 1)
                dve.wait_ge(combined, 6 * i + 1)
                nc.vector.tensor_tensor(squares[0:n], d, d, ALU.mult).then_inc(combined, 1)
                dve.wait_ge(combined, 6 * i + 2)
                nc.vector.tensor_reduce(head_sq[0:n, i], squares[0:n].rearrange("p (h v) -> p h v", h=NH),
                                        AX.X, ALU.add).then_inc(combined, 1)
                nc.vector.tensor_tensor(dh, dh, subln[0:n].unsqueeze(1).to_broadcast([n, NH, P]),
                                        ALU.mult).then_inc(combined, 1)
                dve.wait_ge(combined, 6 * i + 4)
                dve.wait_ge(head_rstd_done, 2 * (i + 1))
                nc.vector.tensor_tensor(dh, dh, head_rstd[0:n, i].unsqueeze(2).to_broadcast([n, NH, P]),
                                        ALU.mult).then_inc(combined, 2)

            def split(i):
                n = tiles[i][1]
                for j in range(2):
                    q = 2 * i + j
                    dve.wait_ge(m_hi, q + 1)
                    nc.vector.tensor_tensor(mT_lo[:, i % 2, 4 * j:4 * j + 4, 0:n], ps_turn[:, q % 4, :, 0:n],
                                            mT_hi[:, i % 2, 4 * j:4 * j + 4, 0:n].bitcast(F32),
                                            ALU.subtract).then_inc(m_lo, 1)

            def add(i):
                n = tiles[i][1]
                for j in range(2):
                    m = 2 * i + j
                    dve.wait_ge(multiplied, m + 1)
                    hh = h_all[0:n, i, j * BANK:(j + 1) * BANK]
                    nc.vector.tensor_tensor(hh, ps_h[0:n, m % 4], hh, ALU.add).then_inc(h_added, 1)

            combine(0)
            for k in range(KD):
                dve.wait_ge(wo_loaded, 16 * KD)
                nc.vector.tensor_copy(wo_hi[:, k], wo_raw[:, k]).then_inc(wo_hi_done, 1)
            dve.wait_ge(h_loaded, 16 * NT)
            for i in range(NT):
                if i + 1 < NT:
                    combine(i + 1)
                split(i)
                if i >= 1:
                    add(i - 1)
            add(NT - 1)

        @block.tensor
        def _(pe):
            def turn(i):
                n = tiles[i][1]
                pe.wait_ge(combined, 6 * i + 6)
                for j in range(2):
                    q = 2 * i + j
                    if q >= 4:
                        pe.wait_ge(m_lo, q - 3)
                    for k in range(4):
                        c = (4 * j + k) * P
                        last = nc.tensor.transpose(ps_turn[:, q % 4, k, 0:n], m0[0:n, i % 2, c:c + P],
                                                   t["ident"][0:n, 0:n])
                    last.then_inc(turned, 1)

            turn(0)
            for i in range(NT):
                n = tiles[i][1]
                if i + 1 < NT:
                    turn(i + 1)
                pe.wait_ge(m_lo, 2 * (i + 1))
                for j in range(2):
                    m = 2 * i + j
                    if m >= 4:
                        pe.wait_ge(h_added, m - 3)
                    for k in range(KD):
                        if m == 0:
                            pe.wait_ge(wo_lo_done, k + 1)
                        out = ps_h[0:n, m % 4]
                        b_hi, b_lo = (x[:, k, j * BANK:(j + 1) * BANK] for x in (wo_hi, wo_lo))
                        nc.tensor.matmul(out, mT_hi[:, i % 2, k, 0:n], b_hi, start=(k == 0), stop=False)
                        nc.tensor.matmul(out, mT_hi[:, i % 2, k, 0:n], b_lo, start=False, stop=False)
                        last = nc.tensor.matmul(out, mT_lo[:, i % 2, k, 0:n], b_hi, start=False, stop=(k == KD - 1))
                    last.then_inc(multiplied, 1)


def norm_turn(nc, t, h_all, nT_hi, nT_lo):
    tiles = token_tiles(t["seq"], t["dec"])
    NT = len(tiles)
    D = h_all.shape[2]
    with ExitStack() as ctx:
        def sbuf(name, shape, dtype=F32):
            return ctx.enter_context(nc.sbuf_tensor(name, shape, dtype))

        def psum(name, shape):
            return ctx.enter_context(nc.psum_tensor(name, shape, F32))

        def sem(name):
            return ctx.enter_context(nc.semaphore(name))

        xn = sbuf("xn4", [P, 2, D])
        squares = sbuf("squares4", [P, D])
        g_sb = sbuf("g4", [P, D])
        sumsq = sbuf("sumsq4", [P, NT])
        ms = sbuf("ms4", [P, NT])
        rstd = sbuf("rstd4", [P, NT])
        ps_turn = psum("ps_turn4", [P, 4, 4, P])
        g_loaded = sem("g_loaded4")
        squared = sem("squared4")
        rstd_done = sem("rstd_done4")
        normed = sem("normed4")
        turned = sem("turned4")
        n_hi = sem("n_hi4")
        n_lo = sem("n_lo4")
        block = ctx.enter_context(nc.Block())
        @block.sync
        def _(sp):
            sp.dma_start(g_sb[:], t["norm_ffn_g"].partition_broadcast(P)).then_inc(g_loaded, 16)

        @block.gpsimd
        def _(pool):
            for i in range(NT):
                n = tiles[i][1]
                pool.wait_ge(squared, i + 1)
                rstd_pool(nc, pool, ms[0:n, i:i + 1], sumsq[0:n, i:i + 1], rstd[0:n, i:i + 1],
                          t["neg_half"][0:n, 0:1], D, rstd_done, i)

        @block.scalar
        def _(act):
            def square(i):
                n = tiles[i][1]
                norm_rows_act(nc, act, h_all[0:n, i], squares[0:n], sumsq[0:n, i:i + 1], squared, i)

            square(0)
            square(1)
            for i in range(NT):
                t0, n = tiles[i]
                if i + 2 < NT:
                    square(i + 2)
                for j in range(2):
                    q = 2 * i + j
                    act.wait_ge(turned, q + 1)
                    nc.scalar.copy(nT_hi[:, 4 * j:4 * j + 4, t0:t0 + n], ps_turn[:, q % 4, :, 0:n]).then_inc(n_hi, 1)

        @block.vector
        def _(dve):
            def norm(i):
                n = tiles[i][1]
                dve.wait_ge(rstd_done, 2 * (i + 1))
                if i == 0:
                    dve.wait_ge(g_loaded, 16)
                if i >= 2:
                    dve.wait_ge(turned, 2 * (i - 1))
                nc.vector.scalar_tensor_tensor(xn[0:n, i % 2], h_all[0:n, i], rstd[0:n, i:i + 1], g_sb[0:n],
                                               ALU.mult, ALU.mult).then_inc(normed, 1)

            norm(0)
            for i in range(NT):
                t0, n = tiles[i]
                if i + 1 < NT:
                    norm(i + 1)
                for j in range(2):
                    q = 2 * i + j
                    dve.wait_ge(n_hi, q + 1)
                    nc.vector.tensor_tensor(nT_lo[:, 4 * j:4 * j + 4, t0:t0 + n], ps_turn[:, q % 4, :, 0:n],
                                            nT_hi[:, 4 * j:4 * j + 4, t0:t0 + n].bitcast(F32),
                                            ALU.subtract).then_inc(n_lo, 1)

        @block.tensor
        def _(pe):
            for i in range(NT):
                n = tiles[i][1]
                pe.wait_ge(normed, i + 1)
                for j in range(2):
                    q = 2 * i + j
                    if q >= 4:
                        pe.wait_ge(n_lo, q - 3)
                    for k in range(4):
                        c = (4 * j + k) * P
                        last = nc.tensor.transpose(ps_turn[:, q % 4, k, 0:n], xn[0:n, i % 2, c:c + P],
                                                   t["ident"][0:n, 0:n])
                    last.then_inc(turned, 1)


def feed(nc, t, h_all, nT_hi, nT_lo):
    tiles = token_tiles(t["seq"], t["dec"])
    NT, T = len(tiles), t["seq"] + t["dec"]
    D = h_all.shape[2]
    KD = D // P
    NF = t["w_gate"].shape[1] // P
    parts = 3
    width = -(-T // parts // 2) * 2
    chunks = [(a, min(width, T - a)) for a in range(0, T, width)]
    G = NF // 2
    NY = 2 * NT
    w_gate = t["w_gate"].rearrange("(k p) n -> p k n", p=P)
    w_up = t["w_up"].rearrange("(k p) n -> p k n", p=P)
    with ExitStack() as ctx:
        def sbuf(name, shape, dtype=F32):
            return ctx.enter_context(nc.sbuf_tensor(name, shape, dtype))

        def psum(name, shape):
            return ctx.enter_context(nc.psum_tensor(name, shape, F32))

        def sem(name):
            return ctx.enter_context(nc.semaphore(name))

        gu_raw = sbuf("gu_raw", [P, KD, 2, P])
        gu_hi = sbuf("gu_hi", [P, 2, KD, 2, P], F32R)
        gu_lo = sbuf("gu_lo", [P, 2, KD, 2, P], F32R)
        wd_raw = sbuf("wd_raw", [P, D])
        wd_hi = sbuf("wd_hi", [P, 3, D], F32R)
        wd_lo = sbuf("wd_lo", [P, 3, D], F32R)
        gate = sbuf("gate", [P, 2, width])
        hidden = sbuf("hidden", [P, 2, width])
        hT_hi = sbuf("hT_hi", [P, 3, T], F32R)
        hT_lo = sbuf("hT_lo", [P, 3, T], F32R)
        ps_g = psum("ps_g", [P, 2, BANK])
        ps_u = psum("ps_u", [P, 2, BANK])
        ps_y = psum("ps_y", [P, 4, BANK])
        gu_loaded = sem("gu_loaded")
        wd_loaded = sem("wd_loaded")
        gu_hi_done = sem("gu_hi_done")
        gu_lo_done = sem("gu_lo_done")
        wd_hi_done = sem("wd_hi_done")
        wd_lo_done = sem("wd_lo_done")
        gu_done = sem("gu_done")
        silu_done = sem("silu_done")
        hidden_done = sem("hidden_done")
        hid_hi = sem("hid_hi")
        hid_lo = sem("hid_lo")
        y_done = sem("y_done")
        y_added = sem("y_added")
        block = ctx.enter_context(nc.Block())
        C = len(chunks)

        @block.sync
        def _(sp):
            for f in range(NF):
                if f >= 1:
                    sp.wait_ge(gu_lo_done, f)
                sp.dma_start(gu_raw[:, :, 0], w_gate[:, :, f * P:(f + 1) * P]).then_inc(gu_loaded, 16)
                sp.dma_start(gu_raw[:, :, 1], w_up[:, :, f * P:(f + 1) * P]).then_inc(gu_loaded, 16)
                if f >= 1:
                    sp.wait_ge(wd_lo_done, f)
                sp.dma_start(wd_raw[:], t["w_down"][f * P:(f + 1) * P, :]).then_inc(wd_loaded, 16)

        @block.gpsimd
        def _(pool):
            def split_gu(f):
                pool.wait_ge(gu_hi_done, f + 1)
                nc.gpsimd.tensor_tensor(gu_lo[:, f % 2].rearrange("p k w n -> p (k w n)"),
                                        gu_raw[:].rearrange("p k w n -> p (k w n)"),
                                        gu_hi[:, f % 2].bitcast(F32).rearrange("p k w n -> p (k w n)"),
                                        ALU.subtract).then_inc(gu_lo_done, 1)

            def split_wd(f):
                pool.wait_ge(wd_hi_done, f + 1)
                nc.gpsimd.tensor_tensor(wd_lo[:, f % 3], wd_raw[:], wd_hi[:, f % 3].bitcast(F32),
                                        ALU.subtract).then_inc(wd_lo_done, 1)

            split_gu(0)
            split_wd(0)
            split_gu(1)
            for f in range(NF):
                for c, (a, n) in enumerate(chunks):
                    q = C * f + c
                    pool.wait_ge(hid_hi, q + 1)
                    nc.gpsimd.tensor_tensor(hT_lo[:, f % 3, a:a + n], hidden[:, q % 2, 0:n],
                                            hT_hi[:, f % 3, a:a + n].bitcast(F32), ALU.subtract).then_inc(hid_lo, 1)
                if f + 2 < NF:
                    split_gu(f + 2)
                if f + 1 < NF:
                    split_wd(f + 1)

        @block.scalar
        def _(act):
            for q in range(C * NF):
                f, c = divmod(q, C)
                a, n = chunks[c]
                act.wait_ge(gu_done, q + 1)
                if q >= 2:
                    act.wait_ge(hidden_done, q - 1)
                nc.scalar.activation(gate[:, q % 2, 0:n], ps_g[:, q % 2, 0:n], ACT.Silu).then_inc(silu_done, 1)
                act.wait_ge(hidden_done, q + 1)
                if f >= 3 and c == 0:
                    act.wait_ge(y_done, NY * ((f - 3) // 2 + 1))
                nc.scalar.copy(hT_hi[:, f % 3, a:a + n], hidden[:, q % 2, 0:n]).then_inc(hid_hi, 1)

        @block.vector
        def _(dve):
            def split_gu(f):
                dve.wait_ge(gu_loaded, 32 * (f + 1))
                if f >= 2:
                    dve.wait_ge(gu_done, C * (f - 1))
                nc.vector.tensor_copy(gu_hi[:, f % 2].rearrange("p k w n -> p (k w n)"),
                                      gu_raw[:].rearrange("p k w n -> p (k w n)")).then_inc(gu_hi_done, 1)

            def split_wd(f):
                dve.wait_ge(wd_loaded, 16 * (f + 1))
                if f >= 3:
                    dve.wait_ge(y_done, NY * ((f - 3) // 2 + 1))
                nc.vector.tensor_copy(wd_hi[:, f % 3], wd_raw[:]).then_inc(wd_hi_done, 1)

            def add(g):
                for i in range(NT):
                    n = tiles[i][1]
                    for j in range(2):
                        y = NY * g + 2 * i + j
                        dve.wait_ge(y_done, y + 1)
                        hh = h_all[0:n, i, j * BANK:(j + 1) * BANK]
                        nc.vector.tensor_tensor(hh, ps_y[0:n, y % 4], hh, ALU.add).then_inc(y_added, 1)

            split_gu(0)
            split_wd(0)
            split_gu(1)
            for f in range(NF):
                for c, (a, n) in enumerate(chunks):
                    q = C * f + c
                    dve.wait_ge(silu_done, q + 1)
                    if q >= 2:
                        dve.wait_ge(hid_lo, q - 1)
                    nc.vector.tensor_tensor(hidden[:, q % 2, 0:n], ps_u[:, q % 2, 0:n], gate[:, q % 2, 0:n],
                                            ALU.mult).then_inc(hidden_done, 1)
                if f % 2 == 0 and f >= 2:
                    add(f // 2 - 1)
                if f + 2 < NF:
                    split_gu(f + 2)
                if f + 1 < NF:
                    split_wd(f + 1)
            add(G - 1)

        @block.tensor
        def _(pe):
            def up(f):
                pe.wait_ge(gu_lo_done, f + 1)
                for c, (a, n) in enumerate(chunks):
                    q = C * f + c
                    if q >= 2:
                        pe.wait_ge(hidden_done, q - 1)
                    for w, ps in ((0, ps_g), (1, ps_u)):
                        out = ps[:, q % 2, 0:n]
                        for k in range(KD):
                            w_h, w_l = gu_hi[:, f % 2, k, w], gu_lo[:, f % 2, k, w]
                            x_h, x_l = nT_hi[:, k, a:a + n], nT_lo[:, k, a:a + n]
                            nc.tensor.matmul(out, w_h, x_h, start=(k == 0), stop=False)
                            nc.tensor.matmul(out, w_h, x_l, start=False, stop=False)
                            last = nc.tensor.matmul(out, w_l, x_h, start=False, stop=(k == KD - 1))
                    last.then_inc(gu_done, 1)

            def down(g):
                pe.wait_ge(hid_lo, C * (2 * g + 2))
                pe.wait_ge(wd_lo_done, 2 * g + 2)
                for i in range(NT):
                    t0, n = tiles[i]
                    for j in range(2):
                        y = NY * g + 2 * i + j
                        if y >= 4:
                            pe.wait_ge(y_added, y - 3)
                        out = ps_y[0:n, y % 4]
                        for f in (2 * g, 2 * g + 1):
                            h_h, h_l = hT_hi[:, f % 3, t0:t0 + n], hT_lo[:, f % 3, t0:t0 + n]
                            b_h, b_l = (x[:, f % 3, j * BANK:(j + 1) * BANK] for x in (wd_hi, wd_lo))
                            nc.tensor.matmul(out, h_h, b_h, start=(f == 2 * g), stop=False)
                            nc.tensor.matmul(out, h_h, b_l, start=False, stop=False)
                            last = nc.tensor.matmul(out, h_l, b_h, start=False, stop=(f == 2 * g + 1))
                        last.then_inc(y_done, 1)

            for f in range(NF):
                up(f)
                if f % 2 == 0 and f >= 2:
                    down(f // 2 - 1)
            down(G - 1)


def final(nc, t, h_all):
    tiles = token_tiles(t["seq"], t["dec"])
    NT = len(tiles)
    D = h_all.shape[2]
    with ExitStack() as ctx:
        def sbuf(name, shape, dtype=F32):
            return ctx.enter_context(nc.sbuf_tensor(name, shape, dtype))

        def psum(name, shape):
            return ctx.enter_context(nc.psum_tensor(name, shape, F32))

        def sem(name):
            return ctx.enter_context(nc.semaphore(name))

        y_sb = sbuf("y_sb", [P, 2, D])
        squares = sbuf("squares5", [P, D])
        g_sb = sbuf("g5", [P, D])
        sumsq = sbuf("sumsq5", [P, NT])
        ms = sbuf("ms5", [P, NT])
        rstd = sbuf("rstd5", [P, NT])
        g_loaded = sem("g_loaded5")
        squared = sem("squared5")
        rstd_done = sem("rstd_done5")
        y_normed = sem("y_normed")
        y_stored = [sem(f"y_stored{i}") for i in range(2)]
        block = ctx.enter_context(nc.Block())

        @block.sync
        def _(sp):
            sp.dma_start(g_sb[:], t["norm_final_g"].partition_broadcast(P)).then_inc(g_loaded, 16)
            for i in range(NT):
                n = tiles[i][1]
                sp.wait_ge(y_normed, i + 1)
                sp.dma_start(split_rows(tiles, t["y_prompt"], t["y_sample"], i), y_sb[0:n, i % 2]) \
                    .then_inc(y_stored[i % 2], 16)
            for s in range(2):
                sp.wait_ge(y_stored[s], 16 * len(range(s, NT, 2)))

        @block.gpsimd
        def _(pool):
            for i in range(NT):
                n = tiles[i][1]
                pool.wait_ge(squared, i + 1)
                rstd_pool(nc, pool, ms[0:n, i:i + 1], sumsq[0:n, i:i + 1], rstd[0:n, i:i + 1],
                          t["neg_half"][0:n, 0:1], D, rstd_done, i)

        @block.scalar
        def _(act):
            for i in range(NT):
                n = tiles[i][1]
                norm_rows_act(nc, act, h_all[0:n, i], squares[0:n], sumsq[0:n, i:i + 1], squared, i)

        @block.vector
        def _(dve):
            dve.wait_ge(g_loaded, 16)
            for i in range(NT):
                n = tiles[i][1]
                dve.wait_ge(rstd_done, 2 * (i + 1))
                if i >= 2:
                    dve.wait_ge(y_stored[i % 2], 16 * (i // 2))
                nc.vector.scalar_tensor_tensor(y_sb[0:n, i % 2], h_all[0:n, i], rstd[0:n, i:i + 1], g_sb[0:n],
                                               ALU.mult, ALU.mult).then_inc(y_normed, 1)


def encoder_step(nc, t):
    D = t["x_prompt"].shape[1]
    tiles = token_tiles(t["seq"], t["dec"])
    T = t["seq"] + t["dec"]
    with (
        nc.sbuf_tensor("ident", [P, P], F32) as ident,
        nc.sbuf_tensor("neg_half", [P, 4], F32) as neg_half,
    ):
        t["ident"], t["neg_half"] = ident, neg_half
        with nc.semaphore("cleared") as cleared, nc.Block() as block:
            @block.gpsimd
            def _(pool):
                nc.gpsimd.memset(ident[:], 0.0).then_inc(cleared, 1)
                nc.gpsimd.memset(neg_half[:], -0.5).then_inc(cleared, 1)
                pool.wait_ge(cleared, 2)
                nc.gpsimd.affine_select(out=ident[:], in_=ident[:], compare_op=ALU.not_equal, fill=1.0, base=0,
                                        pattern=[[-1, P]], channel_multiplier=1).then_inc(cleared, 1)
                pool.wait_ge(cleared, 3)
        project(nc, t)
        attend(nc, t)
        with nc.sbuf_tensor("h_all", [P, len(tiles), D], F32) as h_all:
            mix(nc, t, h_all)
            with (
                nc.sbuf_tensor("n2T_hi", [P, D // P, T], F32R) as nT_hi,
                nc.sbuf_tensor("n2T_lo", [P, D // P, T], F32R) as nT_lo,
            ):
                norm_turn(nc, t, h_all, nT_hi, nT_lo)
                feed(nc, t, h_all, nT_hi, nT_lo)
            final(nc, t, h_all)


_INS = ['x_prompt', 'x_sample', 'cache_diff_k', 'cache_diff_v', 'cache_sb_k', 'cache_sb_v', 'norm_attn_g', 'w_in',
        'lambda_q1', 'lambda_k1', 'lambda_q2', 'lambda_k2', 'diff_subln_g', 'w_out', 'norm_ffn_g', 'w_gate', 'w_up',
        'w_down', 'norm_final_g']
_OUTS = ['y_prompt', 'y_sample', 'prompt_diff_k', 'prompt_diff_v', 'prompt_sb_k', 'prompt_sb_v',
         'sample_diff_k', 'sample_diff_v', 'sample_sb_k', 'sample_sb_v']


def kernel(**inputs):
    import numpy as np
    import concourse.bacc as bacc
    from concourse.bass_utils import run_bass_kernel_spmd

    nc = bacc.Bacc("TRN2", target_bir_lowering=False, num_devices=1)
    xp, xs, ck = inputs["x_prompt"], inputs["x_sample"], inputs["cache_diff_k"]
    seq, dec, past, D = xp.shape[1], xs.shape[1], ck.shape[2], xp.shape[2]
    half = D // 2
    two_d = {"x_prompt": (seq, D), "x_sample": (dec, D), "w_in": inputs["w_in"].shape[1:],
             "w_out": inputs["w_out"].shape[1:], "w_gate": inputs["w_gate"].shape[1:],
             "w_up": inputs["w_up"].shape[1:], "w_down": inputs["w_down"].shape[1:]}
    for name in ("cache_diff_k", "cache_diff_v", "cache_sb_k", "cache_sb_v"):
        two_d[name] = (past, half)
    arrays, t = {}, {"seq": seq, "dec": dec, "past": past}
    for name in _INS:
        a = np.ascontiguousarray(np.asarray(inputs[name]))
        a = a.reshape(two_d.get(name, (a.size,)))
        arrays[f"in_{name}"] = a
        t[name] = nc.dram_tensor(f"in_{name}", a.shape, mybir.dt.from_np(a.dtype), kind="ExternalInput").ap()
    out_shapes = {"y_prompt": (seq, D), "y_sample": (dec, D)}
    for name in _OUTS:
        rows = seq if "prompt" in name else dec
        shape = out_shapes.get(name, (rows, half))
        t[name] = nc.dram_tensor(f"out_{name}", shape, F32, kind="ExternalOutput").ap()
    q_d = nc.dram_tensor("q_diff", (seq + dec, half), F32, kind="Internal").ap()
    q_s = nc.dram_tensor("q_sb", (seq + dec, half), F32, kind="Internal").ap()
    t["mixed"] = nc.dram_tensor("mixed", (seq + dec, D), F32, kind="Internal").ap()
    t["mixed1"] = nc.dram_tensor("mixed1", (seq + dec, half), F32, kind="Internal").ap()
    t["new_dq"], t["sample_dq"] = q_d[0:seq, :], q_d[seq:seq + dec, :]
    t["new_sq"], t["sample_sq"] = q_s[0:seq, :], q_s[seq:seq + dec, :]
    for side, name in (("d", "diff"), ("s", "sb")):
        for kind in "kv":
            t[f"new_{side}{kind}"] = t[f"prompt_{name}_{kind}"]
            t[f"sample_{side}{kind}"] = t[f"sample_{name}_{kind}"]
            t[f"cache_{side}{kind}"] = t[f"cache_{name}_{kind}"]
    t["proj_out"] = [(t[f"new_{side}{kind}"], t[f"sample_{side}{kind}"]) for side in "ds" for kind in "qkv"]
    encoder_step(nc, t)
    r = run_bass_kernel_spmd(nc, [arrays], core_ids=[0]).results[0]
    shapes = {"y_prompt": xp.shape, "y_sample": xs.shape}
    out = []
    for name in _OUTS:
        a = r[f"out_{name}"]
        if name not in shapes:
            heads = inputs["cache_diff_k" if "diff" in name else "cache_sb_k"].shape[3:]
            a = a.reshape((1, 1, a.shape[0]) + tuple(heads))
        else:
            a = a.reshape(shapes[name])
        out.append(a)
    return tuple(out)
```

```python
import math
from contextlib import ExitStack

import concourse.bass as bass
from concourse import mybir

F32 = mybir.dt.float32
F32R = mybir.dt.float32r
ALU = mybir.AluOpType
ACT = mybir.ActivationFunctionType
AX = mybir.AxisListType

P = 128
CHUNK = 64
EPS = 1e-6
NEG_INF = -1e30
LAM_INIT = 0.8 - 0.6 * math.exp(-0.3 * 0)
BANK = 512
SOFTPLUS_LINEAR = 40.0


def token_tiles(seq, dec):
    return [(i * P, P) for i in range(seq // P)] + [(seq, dec)]


def split_rows(tiles, prompt, sample, i):
    t0, n = tiles[i]
    return prompt[t0:t0 + n, :] if i < len(tiles) - 1 else sample[0:n, :]


def norm_rows_act(nc, act, src, junk, sumsq, done, count):
    if count:
        act.wait_ge(done, count)
    nc.scalar.activation(junk, src, ACT.Square, accum_out=sumsq).then_inc(done, 1)


def rstd_pool(nc, pool, ms, sumsq, rstd, neg_half, width, done, count):
    nc.gpsimd.tensor_scalar(ms, sumsq, 1.0 / width, EPS, ALU.mult, ALU.add).then_inc(done, 1)
    pool.wait_ge(done, 2 * count + 1)
    nc.gpsimd.tensor_tensor(rstd, ms, neg_half, ALU.pow).then_inc(done, 1)


def project(nc, t):
    tiles = token_tiles(t["seq"], t["dec"])
    NT, T = len(tiles), t["seq"] + t["dec"]
    D = t["x_prompt"].shape[1]
    KD = D // P
    NG = t["w_in"].shape[1] // BANK
    w_in = t["w_in"].rearrange("(k p) n -> p k n", p=P)
    with ExitStack() as ctx:
        def sbuf(name, shape, dtype=F32):
            return ctx.enter_context(nc.sbuf_tensor(name, shape, dtype))

        def psum(name, shape):
            return ctx.enter_context(nc.psum_tensor(name, shape, F32))

        def sem(name):
            return ctx.enter_context(nc.semaphore(name))

        x_sb = sbuf("x_sb", [P, 3, D])
        xn = sbuf("xn", [P, 2, D])
        squares = sbuf("squares", [P, D])
        g_sb = sbuf("g_sb", [P, D])
        sumsq = sbuf("sumsq", [P, NT])
        ms = sbuf("ms", [P, NT])
        rstd = sbuf("rstd", [P, NT])
        nT_hi = sbuf("nT_hi", [P, KD, T], F32R)
        nT_lo = sbuf("nT_lo", [P, KD, T], F32R)
        w_raw = sbuf("w_raw", [P, 2, KD, BANK])
        w_hi = [sbuf(f"w_hi{b}", [P, KD, BANK], F32R) for b in range(2)]
        w_lo = [sbuf(f"w_lo{b}", [P, KD, BANK], F32R) for b in range(2)]
        out_sb = sbuf("out_sb", [P, 4, BANK])
        ps_turn = psum("ps_turn", [P, 4, 4, P])
        ps_proj = psum("ps_proj", [P, 4, BANK])
        x_loaded = [sem(f"x_loaded{i}") for i in range(3)]
        w_loaded = [sem(f"w_loaded{i}") for i in range(2)]
        g_loaded = sem("g_loaded")
        squared = sem("squared")
        rstd_done = sem("rstd_done")
        normed = sem("normed")
        turned = sem("turned")
        n_hi = sem("n_hi")
        n_lo = sem("n_lo")
        w_hi_done = sem("w_hi_done")
        w_lo_done = sem("w_lo_done")
        projected = sem("projected")
        evacuated = sem("evacuated")
        stored = [sem(f"stored{i}") for i in range(4)]
        block = ctx.enter_context(nc.Block())

        @block.sync
        def _(sp):
            def load_w(g):
                if g >= 2:
                    sp.wait_ge(w_lo_done, KD * (g - 1))
                sp.dma_start(w_raw[:, g % 2], w_in[:, :, g * BANK:(g + 1) * BANK]).then_inc(w_loaded[g % 2], 16)

            for i in range(NT):
                n = tiles[i][1]
                if i >= 3:
                    sp.wait_ge(normed, i - 2)
                sp.dma_start(x_sb[0:n, i % 3], split_rows(tiles, t["x_prompt"], t["x_sample"], i)) \
                    .then_inc(x_loaded[i % 3], 16)
                if i == 0:
                    sp.dma_start(g_sb[:], t["norm_attn_g"].partition_broadcast(P)).then_inc(g_loaded, 16)
                if i in (0, 2):
                    load_w(i // 2)
            for g in range(2, NG):
                load_w(g)

        @block.gpsimd
        def _(pool):
            def split_w(g):
                for k in range(KD):
                    pool.wait_ge(w_hi_done, KD * g + k + 1)
                    if g >= 2 and k == 0:
                        pool.wait_ge(projected, NT * (g - 1))
                    nc.gpsimd.tensor_tensor(w_lo[g % 2][:, k], w_raw[:, g % 2, k],
                                            w_hi[g % 2][:, k].bitcast(F32), ALU.subtract).then_inc(w_lo_done, 1)

            for i in range(NT):
                n = tiles[i][1]
                pool.wait_ge(squared, i + 1)
                rstd_pool(nc, pool, ms[0:n, i:i + 1], sumsq[0:n, i:i + 1], rstd[0:n, i:i + 1],
                          t["neg_half"][0:n, 0:1], D, rstd_done, i)
                if i == 0:
                    split_w(0)
            for g in range(1, NG):
                split_w(g)

        @block.scalar
        def _(act):
            def square(i):
                n = tiles[i][1]
                act.wait_ge(x_loaded[i % 3], 16 * (i // 3 + 1))
                norm_rows_act(nc, act, x_sb[0:n, i % 3], squares[0:n], sumsq[0:n, i:i + 1], squared, i)

            def store(m):
                g, i = divmod(m, NT)
                n = tiles[i][1]
                act.wait_ge(evacuated, m + 1)
                dst = split_rows(tiles, *t["proj_out"][g], i)
                act.dma_start(dst, out_sb[0:n, m % 4]).then_inc(stored[m % 4], 16)

            def evacuate(m):
                n = tiles[m % NT][1]
                act.wait_ge(projected, m + 1)
                if m >= 4:
                    act.wait_ge(stored[m % 4], 16 * (m // 4))
                nc.scalar.copy(out_sb[0:n, m % 4], ps_proj[0:n, m % 4]).then_inc(evacuated, 1)
                if m >= 1:
                    store(m - 1)

            square(0)
            for i in range(NT):
                t0, n = tiles[i]
                if i + 1 < NT:
                    square(i + 1)
                for j in range(2):
                    q = 2 * i + j
                    act.wait_ge(turned, q + 1)
                    nc.scalar.copy(nT_hi[:, 4 * j:4 * j + 4, t0:t0 + n], ps_turn[:, q % 4, :, 0:n]).then_inc(n_hi, 1)
                if i >= 1:
                    evacuate(i - 1)
            for m in range(NT - 1, NG * NT):
                evacuate(m)
            store(NG * NT - 1)
            for s in range(4):
                act.wait_ge(stored[s], 16 * len(range(s, NG * NT, 4)))

        @block.vector
        def _(dve):
            def split_w(g):
                dve.wait_ge(w_loaded[g % 2], 16 * (g // 2 + 1))
                if g >= 2:
                    dve.wait_ge(projected, NT * (g - 1))
                for k in range(KD):
                    nc.vector.tensor_copy(w_hi[g % 2][:, k], w_raw[:, g % 2, k]).then_inc(w_hi_done, 1)

            def norm(i):
                n = tiles[i][1]
                dve.wait_ge(rstd_done, 2 * (i + 1))
                if i == 0:
                    dve.wait_ge(g_loaded, 16)
                if i >= 2:
                    dve.wait_ge(turned, 2 * (i - 1))
                nc.vector.scalar_tensor_tensor(xn[0:n, i % 2], x_sb[0:n, i % 3], rstd[0:n, i:i + 1], g_sb[0:n],
                                               ALU.mult, ALU.mult).then_inc(normed, 1)

            norm(0)
            split_w(0)
            for i in range(NT):
                t0, n = tiles[i]
                if i + 1 < NT:
                    norm(i + 1)
                for j in range(2):
                    q = 2 * i + j
                    dve.wait_ge(n_hi, q + 1)
                    nc.vector.tensor_tensor(nT_lo[:, 4 * j:4 * j + 4, t0:t0 + n], ps_turn[:, q % 4, :, 0:n],
                                            nT_hi[:, 4 * j:4 * j + 4, t0:t0 + n].bitcast(F32),
                                            ALU.subtract).then_inc(n_lo, 1)
            for g in range(1, NG):
                split_w(g)

        @block.tensor
        def _(pe):
            def turn(i):
                n = tiles[i][1]
                pe.wait_ge(normed, i + 1)
                for j in range(2):
                    q = 2 * i + j
                    if q >= 4:
                        pe.wait_ge(n_lo, q - 3)
                    for k in range(4):
                        c = (4 * j + k) * P
                        last = nc.tensor.transpose(ps_turn[:, q % 4, k, 0:n], xn[0:n, i % 2, c:c + P],
                                                   t["ident"][0:n, 0:n])
                    last.then_inc(turned, 1)

            turn(0)
            for g in range(NG):
                for i in range(NT):
                    if g == 0 and i + 1 < NT:
                        turn(i + 1)
                    t0, n = tiles[i]
                    m = g * NT + i
                    if g == 0:
                        pe.wait_ge(n_lo, 2 * (i + 1))
                    if m >= 4:
                        pe.wait_ge(evacuated, m - 3)
                    for k in range(KD):
                        if i == 0:
                            pe.wait_ge(w_lo_done, KD * g + k + 1)
                        a_hi, a_lo = nT_hi[:, k, t0:t0 + n], nT_lo[:, k, t0:t0 + n]
                        b_hi, b_lo = w_hi[g % 2][:, k], w_lo[g % 2][:, k]
                        out = ps_proj[0:n, m % 4]
                        nc.tensor.matmul(out, a_hi, b_hi, start=(k == 0), stop=False)
                        nc.tensor.matmul(out, a_hi, b_lo, start=False, stop=False)
                        last = nc.tensor.matmul(out, a_lo, b_hi, start=False, stop=(k == KD - 1))
                    last.then_inc(projected, 1)


def attend(nc, t):
    seq, dec, past = t["seq"], t["dec"], t["past"]
    NC = seq // CHUNK + 1
    NU, ND = 8, 4
    LIVE = past + dec
    NTASK = NU * NC
    SB0 = ND * NC
    VT = seq // P + -(-LIVE // P)
    QSCALE = 64 ** -0.5
    RAW, TURNED, STATS = 6, 5, 4
    TABLES = 14

    def keys(s):
        c = s % NC
        return CHUNK * (c + 1) if c < NC - 1 else LIVE

    def blocks(s):
        return [(b, min(P, keys(s) - b)) for b in range(0, keys(s), P)]

    def segments(s):
        return [(a, min(BANK, keys(s) - a)) for a in range(0, keys(s), BANK)]

    def groups(s):
        return [blocks(s)[g:g + 4] for g in range(0, len(blocks(s)), 4)]

    def key_base(s):
        return seq if s % NC == NC - 1 else 0

    PP = 4 * P
    pieces = []
    for r in range(0, seq, PP):
        pieces += [("q", "new", r, PP, r // CHUNK), ("k", "new", r, PP, r), ("v", "new", r, PP, r // P)]
    pieces += [("q", "sample", 0, dec, NC - 1), ("k", "sample", 0, dec, seq + past),
               ("v", "sample", 0, dec, (seq + past) // P)]
    for r in range(0, past, PP):
        pieces += [("k", "cache", r, PP, seq + r), ("v", "cache", r, PP, (seq + r) // P)]
    NP = len(pieces)
    turn_order, value_order = {}, {}
    for n in range(NU * NP):
        order = value_order if pieces[n % NP][0] == "v" else turn_order
        order[n] = len(order)
    pieces_in = {}
    for n in range(NU * NP):
        u, j = divmod(n, NP)
        pieces_in.setdefault(NC * (u - 1) + 1 + j * (NC - 5) // NP, []).append(n)

    seg0, grp0 = [0], [0]
    for s in range(NTASK):
        seg0.append(seg0[-1] + len(segments(s)))
        grp0.append(grp0[-1] + len(groups(s)))

    z_slots = [0, seq, LIVE, LIVE + seq - 2 * CHUNK, LIVE + 2 * seq - 3 * CHUNK]
    Z_WIDTH, W_WIDTH = z_slots[4] + seq, LIVE + seq

    def z_place(c):
        return {0: z_slots[3] - CHUNK, 1: z_slots[3] - 3 * CHUNK, 2: z_slots[4] - 3 * CHUNK,
                NC - 1: 0}.get(c, z_slots[(c - 1) % 5])

    def w_place(c):
        return {0: LIVE, 1: LIVE + CHUNK, NC - 1: 0}.get(c, c % 2 * LIVE)

    def overwritten(places, s):
        return max([r for r in range(max(0, s - NC), s)
                    if places[r] < places[s] + keys(s) and places[s] < places[r] + keys(r)], default=-1)

    z_at = [z_place(s % NC) for s in range(NTASK)]
    w_at = [w_place(s % NC) for s in range(NTASK)]
    z_over = [overwritten(z_at, s) for s in range(NTASK)]
    w_over = [overwritten(w_at, s) for s in range(NTASK)]
    for s in range(NTASK):
        assert z_over[s] <= max(s - 4, -1) or (z_over[s] == s - 3 and len(groups(s - 3)) <= 2)
        assert w_over[s] <= max(s - 2, -1)

    def source(u, kind, where):
        side = "d" if u < ND else "s"
        return t[f"{where}_{side}{kind}"][:, (u % ND) * P:(u % ND + 1) * P]

    with ExitStack() as ctx:
        def sbuf(name, shape, dtype=F32):
            return ctx.enter_context(nc.sbuf_tensor(name, shape, dtype))

        def psum(name, shape):
            return ctx.enter_context(nc.psum_tensor(name, shape, F32))

        def sem(name):
            return ctx.enter_context(nc.semaphore(name))

        kT_hi = [sbuf(f"kT_hi{b}", [P, seq + LIVE], F32R) for b in range(2)]
        kT_lo = [sbuf(f"kT_lo{b}", [P, seq + LIVE], F32R) for b in range(2)]
        v = [sbuf(f"v{b}", [P, VT, 2, P], F32R) for b in range(2)]
        qT_hi = [sbuf(f"qT_hi{b}", [P, NC, P], F32R) for b in range(2)]
        qT_lo = [sbuf(f"qT_lo{b}", [P, NC, P], F32R) for b in range(2)]
        raw = sbuf("raw", [P, RAW, 4, P])
        z_arena = sbuf("z", [P, Z_WIDTH])
        w_arena = sbuf("w", [P, W_WIDTH])
        aT_hi = sbuf("aT_hi", [P, TURNED, 4, P], F32R)
        aT_lo = sbuf("aT_lo", [P, TURNED, 4, P], F32R)
        bias = w_arena[:, 0:LIVE]
        mask = sbuf("mask", [P, CHUNK])
        mask_r = sbuf("mask_r", [P, CHUNK], F32R)
        ident_r = sbuf("ident_r", [P, P], F32R)
        seg_max = sbuf("seg_max", [P, STATS, 8])
        neg_max = sbuf("neg_max", [P, STATS])
        row_sum = sbuf("row_sum", [P, STATS])
        inv_sum = sbuf("inv_sum", [P, STATS])
        o_sb = sbuf("o_sb", [P, 4, P])
        ps_prep = psum("ps_prep", [P, 2, 4, P])
        ps_z = psum("ps_z", [P, 2, BANK])
        ps_aT = psum("ps_aT", [P, 2, 4, P])
        ps_o = psum("ps_o", [P, 2, BANK])
        raw_loaded = [sem(f"raw_loaded{i}") for i in range(RAW)]
        tables = sem("tables")
        mask_ready = sem("mask_ready")
        bias_done = sem("bias_done")
        prep_turned = sem("prep_turned")
        prep_hi = sem("prep_hi")
        prep_lo = sem("prep_lo")
        v_hi = sem("v_hi")
        v_lo = sem("v_lo")
        scored = sem("scored")
        biased = sem("biased")
        copied = sem("copied")
        max_step = sem("max_step")
        max_ready = sem("max_ready")
        clamped = sem("clamped")
        exp_done = sem("exp_done")
        kept = sem("kept")
        summed = sem("summed")
        exponents = sem("exponents")
        weights = sem("weights")
        inv_done = sem("inv_done")
        a_turned = sem("a_turned")
        a_hi = sem("a_hi")
        a_lo = sem("a_lo")
        a_used = sem("a_used")
        o_half = sem("o_half")
        o_done = sem("o_done")
        o_stored = [sem(f"o_stored{i}") for i in range(4)]
        block = ctx.enter_context(nc.Block())

        def is_diff(s):
            return s < SB0

        def is_sb(s):
            return SB0 <= s < NTASK

        def z(s, a=0, n=None):
            n = keys(s) - a if n is None else n
            return z_arena[:, z_at[s] + a:z_at[s] + a + n]

        def w(s):
            return w_arena[:, w_at[s]:w_at[s] + keys(s)]

        def stat(tile, s):
            return tile[:, s % STATS:s % STATS + 1]

        steps = range(min(pieces_in), NTASK + 2)

        @block.sync
        def _(sp):
            def load(n):
                u, j = divmod(n, NP)
                kind, where, r, rows, _ = pieces[j]
                m = n - RAW
                if m in turn_order:
                    sp.wait_ge(prep_turned, turn_order[m] + 1)
                elif m in value_order:
                    sp.wait_ge(v_lo, value_order[m] + 1)
                src = source(u, kind, where)[r:r + rows, :]
                if rows >= P:
                    src = src.rearrange("(i p) n -> p i n", p=P)
                    sp.dma_start(raw[:, n % RAW, 0:rows // P], src).then_inc(raw_loaded[n % RAW], 16)
                else:
                    sp.dma_start(raw[0:rows, n % RAW, 0], src).then_inc(raw_loaded[n % RAW], 16)

            def store(s):
                u, c = divmod(s, NC)
                tok, col = c * CHUNK, u * P
                sp.wait_ge(o_done, s + 1)
                o = o_sb[:, s % 4]
                if u < ND:
                    sp.dma_start(t["mixed"][tok:tok + CHUNK, col:col + P], o[0:CHUNK]) \
                        .then_inc(o_stored[s % 4], 16)
                    sp.dma_start(t["mixed1"][tok:tok + CHUNK, col:col + P], o[CHUNK:P]) \
                        .then_inc(o_stored[s % 4], 16)
                else:
                    for a in (0, CHUNK):
                        sp.dma_start(t["mixed"][tok:tok + CHUNK, col + a:col + a + CHUNK],
                                     o[a:a + CHUNK, a:a + CHUNK]).then_inc(o_stored[s % 4], 16)

            for n in range(RAW - 1):
                load(n)
            ahead = RAW - 1
            for s in steps:
                for n in pieces_in.get(s, ()):
                    if n + ahead < NU * NP:
                        load(n + ahead)
                if 0 <= s - 3:
                    store(s - 3)
            store(NTASK - 1)
            for i in range(4):
                sp.wait_ge(o_stored[i], 32 * len(range(i, NTASK, 4)))

        @block.gpsimd
        def _(pool):
            made = 0
            for q in (qT_hi[0], qT_lo[0], qT_hi[1], qT_lo[1]):
                for a in (0, CHUNK):
                    off = q[a:a + CHUNK, :, CHUNK - a:P - a].bitcast(mybir.dt.uint32)
                    if made:
                        pool.wait_ge(tables, made)
                    nc.gpsimd.memset(off, 0).then_inc(tables, 1)
                    made += 1
            for a in (0, CHUNK):
                pool.wait_ge(tables, made)
                nc.gpsimd.iota(w_arena[a:a + CHUNK, 0:LIVE], [[-1, LIVE]], base=past, channel_multiplier=1,
                               allow_small_or_imprecise_dtypes=True).then_inc(tables, 1)
                made += 1
            pool.wait_ge(tables, made)
            nc.gpsimd.memset(mask[:], 0.0).then_inc(tables, 1)
            made += 1
            for a in (0, CHUNK):
                pool.wait_ge(tables, made)
                nc.gpsimd.affine_select(out=mask[a:a + CHUNK], in_=mask[a:a + CHUNK], compare_op=ALU.is_gt,
                                        fill=NEG_INF, base=0, pattern=[[-1, CHUNK]],
                                        channel_multiplier=1).then_inc(tables, 1)
                made += 1
            pool.wait_ge(tables, made)
            nc.gpsimd.tensor_copy(ident_r[:], t["ident"][:]).then_inc(tables, 1)
            made += 1
            assert made == TABLES
            pool.wait_ge(tables, made)
            nc.gpsimd.tensor_copy(mask_r[:], mask[:]).then_inc(mask_ready, 1)

            def split_values(n):
                u, j = divmod(n, NP)
                _, _, _, rows, place = pieces[j]
                k, m = max(1, rows // P), min(P, rows)
                pool.wait_ge(v_hi, value_order[n] + 1)
                nc.gpsimd.tensor_tensor(v[u % 2][0:m, place:place + k, 1, :], raw[0:m, n % RAW, 0:k],
                                        v[u % 2][0:m, place:place + k, 0, :].bitcast(F32),
                                        ALU.subtract).then_inc(v_lo, 1)

            def exponent(s):
                pool.wait_ge(summed, 2 * (s - SB0 + 1))
                nc.gpsimd.tensor_tensor(z(s), z(s), w(s), ALU.subtract).then_inc(exponents, 1)

            def maximum(s):
                nb = len(segments(s))
                pool.wait_ge(biased, seg0[s + 1])
                if s >= STATS:
                    pool.wait_ge(weights, s - STATS + 1)
                sm = seg_max[:, s % STATS]
                for b in range(1, nb - 1):
                    nc.gpsimd.tensor_scalar(sm[:, b:b + 1], sm[:, b:b + 1], sm[:, b - 1:b], None,
                                            ALU.max).then_inc(max_step, 1)
                    pool.wait_ge(max_step, (nb - 2) * (s // NC) + b)
                last = sm[:, nb - 1:nb]
                if nb > 1:
                    nc.gpsimd.tensor_scalar(stat(neg_max, s), last, sm[:, nb - 2:nb - 1], -1.0, ALU.max,
                                            ALU.mult).then_inc(max_ready, 1)
                else:
                    nc.gpsimd.tensor_scalar(stat(neg_max, s), last, -1.0, None, ALU.mult).then_inc(max_ready, 1)

            for s in steps:
                for n in pieces_in.get(s, ()):
                    if n in value_order:
                        split_values(n)
                if is_sb(s + 2):
                    exponent(s + 2)
                if 0 <= s + 3 and is_diff(s + 3):
                    maximum(s + 3)

        @block.scalar
        def _(act):
            nc.scalar.preload_act_table_set("natural_log_exp_and_others")

            def prepare(n):
                u, j = divmod(n, NP)
                kind, _, _, rows, place = pieces[j]
                k, m = max(1, rows // P), min(P, rows)
                if u >= 2:
                    act.wait_ge(a_used, grp0[NC * (u - 1)])
                if kind == "v":
                    act.wait_ge(raw_loaded[n % RAW], 16 * (n // RAW + 1))
                    nc.scalar.copy(v[u % 2][0:m, place:place + k, 0, :], raw[0:m, n % RAW, 0:k]).then_inc(v_hi, 1)
                    return
                e = turn_order[n]
                act.wait_ge(prep_turned, e + 1)
                src = ps_prep[:, e % 2].rearrange("p a b -> p (a b)")
                if kind == "k":
                    nc.scalar.copy(kT_hi[u % 2][:, place:place + rows], src[:, 0:rows]).then_inc(prep_hi, 1)
                else:
                    ch = rows // CHUNK
                    srcq = src[:, 0:rows].rearrange("p (c q) -> p c q", q=CHUNK)
                    for a in (0, CHUNK):
                        last = nc.scalar.activation(qT_hi[u % 2][a:a + CHUNK, place:place + ch, a:a + CHUNK],
                                                    srcq[a:a + CHUNK], ACT.Copy, scale=QSCALE)
                    last.then_inc(prep_hi, 1)

            def copy_scores(s):
                if z_over[s] >= 0:
                    act.wait_ge(a_turned, grp0[z_over[s] + 1])
                for b, (a, n) in enumerate(segments(s)):
                    e = seg0[s] + b
                    act.wait_ge(scored, e + 1)
                    nc.scalar.copy(z(s, a, n), ps_z[:, e % 2, 0:n]).then_inc(copied, 1)

            def begin(s):
                if is_diff(s):
                    act.wait_ge(max_ready, s + 1)
                    if s >= STATS:
                        act.wait_ge(inv_done, s - STATS + 1)
                    nc.scalar.activation(z(s), z(s), ACT.Exp, bias=stat(neg_max, s),
                                         accum_out=stat(row_sum, s)).then_inc(weights, 1)
                else:
                    act.wait_ge(clamped, s - SB0 + 1)
                    nc.scalar.activation(w(s), w(s), ACT.Exp).then_inc(exp_done, 1)
                    act.wait_ge(exp_done, s - SB0 + 1)
                    nc.scalar.activation(w(s), w(s), ACT.Ln, bias=1.0).then_inc(kept, 1)

            def finish(s):
                act.wait_ge(exponents, s - SB0 + 1)
                nc.scalar.activation(z(s), z(s), ACT.Exp).then_inc(weights, 1)

            def split(s):
                for g, bl in enumerate(groups(s)):
                    e = grp0[s] + g
                    act.wait_ge(a_turned, e + 1)
                    if e >= TURNED:
                        act.wait_ge(a_used, e - TURNED + 1)
                    f = sum(m == P for _, m in bl)
                    if f:
                        last = nc.scalar.copy(aT_hi[:, e % TURNED, 0:f], ps_aT[:, e % 2, 0:f])
                    if f < len(bl):
                        m = bl[f][1]
                        last = nc.scalar.copy(aT_hi[0:m, e % TURNED, f], ps_aT[0:m, e % 2, f])
                    last.then_inc(a_hi, 1)

            def left(s):
                act.wait_ge(a_used, grp0[s + 1])
                if s >= 4:
                    act.wait_ge(o_stored[s % 4], 32 * (s // 4))
                act.wait_ge(inv_done, s + 1)
                nc.scalar.activation(o_sb[:, s % 4], ps_o[:, s % 2, 0:P], ACT.Copy,
                                     scale=stat(inv_sum, s)).then_inc(o_half, 1)

            act.wait_ge(tables, TABLES)
            for s in steps:
                for n in pieces_in.get(s, ()):
                    prepare(n)
                if 0 <= s + 2 < NTASK:
                    begin(s + 2)
                if 0 <= s < NTASK:
                    split(s)
                if is_sb(s + 3):
                    copy_scores(s + 3)
                if is_sb(s + 1):
                    finish(s + 1)
                if 0 <= s - 2 and is_diff(s - 2):
                    left(s - 2)

        @block.vector
        def _(dve):
            def prepare(n):
                u, j = divmod(n, NP)
                kind, _, _, rows, place = pieces[j]
                e = turn_order[n]
                dve.wait_ge(prep_hi, e + 1)
                src = ps_prep[:, e % 2].rearrange("p a b -> p (a b)")
                if kind == "k":
                    nc.vector.tensor_tensor(kT_lo[u % 2][:, place:place + rows], src[:, 0:rows],
                                            kT_hi[u % 2][:, place:place + rows].bitcast(F32),
                                            ALU.subtract).then_inc(prep_lo, 1)
                else:
                    ch = rows // CHUNK
                    srcq = src[:, 0:rows].rearrange("p (c q) -> p c q", q=CHUNK)
                    for a in (0, CHUNK):
                        part = (slice(a, a + CHUNK), slice(place, place + ch), slice(a, a + CHUNK))
                        last = nc.vector.scalar_tensor_tensor(qT_lo[u % 2][part], srcq[a:a + CHUNK], QSCALE,
                                                              qT_hi[u % 2][part].bitcast(F32), ALU.mult,
                                                              ALU.subtract)
                    last.then_inc(prep_lo, 1)

            def sum_softplus(s):
                q = 2 * (s - SB0)
                dve.wait_ge(kept, s - SB0 + 1)
                nc.vector.tensor_tensor(w(s), z(s), w(s), ALU.max).then_inc(summed, 1)
                dve.wait_ge(summed, q + 1)
                back = w(s)[:, ::-1]
                nc.vector.tensor_tensor_scan(back, back, back, 0.0, ALU.add, ALU.bypass).then_inc(summed, 1)

            def read_scores(s):
                n = keys(s)
                if is_diff(s):
                    if s % NC == 0:
                        u = s // NC
                        if u == 0:
                            dve.wait_ge(tables, TABLES)
                            nc.vector.scalar_tensor_tensor(bias, bias, -1.0, bias,
                                                           ALU.mult, ALU.min).then_inc(bias_done, 1)
                            dve.wait_ge(bias_done, 1)
                        else:
                            dve.wait_ge(biased, seg0[s])
                        nc.vector.tensor_scalar(bias, bias, 0.25, None, ALU.mult).then_inc(bias_done, 1)
                        dve.wait_ge(bias_done, u + 2)
                    if z_over[s] >= 0:
                        dve.wait_ge(a_turned, grp0[z_over[s] + 1])
                    if s >= STATS:
                        dve.wait_ge(max_ready, s - STATS + 1)
                    for b, (a, m) in enumerate(segments(s)):
                        e = seg0[s] + b
                        dve.wait_ge(scored, e + 1)
                        off = LIVE - n + a
                        nc.vector.tensor_tensor_reduce(z(s, a, m), ps_z[:, e % 2, 0:m], bias[:, off:off + m],
                                                       1.0, -3e38, ALU.add, ALU.max,
                                                       seg_max[:, s % STATS, b:b + 1]).then_inc(biased, 1)
                else:
                    dve.wait_ge(copied, seg0[s + 1] - seg0[SB0])
                    if w_over[s] >= SB0:
                        dve.wait_ge(exponents, w_over[s] - SB0 + 1)
                    else:
                        dve.wait_ge(biased, seg0[SB0])
                    nc.vector.tensor_scalar(w(s), z(s), SOFTPLUS_LINEAR, None, ALU.min).then_inc(clamped, 1)

            def split(s):
                for g, bl in enumerate(groups(s)):
                    e = grp0[s] + g
                    dve.wait_ge(a_hi, e + 1)
                    f = sum(m == P for _, m in bl)
                    if f:
                        last = nc.vector.tensor_tensor(aT_lo[:, e % TURNED, 0:f], ps_aT[:, e % 2, 0:f],
                                                       aT_hi[:, e % TURNED, 0:f].bitcast(F32), ALU.subtract)
                    if f < len(bl):
                        m = bl[f][1]
                        last = nc.vector.tensor_tensor(aT_lo[0:m, e % TURNED, f], ps_aT[0:m, e % 2, f],
                                                       aT_hi[0:m, e % TURNED, f].bitcast(F32), ALU.subtract)
                    last.then_inc(a_lo, 1)
                if is_diff(s):
                    dve.wait_ge(weights, s + 1)
                    nc.vector.reciprocal(stat(inv_sum, s), stat(row_sum, s)).then_inc(inv_done, 1)

            def output(s):
                o, half = o_sb[:, s % 4], ps_o[:, s % 2, P:2 * P]
                if is_diff(s):
                    dve.wait_ge(o_half, s + 1)
                    nc.vector.scalar_tensor_tensor(o, half, stat(inv_sum, s), o, ALU.mult,
                                                   ALU.add).then_inc(o_done, 1)
                else:
                    dve.wait_ge(a_used, grp0[s + 1])
                    dve.wait_ge(o_stored[s % 4], 32 * (s // 4))
                    halves = ps_o[:, s % 2, 0:2 * P].rearrange("p (a n) -> p n a", a=2)
                    nc.vector.tensor_reduce(o, halves, AX.X, ALU.add).then_inc(o_done, 1)

            for s in steps:
                for n in pieces_in.get(s, ()):
                    if n in turn_order:
                        prepare(n)
                if 0 <= s + 3 and is_diff(s + 3):
                    read_scores(s + 3)
                if 0 <= s < NTASK:
                    split(s)
                if 0 <= s - 2:
                    output(s - 2)
                if is_sb(s + 3):
                    read_scores(s + 3)
                if is_sb(s + 2):
                    sum_softplus(s + 2)

        @block.tensor
        def _(pe):
            def prepare(n):
                rows = pieces[n % NP][3]
                e = turn_order[n]
                pe.wait_ge(raw_loaded[n % RAW], 16 * (n // RAW + 1))
                if e >= 2:
                    pe.wait_ge(prep_lo, e - 1)
                for i in range(max(1, rows // P)):
                    m = min(P, rows)
                    last = nc.tensor.transpose(ps_prep[:, e % 2, i, 0:m], raw[0:m, n % RAW, i], t["ident"][0:m, 0:m])
                last.then_inc(prep_turned, 1)

            def score(s, first, last):
                u, c = divmod(s, NC)
                if c == 0 and first == 0:
                    pe.wait_ge(prep_lo, sum(n < NP * (u + 1) for n in turn_order))
                    pe.wait_ge(v_lo, sum(n < NP * (u + 1) for n in value_order))
                if s == SB0 and first == 0:
                    pe.wait_ge(mask_ready, 1)
                q_hi, q_lo = qT_hi[u % 2][:, c], qT_lo[u % 2][:, c]
                for b, (a, n) in list(enumerate(segments(s)))[first:last]:
                    e = seg0[s] + b
                    if e >= 2:
                        if e - 2 < seg0[SB0]:
                            pe.wait_ge(biased, e - 1)
                        else:
                            pe.wait_ge(copied, e - 1 - seg0[SB0])
                    out = ps_z[:, e % 2, 0:n]
                    k0 = key_base(s) + a
                    k_hi, k_lo = kT_hi[u % 2][:, k0:k0 + n], kT_lo[u % 2][:, k0:k0 + n]
                    nc.tensor.matmul(out, q_hi, k_hi, start=True, stop=False)
                    nc.tensor.matmul(out, q_hi, k_lo, start=False, stop=False)
                    if is_sb(s) and a + n == keys(s):
                        nc.tensor.matmul(out[:, n - CHUNK:n], ident_r[:], mask_r[:], start=False, stop=False)
                    nc.tensor.matmul(out, q_lo, k_hi, start=False, stop=True).then_inc(scored, 1)

            def turn(s, g):
                e = grp0[s] + g
                if g == 0:
                    pe.wait_ge(weights, s + 1)
                if e >= 2:
                    pe.wait_ge(a_lo, e - 1)
                for i, (b, m) in enumerate(groups(s)[g]):
                    last = nc.tensor.transpose(ps_aT[0:m, e % 2, i], z(s, b, m), t["ident"][:, :])
                last.then_inc(a_turned, 1)

            def values(s, g):
                u = s // NC
                e = grp0[s] + g
                pe.wait_ge(a_lo, e + 1)
                if g == 0 and s >= 2:
                    pe.wait_ge(o_done, s - 1)
                out = ps_o[:, s % 2, 0:2 * P]
                for i, (b, m) in enumerate(groups(s)[g]):
                    rhs = v[u % 2][0:m, (key_base(s) + b) // P].rearrange("p a n -> p (a n)")
                    nc.tensor.matmul(out, aT_hi[0:m, e % TURNED, i], rhs, start=(b == 0), stop=False)
                    last = nc.tensor.matmul(out, aT_lo[0:m, e % TURNED, i], rhs,
                                            start=False, stop=(b + m == keys(s)))
                last.then_inc(a_used, 1)

            for s in steps:
                for n in pieces_in.get(s, ()):
                    if n in turn_order:
                        prepare(n)
                turns = [(turn, s, g) for g in range(len(groups(s)))] if 0 <= s < NTASK else []
                uses = [(values, s - 1, g) for g in range(len(groups(s - 1)))] if 1 <= s <= NTASK else []
                for i in range(max(len(turns), len(uses))):
                    for f, x, g in turns[i:i + 1] + uses[i:i + 1]:
                        f(x, g)
                if 0 <= s + 3 < NTASK:
                    score(s + 3, 2, None)
                if 0 <= s + 4 < NTASK:
                    score(s + 4, 0, 2)


def mix(nc, t, h_all):
    tiles = token_tiles(t["seq"], t["dec"])
    NT = len(tiles)
    D = t["x_prompt"].shape[1]
    KD = D // P
    DW = t["mixed1"].shape[1]
    NH = DW // P
    w_out = t["w_out"].rearrange("(k p) n -> p k n", p=P)
    with ExitStack() as ctx:
        def sbuf(name, shape, dtype=F32):
            return ctx.enter_context(nc.sbuf_tensor(name, shape, dtype))

        def psum(name, shape):
            return ctx.enter_context(nc.psum_tensor(name, shape, F32))

        def sem(name):
            return ctx.enter_context(nc.semaphore(name))

        m0 = sbuf("m0", [P, 2, D])
        m1 = sbuf("m1", [P, 2, DW])
        squares = sbuf("squares3", [P, DW])
        lambdas = sbuf("lambdas", [P, 4, 64])
        lam_prod = sbuf("lam_prod", [P, 2, 64])
        lam = sbuf("lam", [P, 8])
        subln = sbuf("subln", [P, P])
        head_sq = sbuf("head_sq", [P, NT, NH])
        head_ms = sbuf("head_ms", [P, NT, NH])
        head_rstd = sbuf("head_rstd", [P, NT, NH])
        wo_raw = sbuf("wo_raw", [P, KD, D])
        wo_hi = sbuf("wo_hi", [P, KD, D], F32R)
        wo_lo = sbuf("wo_lo", [P, KD, D], F32R)
        mT_hi = sbuf("mT_hi", [P, 2, KD, P], F32R)
        mT_lo = sbuf("mT_lo", [P, 2, KD, P], F32R)
        ps_turn = psum("ps_turn3", [P, 4, 4, P])
        ps_h = psum("ps_h", [P, 4, BANK])
        m_loaded = [sem(f"m_loaded{i}") for i in range(2)]
        h_loaded = sem("h_loaded")
        wo_loaded = sem("wo_loaded")
        small_loaded = sem("small_loaded")
        lam_dve = sem("lam_dve")
        lam_act = sem("lam_act")
        combined = sem("combined")
        head_rstd_done = sem("head_rstd_done")
        wo_hi_done = sem("wo_hi_done")
        wo_lo_done = sem("wo_lo_done")
        turned = sem("turned3")
        m_hi = sem("m_hi")
        m_lo = sem("m_lo")
        multiplied = sem("multiplied")
        h_added = sem("h_added")
        block = ctx.enter_context(nc.Block())

        @block.sync
        def _(sp):
            for j, name in enumerate(("lambda_q1", "lambda_k1", "lambda_q2", "lambda_k2")):
                sp.dma_start(lambdas[:, j], t[name].partition_broadcast(P)).then_inc(small_loaded, 16)
            sp.dma_start(subln[:], t["diff_subln_g"].partition_broadcast(P)).then_inc(small_loaded, 16)
            for i in range(NT):
                t0, n = tiles[i]
                if i >= 2:
                    sp.wait_ge(turned, 2 * (i - 1))
                sp.dma_start(m0[0:n, i % 2], t["mixed"][t0:t0 + n, :]).then_inc(m_loaded[i % 2], 16)
                sp.dma_start(m1[0:n, i % 2], t["mixed1"][t0:t0 + n, :]).then_inc(m_loaded[i % 2], 16)
                if i == 0:
                    for k in range(KD):
                        sp.dma_start(wo_raw[:, k], w_out[:, k]).then_inc(wo_loaded, 16)
                    for j in range(NT):
                        m = tiles[j][1]
                        sp.dma_start(h_all[0:m, j], split_rows(tiles, t["x_prompt"], t["x_sample"], j)) \
                            .then_inc(h_loaded, 16)

        @block.gpsimd
        def _(pool):
            def rstd(i):
                n = tiles[i][1]
                pool.wait_ge(combined, 6 * i + 3)
                rstd_pool(nc, pool, head_ms[0:n, i], head_sq[0:n, i], head_rstd[0:n, i],
                          t["neg_half"][0:n, 0:NH], P, head_rstd_done, i)

            rstd(0)
            for k in range(KD):
                pool.wait_ge(wo_hi_done, k + 1)
                nc.gpsimd.tensor_tensor(wo_lo[:, k], wo_raw[:, k], wo_hi[:, k].bitcast(F32),
                                        ALU.subtract).then_inc(wo_lo_done, 1)
                if k == 0:
                    rstd(1)
            for i in range(2, NT):
                rstd(i)

        @block.scalar
        def _(act):
            act.wait_ge(lam_dve, 2)
            nc.scalar.activation(lam[:, 2:4], lam[:, 0:2], ACT.Exp).then_inc(lam_act, 1)
            for i in range(NT):
                n = tiles[i][1]
                for j in range(2):
                    q = 2 * i + j
                    act.wait_ge(turned, q + 1)
                    if i >= 2:
                        act.wait_ge(multiplied, 2 * (i - 1))
                    nc.scalar.copy(mT_hi[:, i % 2, 4 * j:4 * j + 4, 0:n], ps_turn[:, q % 4, :, 0:n]).then_inc(m_hi, 1)

        @block.vector
        def _(dve):
            dve.wait_ge(small_loaded, 80)
            for j in range(2):
                nc.vector.tensor_tensor_reduce(lam_prod[:, j], lambdas[:, 2 * j], lambdas[:, 2 * j + 1], 1.0, 0.0,
                                               ALU.mult, ALU.add, lam[:, j:j + 1]).then_inc(lam_dve, 1)
            dve.wait_ge(lam_act, 1)
            nc.vector.tensor_tensor(lam[:, 4:5], lam[:, 3:4], lam[:, 2:3], ALU.subtract).then_inc(lam_dve, 1)
            dve.wait_ge(lam_dve, 3)
            nc.vector.tensor_scalar(lam[:, 5:6], lam[:, 4:5], -LAM_INIT, None, ALU.add).then_inc(lam_dve, 1)
            nc.vector.tensor_scalar(subln[:], subln[:], 1.0 - LAM_INIT, None, ALU.mult).then_inc(lam_dve, 1)
            dve.wait_ge(lam_dve, 5)

            def combine(i):
                n = tiles[i][1]
                d = m0[0:n, i % 2, 0:DW]
                dh = d.rearrange("p (h v) -> p h v", h=NH)
                dve.wait_ge(m_loaded[i % 2], 32 * (i // 2 + 1))
                nc.vector.scalar_tensor_tensor(d, m1[0:n, i % 2], lam[0:n, 5:6], d, ALU.mult,
                                               ALU.add).then_inc(combined, 1)
                dve.wait_ge(combined, 6 * i + 1)
                nc.vector.tensor_tensor(squares[0:n], d, d, ALU.mult).then_inc(combined, 1)
                dve.wait_ge(combined, 6 * i + 2)
                nc.vector.tensor_reduce(head_sq[0:n, i], squares[0:n].rearrange("p (h v) -> p h v", h=NH),
                                        AX.X, ALU.add).then_inc(combined, 1)
                nc.vector.tensor_tensor(dh, dh, subln[0:n].unsqueeze(1).to_broadcast([n, NH, P]),
                                        ALU.mult).then_inc(combined, 1)
                dve.wait_ge(combined, 6 * i + 4)
                dve.wait_ge(head_rstd_done, 2 * (i + 1))
                nc.vector.tensor_tensor(dh, dh, head_rstd[0:n, i].unsqueeze(2).to_broadcast([n, NH, P]),
                                        ALU.mult).then_inc(combined, 2)

            def split(i):
                n = tiles[i][1]
                for j in range(2):
                    q = 2 * i + j
                    dve.wait_ge(m_hi, q + 1)
                    nc.vector.tensor_tensor(mT_lo[:, i % 2, 4 * j:4 * j + 4, 0:n], ps_turn[:, q % 4, :, 0:n],
                                            mT_hi[:, i % 2, 4 * j:4 * j + 4, 0:n].bitcast(F32),
                                            ALU.subtract).then_inc(m_lo, 1)

            def add(i):
                n = tiles[i][1]
                for j in range(2):
                    m = 2 * i + j
                    dve.wait_ge(multiplied, m + 1)
                    hh = h_all[0:n, i, j * BANK:(j + 1) * BANK]
                    nc.vector.tensor_tensor(hh, ps_h[0:n, m % 4], hh, ALU.add).then_inc(h_added, 1)

            combine(0)
            for k in range(KD):
                dve.wait_ge(wo_loaded, 16 * KD)
                nc.vector.tensor_copy(wo_hi[:, k], wo_raw[:, k]).then_inc(wo_hi_done, 1)
            dve.wait_ge(h_loaded, 16 * NT)
            for i in range(NT):
                if i + 1 < NT:
                    combine(i + 1)
                split(i)
                if i >= 1:
                    add(i - 1)
            add(NT - 1)

        @block.tensor
        def _(pe):
            def turn(i):
                n = tiles[i][1]
                pe.wait_ge(combined, 6 * i + 6)
                for j in range(2):
                    q = 2 * i + j
                    if q >= 4:
                        pe.wait_ge(m_lo, q - 3)
                    for k in range(4):
                        c = (4 * j + k) * P
                        last = nc.tensor.transpose(ps_turn[:, q % 4, k, 0:n], m0[0:n, i % 2, c:c + P],
                                                   t["ident"][0:n, 0:n])
                    last.then_inc(turned, 1)

            turn(0)
            for i in range(NT):
                n = tiles[i][1]
                if i + 1 < NT:
                    turn(i + 1)
                pe.wait_ge(m_lo, 2 * (i + 1))
                for j in range(2):
                    m = 2 * i + j
                    if m >= 4:
                        pe.wait_ge(h_added, m - 3)
                    for k in range(KD):
                        if m == 0:
                            pe.wait_ge(wo_lo_done, k + 1)
                        out = ps_h[0:n, m % 4]
                        b_hi, b_lo = (x[:, k, j * BANK:(j + 1) * BANK] for x in (wo_hi, wo_lo))
                        nc.tensor.matmul(out, mT_hi[:, i % 2, k, 0:n], b_hi, start=(k == 0), stop=False)
                        nc.tensor.matmul(out, mT_hi[:, i % 2, k, 0:n], b_lo, start=False, stop=False)
                        last = nc.tensor.matmul(out, mT_lo[:, i % 2, k, 0:n], b_hi, start=False, stop=(k == KD - 1))
                    last.then_inc(multiplied, 1)


def norm_turn(nc, t, h_all, nT_hi, nT_lo):
    tiles = token_tiles(t["seq"], t["dec"])
    NT = len(tiles)
    D = h_all.shape[2]
    with ExitStack() as ctx:
        def sbuf(name, shape, dtype=F32):
            return ctx.enter_context(nc.sbuf_tensor(name, shape, dtype))

        def psum(name, shape):
            return ctx.enter_context(nc.psum_tensor(name, shape, F32))

        def sem(name):
            return ctx.enter_context(nc.semaphore(name))

        xn = sbuf("xn4", [P, 2, D])
        squares = sbuf("squares4", [P, D])
        g_sb = sbuf("g4", [P, D])
        sumsq = sbuf("sumsq4", [P, NT])
        ms = sbuf("ms4", [P, NT])
        rstd = sbuf("rstd4", [P, NT])
        ps_turn = psum("ps_turn4", [P, 4, 4, P])
        g_loaded = sem("g_loaded4")
        squared = sem("squared4")
        rstd_done = sem("rstd_done4")
        normed = sem("normed4")
        turned = sem("turned4")
        n_hi = sem("n_hi4")
        n_lo = sem("n_lo4")
        block = ctx.enter_context(nc.Block())
        @block.sync
        def _(sp):
            sp.dma_start(g_sb[:], t["norm_ffn_g"].partition_broadcast(P)).then_inc(g_loaded, 16)

        @block.gpsimd
        def _(pool):
            for i in range(NT):
                n = tiles[i][1]
                pool.wait_ge(squared, i + 1)
                rstd_pool(nc, pool, ms[0:n, i:i + 1], sumsq[0:n, i:i + 1], rstd[0:n, i:i + 1],
                          t["neg_half"][0:n, 0:1], D, rstd_done, i)

        @block.scalar
        def _(act):
            def square(i):
                n = tiles[i][1]
                norm_rows_act(nc, act, h_all[0:n, i], squares[0:n], sumsq[0:n, i:i + 1], squared, i)

            square(0)
            square(1)
            for i in range(NT):
                t0, n = tiles[i]
                if i + 2 < NT:
                    square(i + 2)
                for j in range(2):
                    q = 2 * i + j
                    act.wait_ge(turned, q + 1)
                    nc.scalar.copy(nT_hi[:, 4 * j:4 * j + 4, t0:t0 + n], ps_turn[:, q % 4, :, 0:n]).then_inc(n_hi, 1)

        @block.vector
        def _(dve):
            def norm(i):
                n = tiles[i][1]
                dve.wait_ge(rstd_done, 2 * (i + 1))
                if i == 0:
                    dve.wait_ge(g_loaded, 16)
                if i >= 2:
                    dve.wait_ge(turned, 2 * (i - 1))
                nc.vector.scalar_tensor_tensor(xn[0:n, i % 2], h_all[0:n, i], rstd[0:n, i:i + 1], g_sb[0:n],
                                               ALU.mult, ALU.mult).then_inc(normed, 1)

            norm(0)
            for i in range(NT):
                t0, n = tiles[i]
                if i + 1 < NT:
                    norm(i + 1)
                for j in range(2):
                    q = 2 * i + j
                    dve.wait_ge(n_hi, q + 1)
                    nc.vector.tensor_tensor(nT_lo[:, 4 * j:4 * j + 4, t0:t0 + n], ps_turn[:, q % 4, :, 0:n],
                                            nT_hi[:, 4 * j:4 * j + 4, t0:t0 + n].bitcast(F32),
                                            ALU.subtract).then_inc(n_lo, 1)

        @block.tensor
        def _(pe):
            for i in range(NT):
                n = tiles[i][1]
                pe.wait_ge(normed, i + 1)
                for j in range(2):
                    q = 2 * i + j
                    if q >= 4:
                        pe.wait_ge(n_lo, q - 3)
                    for k in range(4):
                        c = (4 * j + k) * P
                        last = nc.tensor.transpose(ps_turn[:, q % 4, k, 0:n], xn[0:n, i % 2, c:c + P],
                                                   t["ident"][0:n, 0:n])
                    last.then_inc(turned, 1)


def feed(nc, t, h_all, nT_hi, nT_lo):
    tiles = token_tiles(t["seq"], t["dec"])
    NT, T = len(tiles), t["seq"] + t["dec"]
    D = h_all.shape[2]
    KD = D // P
    NF = t["w_gate"].shape[1] // P
    parts = 3
    width = -(-T // parts // 2) * 2
    chunks = [(a, min(width, T - a)) for a in range(0, T, width)]
    G = NF // 2
    NY = 2 * NT
    w_gate = t["w_gate"].rearrange("(k p) n -> p k n", p=P)
    w_up = t["w_up"].rearrange("(k p) n -> p k n", p=P)
    with ExitStack() as ctx:
        def sbuf(name, shape, dtype=F32):
            return ctx.enter_context(nc.sbuf_tensor(name, shape, dtype))

        def psum(name, shape):
            return ctx.enter_context(nc.psum_tensor(name, shape, F32))

        def sem(name):
            return ctx.enter_context(nc.semaphore(name))

        gu_raw = sbuf("gu_raw", [P, KD, 2, P])
        gu_hi = sbuf("gu_hi", [P, 2, KD, 2, P], F32R)
        gu_lo = sbuf("gu_lo", [P, 2, KD, 2, P], F32R)
        wd_raw = sbuf("wd_raw", [P, D])
        wd_hi = sbuf("wd_hi", [P, 3, D], F32R)
        wd_lo = sbuf("wd_lo", [P, 3, D], F32R)
        gate = sbuf("gate", [P, 2, width])
        hidden = sbuf("hidden", [P, 2, width])
        hT_hi = sbuf("hT_hi", [P, 3, T], F32R)
        hT_lo = sbuf("hT_lo", [P, 3, T], F32R)
        ps_g = psum("ps_g", [P, 2, BANK])
        ps_u = psum("ps_u", [P, 2, BANK])
        ps_y = psum("ps_y", [P, 4, BANK])
        gu_loaded = sem("gu_loaded")
        wd_loaded = sem("wd_loaded")
        gu_hi_done = sem("gu_hi_done")
        gu_lo_done = sem("gu_lo_done")
        wd_hi_done = sem("wd_hi_done")
        wd_lo_done = sem("wd_lo_done")
        gu_done = sem("gu_done")
        silu_done = sem("silu_done")
        hidden_done = sem("hidden_done")
        hid_hi = sem("hid_hi")
        hid_lo = sem("hid_lo")
        y_done = sem("y_done")
        y_added = sem("y_added")
        block = ctx.enter_context(nc.Block())
        C = len(chunks)

        @block.sync
        def _(sp):
            for f in range(NF):
                if f >= 1:
                    sp.wait_ge(gu_lo_done, f)
                sp.dma_start(gu_raw[:, :, 0], w_gate[:, :, f * P:(f + 1) * P]).then_inc(gu_loaded, 16)
                sp.dma_start(gu_raw[:, :, 1], w_up[:, :, f * P:(f + 1) * P]).then_inc(gu_loaded, 16)
                if f >= 1:
                    sp.wait_ge(wd_lo_done, f)
                sp.dma_start(wd_raw[:], t["w_down"][f * P:(f + 1) * P, :]).then_inc(wd_loaded, 16)

        @block.gpsimd
        def _(pool):
            def split_gu(f):
                pool.wait_ge(gu_hi_done, f + 1)
                nc.gpsimd.tensor_tensor(gu_lo[:, f % 2].rearrange("p k w n -> p (k w n)"),
                                        gu_raw[:].rearrange("p k w n -> p (k w n)"),
                                        gu_hi[:, f % 2].bitcast(F32).rearrange("p k w n -> p (k w n)"),
                                        ALU.subtract).then_inc(gu_lo_done, 1)

            def split_wd(f):
                pool.wait_ge(wd_hi_done, f + 1)
                nc.gpsimd.tensor_tensor(wd_lo[:, f % 3], wd_raw[:], wd_hi[:, f % 3].bitcast(F32),
                                        ALU.subtract).then_inc(wd_lo_done, 1)

            split_gu(0)
            split_wd(0)
            split_gu(1)
            for f in range(NF):
                for c, (a, n) in enumerate(chunks):
                    q = C * f + c
                    pool.wait_ge(hid_hi, q + 1)
                    nc.gpsimd.tensor_tensor(hT_lo[:, f % 3, a:a + n], hidden[:, q % 2, 0:n],
                                            hT_hi[:, f % 3, a:a + n].bitcast(F32), ALU.subtract).then_inc(hid_lo, 1)
                if f + 2 < NF:
                    split_gu(f + 2)
                if f + 1 < NF:
                    split_wd(f + 1)

        @block.scalar
        def _(act):
            for q in range(C * NF):
                f, c = divmod(q, C)
                a, n = chunks[c]
                act.wait_ge(gu_done, q + 1)
                if q >= 2:
                    act.wait_ge(hidden_done, q - 1)
                nc.scalar.activation(gate[:, q % 2, 0:n], ps_g[:, q % 2, 0:n], ACT.Silu).then_inc(silu_done, 1)
                act.wait_ge(hidden_done, q + 1)
                if f >= 3 and c == 0:
                    act.wait_ge(y_done, NY * ((f - 3) // 2 + 1))
                nc.scalar.copy(hT_hi[:, f % 3, a:a + n], hidden[:, q % 2, 0:n]).then_inc(hid_hi, 1)

        @block.vector
        def _(dve):
            def split_gu(f):
                dve.wait_ge(gu_loaded, 32 * (f + 1))
                if f >= 2:
                    dve.wait_ge(gu_done, C * (f - 1))
                nc.vector.tensor_copy(gu_hi[:, f % 2].rearrange("p k w n -> p (k w n)"),
                                      gu_raw[:].rearrange("p k w n -> p (k w n)")).then_inc(gu_hi_done, 1)

            def split_wd(f):
                dve.wait_ge(wd_loaded, 16 * (f + 1))
                if f >= 3:
                    dve.wait_ge(y_done, NY * ((f - 3) // 2 + 1))
                nc.vector.tensor_copy(wd_hi[:, f % 3], wd_raw[:]).then_inc(wd_hi_done, 1)

            def add(g):
                for i in range(NT):
                    n = tiles[i][1]
                    for j in range(2):
                        y = NY * g + 2 * i + j
                        dve.wait_ge(y_done, y + 1)
                        hh = h_all[0:n, i, j * BANK:(j + 1) * BANK]
                        nc.vector.tensor_tensor(hh, ps_y[0:n, y % 4], hh, ALU.add).then_inc(y_added, 1)

            split_gu(0)
            split_wd(0)
            split_gu(1)
            for f in range(NF):
                for c, (a, n) in enumerate(chunks):
                    q = C * f + c
                    dve.wait_ge(silu_done, q + 1)
                    if q >= 2:
                        dve.wait_ge(hid_lo, q - 1)
                    nc.vector.tensor_tensor(hidden[:, q % 2, 0:n], ps_u[:, q % 2, 0:n], gate[:, q % 2, 0:n],
                                            ALU.mult).then_inc(hidden_done, 1)
                if f % 2 == 0 and f >= 2:
                    add(f // 2 - 1)
                if f + 2 < NF:
                    split_gu(f + 2)
                if f + 1 < NF:
                    split_wd(f + 1)
            add(G - 1)

        @block.tensor
        def _(pe):
            def up(f):
                pe.wait_ge(gu_lo_done, f + 1)
                for c, (a, n) in enumerate(chunks):
                    q = C * f + c
                    if q >= 2:
                        pe.wait_ge(hidden_done, q - 1)
                    for w, ps in ((0, ps_g), (1, ps_u)):
                        out = ps[:, q % 2, 0:n]
                        for k in range(KD):
                            w_h, w_l = gu_hi[:, f % 2, k, w], gu_lo[:, f % 2, k, w]
                            x_h, x_l = nT_hi[:, k, a:a + n], nT_lo[:, k, a:a + n]
                            nc.tensor.matmul(out, w_h, x_h, start=(k == 0), stop=False)
                            nc.tensor.matmul(out, w_h, x_l, start=False, stop=False)
                            last = nc.tensor.matmul(out, w_l, x_h, start=False, stop=(k == KD - 1))
                    last.then_inc(gu_done, 1)

            def down(g):
                pe.wait_ge(hid_lo, C * (2 * g + 2))
                pe.wait_ge(wd_lo_done, 2 * g + 2)
                for i in range(NT):
                    t0, n = tiles[i]
                    for j in range(2):
                        y = NY * g + 2 * i + j
                        if y >= 4:
                            pe.wait_ge(y_added, y - 3)
                        out = ps_y[0:n, y % 4]
                        for f in (2 * g, 2 * g + 1):
                            h_h, h_l = hT_hi[:, f % 3, t0:t0 + n], hT_lo[:, f % 3, t0:t0 + n]
                            b_h, b_l = (x[:, f % 3, j * BANK:(j + 1) * BANK] for x in (wd_hi, wd_lo))
                            nc.tensor.matmul(out, h_h, b_h, start=(f == 2 * g), stop=False)
                            nc.tensor.matmul(out, h_h, b_l, start=False, stop=False)
                            last = nc.tensor.matmul(out, h_l, b_h, start=False, stop=(f == 2 * g + 1))
                        last.then_inc(y_done, 1)

            for f in range(NF):
                up(f)
                if f % 2 == 0 and f >= 2:
                    down(f // 2 - 1)
            down(G - 1)


def final(nc, t, h_all):
    tiles = token_tiles(t["seq"], t["dec"])
    NT = len(tiles)
    D = h_all.shape[2]
    with ExitStack() as ctx:
        def sbuf(name, shape, dtype=F32):
            return ctx.enter_context(nc.sbuf_tensor(name, shape, dtype))

        def psum(name, shape):
            return ctx.enter_context(nc.psum_tensor(name, shape, F32))

        def sem(name):
            return ctx.enter_context(nc.semaphore(name))

        y_sb = sbuf("y_sb", [P, 2, D])
        squares = sbuf("squares5", [P, D])
        g_sb = sbuf("g5", [P, D])
        sumsq = sbuf("sumsq5", [P, NT])
        ms = sbuf("ms5", [P, NT])
        rstd = sbuf("rstd5", [P, NT])
        g_loaded = sem("g_loaded5")
        squared = sem("squared5")
        rstd_done = sem("rstd_done5")
        y_normed = sem("y_normed")
        y_stored = [sem(f"y_stored{i}") for i in range(2)]
        block = ctx.enter_context(nc.Block())

        @block.sync
        def _(sp):
            sp.dma_start(g_sb[:], t["norm_final_g"].partition_broadcast(P)).then_inc(g_loaded, 16)
            for i in range(NT):
                n = tiles[i][1]
                sp.wait_ge(y_normed, i + 1)
                sp.dma_start(split_rows(tiles, t["y_prompt"], t["y_sample"], i), y_sb[0:n, i % 2]) \
                    .then_inc(y_stored[i % 2], 16)
            for s in range(2):
                sp.wait_ge(y_stored[s], 16 * len(range(s, NT, 2)))

        @block.gpsimd
        def _(pool):
            for i in range(NT):
                n = tiles[i][1]
                pool.wait_ge(squared, i + 1)
                rstd_pool(nc, pool, ms[0:n, i:i + 1], sumsq[0:n, i:i + 1], rstd[0:n, i:i + 1],
                          t["neg_half"][0:n, 0:1], D, rstd_done, i)

        @block.scalar
        def _(act):
            for i in range(NT):
                n = tiles[i][1]
                norm_rows_act(nc, act, h_all[0:n, i], squares[0:n], sumsq[0:n, i:i + 1], squared, i)

        @block.vector
        def _(dve):
            dve.wait_ge(g_loaded, 16)
            for i in range(NT):
                n = tiles[i][1]
                dve.wait_ge(rstd_done, 2 * (i + 1))
                if i >= 2:
                    dve.wait_ge(y_stored[i % 2], 16 * (i // 2))
                nc.vector.scalar_tensor_tensor(y_sb[0:n, i % 2], h_all[0:n, i], rstd[0:n, i:i + 1], g_sb[0:n],
                                               ALU.mult, ALU.mult).then_inc(y_normed, 1)


def encoder_step(nc, t):
    D = t["x_prompt"].shape[1]
    tiles = token_tiles(t["seq"], t["dec"])
    T = t["seq"] + t["dec"]
    with (
        nc.sbuf_tensor("ident", [P, P], F32) as ident,
        nc.sbuf_tensor("neg_half", [P, 4], F32) as neg_half,
    ):
        t["ident"], t["neg_half"] = ident, neg_half
        with nc.semaphore("cleared") as cleared, nc.Block() as block:
            @block.gpsimd
            def _(pool):
                nc.gpsimd.memset(ident[:], 0.0).then_inc(cleared, 1)
                nc.gpsimd.memset(neg_half[:], -0.5).then_inc(cleared, 1)
                pool.wait_ge(cleared, 2)
                nc.gpsimd.affine_select(out=ident[:], in_=ident[:], compare_op=ALU.not_equal, fill=1.0, base=0,
                                        pattern=[[-1, P]], channel_multiplier=1).then_inc(cleared, 1)
                pool.wait_ge(cleared, 3)
        project(nc, t)
        attend(nc, t)
        with nc.sbuf_tensor("h_all", [P, len(tiles), D], F32) as h_all:
            mix(nc, t, h_all)
            with (
                nc.sbuf_tensor("n2T_hi", [P, D // P, T], F32R) as nT_hi,
                nc.sbuf_tensor("n2T_lo", [P, D // P, T], F32R) as nT_lo,
            ):
                norm_turn(nc, t, h_all, nT_hi, nT_lo)
                feed(nc, t, h_all, nT_hi, nT_lo)
            final(nc, t, h_all)


_INS = ['x_prompt', 'x_sample', 'cache_diff_k', 'cache_diff_v', 'cache_sb_k', 'cache_sb_v', 'norm_attn_g', 'w_in',
        'lambda_q1', 'lambda_k1', 'lambda_q2', 'lambda_k2', 'diff_subln_g', 'w_out', 'norm_ffn_g', 'w_gate', 'w_up',
        'w_down', 'norm_final_g']
_OUTS = ['y_prompt', 'y_sample', 'prompt_diff_k', 'prompt_diff_v', 'prompt_sb_k', 'prompt_sb_v',
         'sample_diff_k', 'sample_diff_v', 'sample_sb_k', 'sample_sb_v']


def kernel(**inputs):
    import numpy as np
    import concourse.bacc as bacc
    from concourse.bass_utils import run_bass_kernel_spmd

    nc = bacc.Bacc("TRN2", target_bir_lowering=False, num_devices=1)
    xp, xs, ck = inputs["x_prompt"], inputs["x_sample"], inputs["cache_diff_k"]
    seq, dec, past, D = xp.shape[1], xs.shape[1], ck.shape[2], xp.shape[2]
    half = D // 2
    two_d = {"x_prompt": (seq, D), "x_sample": (dec, D), "w_in": inputs["w_in"].shape[1:],
             "w_out": inputs["w_out"].shape[1:], "w_gate": inputs["w_gate"].shape[1:],
             "w_up": inputs["w_up"].shape[1:], "w_down": inputs["w_down"].shape[1:]}
    for name in ("cache_diff_k", "cache_diff_v", "cache_sb_k", "cache_sb_v"):
        two_d[name] = (past, half)
    arrays, t = {}, {"seq": seq, "dec": dec, "past": past}
    for name in _INS:
        a = np.ascontiguousarray(np.asarray(inputs[name]))
        a = a.reshape(two_d.get(name, (a.size,)))
        arrays[f"in_{name}"] = a
        t[name] = nc.dram_tensor(f"in_{name}", a.shape, mybir.dt.from_np(a.dtype), kind="ExternalInput").ap()
    out_shapes = {"y_prompt": (seq, D), "y_sample": (dec, D)}
    for name in _OUTS:
        rows = seq if "prompt" in name else dec
        shape = out_shapes.get(name, (rows, half))
        t[name] = nc.dram_tensor(f"out_{name}", shape, F32, kind="ExternalOutput").ap()
    q_d = nc.dram_tensor("q_diff", (seq + dec, half), F32, kind="Internal").ap()
    q_s = nc.dram_tensor("q_sb", (seq + dec, half), F32, kind="Internal").ap()
    t["mixed"] = nc.dram_tensor("mixed", (seq + dec, D), F32, kind="Internal").ap()
    t["mixed1"] = nc.dram_tensor("mixed1", (seq + dec, half), F32, kind="Internal").ap()
    t["new_dq"], t["sample_dq"] = q_d[0:seq, :], q_d[seq:seq + dec, :]
    t["new_sq"], t["sample_sq"] = q_s[0:seq, :], q_s[seq:seq + dec, :]
    for side, name in (("d", "diff"), ("s", "sb")):
        for kind in "kv":
            t[f"new_{side}{kind}"] = t[f"prompt_{name}_{kind}"]
            t[f"sample_{side}{kind}"] = t[f"sample_{name}_{kind}"]
            t[f"cache_{side}{kind}"] = t[f"cache_{name}_{kind}"]
    t["proj_out"] = [(t[f"new_{side}{kind}"], t[f"sample_{side}{kind}"]) for side in "ds" for kind in "qkv"]
    encoder_step(nc, t)
    r = run_bass_kernel_spmd(nc, [arrays], core_ids=[0]).results[0]
    shapes = {"y_prompt": xp.shape, "y_sample": xs.shape}
    out = []
    for name in _OUTS:
        a = r[f"out_{name}"]
        if name not in shapes:
            heads = inputs["cache_diff_k" if "diff" in name else "cache_sb_k"].shape[3:]
            a = a.reshape((1, 1, a.shape[0]) + tuple(heads))
        else:
            a = a.reshape(shapes[name])
        out.append(a)
    return tuple(out)
```

```python
import math
from contextlib import ExitStack

import concourse.bass as bass
from concourse import mybir

F32 = mybir.dt.float32
F32R = mybir.dt.float32r
ALU = mybir.AluOpType
ACT = mybir.ActivationFunctionType
AX = mybir.AxisListType

P = 128
CHUNK = 64
EPS = 1e-6
NEG_INF = -1e30
LAM_INIT = 0.8 - 0.6 * math.exp(-0.3 * 0)
BANK = 512
SOFTPLUS_LINEAR = 40.0


def token_tiles(seq, dec):
    return [(i * P, P) for i in range(seq // P)] + [(seq, dec)]


def split_rows(tiles, prompt, sample, i):
    t0, n = tiles[i]
    return prompt[t0:t0 + n, :] if i < len(tiles) - 1 else sample[0:n, :]


def norm_rows_act(nc, act, src, junk, sumsq, done, count):
    if count:
        act.wait_ge(done, count)
    nc.scalar.activation(junk, src, ACT.Square, accum_out=sumsq).then_inc(done, 1)


def rstd_pool(nc, pool, ms, sumsq, rstd, neg_half, width, done, count):
    nc.gpsimd.tensor_scalar(ms, sumsq, 1.0 / width, EPS, ALU.mult, ALU.add).then_inc(done, 1)
    pool.wait_ge(done, 2 * count + 1)
    nc.gpsimd.tensor_tensor(rstd, ms, neg_half, ALU.pow).then_inc(done, 1)


def project(nc, t):
    tiles = token_tiles(t["seq"], t["dec"])
    NT, T = len(tiles), t["seq"] + t["dec"]
    D = t["x_prompt"].shape[1]
    KD = D // P
    NG = t["w_in"].shape[1] // BANK
    w_in = t["w_in"].rearrange("(k p) n -> p k n", p=P)
    with ExitStack() as ctx:
        def sbuf(name, shape, dtype=F32):
            return ctx.enter_context(nc.sbuf_tensor(name, shape, dtype))

        def psum(name, shape):
            return ctx.enter_context(nc.psum_tensor(name, shape, F32))

        def sem(name):
            return ctx.enter_context(nc.semaphore(name))

        x_sb = sbuf("x_sb", [P, 3, D])
        xn = sbuf("xn", [P, 2, D])
        squares = sbuf("squares", [P, D])
        g_sb = sbuf("g_sb", [P, D])
        sumsq = sbuf("sumsq", [P, NT])
        ms = sbuf("ms", [P, NT])
        rstd = sbuf("rstd", [P, NT])
        nT_hi = sbuf("nT_hi", [P, KD, T], F32R)
        nT_lo = sbuf("nT_lo", [P, KD, T], F32R)
        w_raw = sbuf("w_raw", [P, 2, KD, BANK])
        w_hi, w_lo = ([t["shared"][:, (2 * b + a) * KD * BANK:(2 * b + a + 1) * KD * BANK]
                       .rearrange("p (k n) -> p k n", k=KD) for b in range(2)] for a in range(2))
        out_sb = t["staging"][:, 0:4 * BANK].rearrange("p (s n) -> p s n", n=BANK)
        ps_turn = psum("ps_turn", [P, 4, 4, P])
        ps_proj = psum("ps_proj", [P, 4, BANK])
        x_loaded = [sem(f"x_loaded{i}") for i in range(3)]
        w_first_loaded = [sem(f"w_first_loaded{i}") for i in range(2)]
        w_loaded = [sem(f"w_loaded{i}") for i in range(2)]
        g_loaded = sem("g_loaded")
        squared = sem("squared")
        rstd_done = sem("rstd_done")
        normed = sem("normed")
        turned = sem("turned")
        n_hi = sem("n_hi")
        n_lo = sem("n_lo")
        w_hi_done = sem("w_hi_done")
        w_lo_done = sem("w_lo_done")
        w_lo_first = sem("w_lo_first")
        projected = sem("projected")
        evacuated = sem("evacuated")
        stored = [sem(f"stored{i}") for i in range(4)]
        block = ctx.enter_context(nc.Block())

        def lo_parts(g, k):
            return KD * g + k - KD // 2 if g else (k + 1) // 2

        @block.sync
        def _(sp):
            def load_w(g):
                if g >= 2:
                    sp.wait_ge(w_lo_done, lo_parts(g - 2, KD))
                    sp.wait_ge(w_lo_first, KD // 2)
                sp.dma_start(w_raw[:, g % 2], w_in[:, :, g * BANK:(g + 1) * BANK]).then_inc(w_loaded[g % 2], 16)

            for i in range(NT):
                n = tiles[i][1]
                if i >= 3:
                    sp.wait_ge(normed, i - 2)
                sp.dma_start(x_sb[0:n, i % 3], split_rows(tiles, t["x_prompt"], t["x_sample"], i)) \
                    .then_inc(x_loaded[i % 3], 16)
                if i == 0:
                    sp.dma_start(g_sb[:], t["norm_attn_g"].partition_broadcast(P)).then_inc(g_loaded, 16)
                if i < 2:
                    half = slice(i * KD // 2, (i + 1) * KD // 2)
                    sp.dma_start(w_raw[:, 0, half], w_in[:, half, 0:BANK]).then_inc(w_first_loaded[i], 16)
                if i == 2:
                    load_w(1)
            for g in range(2, NG):
                load_w(g)

        @block.gpsimd
        def _(pool):
            def split_w(g):
                for k in range(0, KD, 1 if g else 2):
                    pool.wait_ge(w_hi_done, KD * g + k + 1)
                    if g >= 2 and k == 0:
                        pool.wait_ge(projected, NT * (g - 1))
                    nc.gpsimd.tensor_tensor(w_lo[g % 2][:, k], w_raw[:, g % 2, k],
                                            w_hi[g % 2][:, k].bitcast(F32), ALU.subtract).then_inc(w_lo_done, 1)

            for i in range(NT):
                n = tiles[i][1]
                pool.wait_ge(squared, i + 1)
                rstd_pool(nc, pool, ms[0:n, i:i + 1], sumsq[0:n, i:i + 1], rstd[0:n, i:i + 1],
                          t["neg_half"][0:n, 0:1], D, rstd_done, i)
                if i == 0:
                    split_w(0)
            for g in range(1, NG):
                split_w(g)

        @block.scalar
        def _(act):
            def square(i):
                n = tiles[i][1]
                act.wait_ge(x_loaded[i % 3], 16 * (i // 3 + 1))
                norm_rows_act(nc, act, x_sb[0:n, i % 3], squares[0:n], sumsq[0:n, i:i + 1], squared, i)

            def store(m):
                g, i = divmod(m, NT)
                n = tiles[i][1]
                act.wait_ge(evacuated, m + 1)
                dst = split_rows(tiles, *t["proj_out"][g], i)
                act.dma_start(dst, out_sb[0:n, m % 4]).then_inc(stored[m % 4], 16)

            def evacuate(m):
                n = tiles[m % NT][1]
                act.wait_ge(projected, m + 1)
                if m >= 4:
                    act.wait_ge(stored[m % 4], 16 * (m // 4))
                nc.scalar.copy(out_sb[0:n, m % 4], ps_proj[0:n, m % 4]).then_inc(evacuated, 1)
                if m >= 1:
                    store(m - 1)

            square(0)
            for i in range(NT):
                t0, n = tiles[i]
                if 1 < i + 1 < NT:
                    square(i + 1)
                for j in range(2):
                    q = 2 * i + j
                    act.wait_ge(turned, q + 1)
                    nc.scalar.copy(nT_hi[:, 4 * j:4 * j + 4, t0:t0 + n], ps_turn[:, q % 4, :, 0:n]).then_inc(n_hi, 1)
                if i == 0:
                    square(1)
                if i >= 1:
                    evacuate(i - 1)
            for m in range(NT - 1, NG * NT):
                evacuate(m)
            store(NG * NT - 1)
            for s in range(4):
                act.wait_ge(stored[s], 16 * len(range(s, NG * NT, 4)))

        @block.vector
        def _(dve):
            def split_w(g):
                dve.wait_ge(w_loaded[g % 2], 16 * (g // 2 + g % 2))
                if g >= 2:
                    dve.wait_ge(projected, NT * (g - 1))
                for k in range(KD):
                    nc.vector.tensor_copy(w_hi[g % 2][:, k], w_raw[:, g % 2, k]).then_inc(w_hi_done, 1)

            def norm(i):
                n = tiles[i][1]
                dve.wait_ge(rstd_done, 2 * (i + 1))
                if i == 0:
                    dve.wait_ge(g_loaded, 16)
                if i >= 2:
                    dve.wait_ge(turned, 2 * (i - 1))
                nc.vector.scalar_tensor_tensor(xn[0:n, i % 2], x_sb[0:n, i % 3], rstd[0:n, i:i + 1], g_sb[0:n],
                                               ALU.mult, ALU.mult).then_inc(normed, 1)

            def split_n(i):
                t0, n = tiles[i]
                for j in range(2):
                    q = 2 * i + j
                    dve.wait_ge(n_hi, q + 1)
                    nc.vector.tensor_tensor(nT_lo[:, 4 * j:4 * j + 4, t0:t0 + n], ps_turn[:, q % 4, :, 0:n],
                                            nT_hi[:, 4 * j:4 * j + 4, t0:t0 + n].bitcast(F32),
                                            ALU.subtract).then_inc(n_lo, 1)

            norm(0)
            for half in range(2):
                dve.wait_ge(w_first_loaded[half], 16)
                for k in range(half * KD // 2, (half + 1) * KD // 2):
                    nc.vector.tensor_copy(w_hi[0][:, k], w_raw[:, 0, k]).then_inc(w_hi_done, 1)
                    if k % 2:
                        dve.wait_ge(w_hi_done, k + 1)
                        nc.vector.tensor_tensor(w_lo[0][:, k], w_raw[:, 0, k], w_hi[0][:, k].bitcast(F32),
                                                ALU.subtract).then_inc(w_lo_first, 1)
                if half == 0:
                    split_n(0)
            norm(1)
            for i in range(1, NT):
                if i + 1 < NT:
                    norm(i + 1)
                split_n(i)
            for g in range(1, NG):
                split_w(g)

        @block.tensor
        def _(pe):
            def turn(i):
                n = tiles[i][1]
                pe.wait_ge(normed, i + 1)
                for j in range(2):
                    q = 2 * i + j
                    if q >= 4:
                        pe.wait_ge(n_lo, q - 3)
                    for k in range(4):
                        c = (4 * j + k) * P
                        last = nc.tensor.transpose(ps_turn[:, q % 4, k, 0:n], xn[0:n, i % 2, c:c + P],
                                                   t["ident"][0:n, 0:n])
                    last.then_inc(turned, 1)

            turn(0)
            for g in range(NG):
                for i in range(NT):
                    if g == 0 and 1 < i + 1 < NT:
                        turn(i + 1)
                    t0, n = tiles[i]
                    m = g * NT + i
                    if g == 0:
                        pe.wait_ge(n_lo, 2 * (i + 1))
                    if m >= 4:
                        pe.wait_ge(evacuated, m - 3)
                    for k in range(KD):
                        if i == 0 and g == 0 and k % 2:
                            pe.wait_ge(w_lo_first, k // 2 + 1)
                        elif i == 0:
                            pe.wait_ge(w_lo_done, lo_parts(g, k + 1))
                        a_hi, a_lo = nT_hi[:, k, t0:t0 + n], nT_lo[:, k, t0:t0 + n]
                        b_hi, b_lo = w_hi[g % 2][:, k], w_lo[g % 2][:, k]
                        out = ps_proj[0:n, m % 4]
                        nc.tensor.matmul(out, a_hi, b_hi, start=(k == 0), stop=False)
                        nc.tensor.matmul(out, a_hi, b_lo, start=False, stop=False)
                        last = nc.tensor.matmul(out, a_lo, b_hi, start=False, stop=(k == KD - 1))
                    last.then_inc(projected, 1)
                    if m == 0:
                        turn(1)


def load_mixed(t, sp, i):
    t0, n = token_tiles(t["seq"], t["dec"])[i]
    sp.dma_start(t["m0"][0:n, i % 2], t["mixed"][t0:t0 + n, :]).then_inc(t["m_loaded"][i % 2], 16)
    sp.dma_start(t["m1"][0:n, i % 2], t["mixed1"][t0:t0 + n, :]).then_inc(t["m_loaded"][i % 2], 16)


def attend(nc, t):
    seq, dec, past = t["seq"], t["dec"], t["past"]
    NC = seq // CHUNK + 1
    NU, ND = 8, 4
    LIVE = past + dec
    NTASK = NU * NC
    SB0 = ND * NC
    VT = seq // P + -(-LIVE // P)
    QSCALE = 64 ** -0.5
    WIDE = 256
    MASK0 = WIDE - CHUNK
    RAW, TURNED, STATS = 6, 5, 4
    DISTANCES, TABLES = 2, 11

    def keys(s):
        c = s % NC
        return CHUNK * (c + 1) if c < NC - 1 else LIVE

    def blocks(s):
        return [(b, min(P, keys(s) - b)) for b in range(0, keys(s), P)]

    def segments(s):
        n = keys(s)
        ends = list(range(BANK, n, BANK)) + [n]
        if len(ends) > 1 and n - ends[-2] < WIDE:
            ends[-2] = n - WIDE
        return list(zip([0] + ends[:-1], [b - a for a, b in zip([0] + ends[:-1], ends)]))

    def groups(s):
        return [blocks(s)[g:g + 4] for g in range(0, len(blocks(s)), 4)]

    def key_base(s):
        return seq if s % NC == NC - 1 else 0

    PP = 4 * P
    pieces = []
    for r in range(0, seq, PP):
        pieces += [("q", "new", r, PP, r // CHUNK), ("k", "new", r, PP, r), ("v", "new", r, PP, r // P)]
    pieces += [("q", "sample", 0, dec, NC - 1), ("k", "sample", 0, dec, seq + past),
               ("v", "sample", 0, dec, (seq + past) // P)]
    for r in range(0, past, PP):
        pieces += [("k", "cache", r, PP, seq + r), ("v", "cache", r, PP, (seq + r) // P)]
    NP = len(pieces)
    turn_order, value_order = {}, {}
    for n in range(NU * NP):
        order = value_order if pieces[n % NP][0] == "v" else turn_order
        order[n] = len(order)
    pieces_in = {}
    PROMPT = 3 * seq // PP
    for n in range(NU * NP):
        u, j = divmod(n, NP)
        if u == 0:
            s = -3 + (j - PROMPT) // 2 if j >= PROMPT else j - PROMPT - 3
        else:
            first = 3 if u == 1 else 1
            s = NC * (u - 1) + first + j * (NC - 4 - first) // NP
        pieces_in.setdefault(s, []).append(n)

    KD = t["w_out"].shape[0] // P
    w_out = t["w_out"].rearrange("(k p) (j n) -> p k j n", p=P, n=BANK)
    WO0 = NU * NP
    for i in range(2 * KD):
        pieces_in.setdefault(NC * (NU - 1) + 1 + i, []).append(WO0 + i)

    seg0, grp0 = [0], [0]
    for s in range(NTASK):
        seg0.append(seg0[-1] + len(segments(s)))
        grp0.append(grp0[-1] + len(groups(s)))

    z_slots = [0, seq, LIVE, LIVE + seq - 2 * CHUNK, LIVE + 2 * seq - 3 * CHUNK]
    Z_WIDTH, W_WIDTH = z_slots[4] + seq, LIVE + seq

    def z_place(c):
        return {0: z_slots[3] - CHUNK, 1: z_slots[3] - 3 * CHUNK, 2: z_slots[4] - 3 * CHUNK,
                NC - 1: 0}.get(c, z_slots[(c - 1) % 5])

    def w_place(c):
        return {0: LIVE, 1: LIVE + CHUNK, NC - 1: 0}.get(c, c % 2 * LIVE)

    def overwritten(places, s):
        return max([r for r in range(max(0, s - NC), s)
                    if places[r] < places[s] + keys(s) and places[s] < places[r] + keys(r)], default=-1)

    z_at = [z_place(s % NC) for s in range(NTASK)]
    w_at = [w_place(s % NC) for s in range(NTASK)]
    z_over = [overwritten(z_at, s) for s in range(NTASK)]
    w_over = [overwritten(w_at, s) for s in range(NTASK)]
    for s in range(NTASK):
        assert z_over[s] <= max(s - 4, -1) or (z_over[s] == s - 3 and len(groups(s - 3)) <= 2)
        assert w_over[s] <= max(s - 2, -1)

    def source(u, kind, where):
        side = "d" if u < ND else "s"
        return t[f"{where}_{side}{kind}"][:, (u % ND) * P:(u % ND + 1) * P]

    with ExitStack() as ctx:
        def sbuf(name, shape, dtype=F32):
            return ctx.enter_context(nc.sbuf_tensor(name, shape, dtype))

        def psum(name, shape):
            return ctx.enter_context(nc.psum_tensor(name, shape, F32))

        def sem(name):
            return ctx.enter_context(nc.semaphore(name))

        KW, VW, QW = seq + LIVE, VT * 2 * P, NC * P
        assert 2 * KW + VW + QW <= t["shared"].shape[1]

        def share(a, n):
            return t["shared"][:, a:a + n]

        kT_hi = [share(0, KW), sbuf("kT_hi", [P, KW], F32R)[:]]
        kT_lo = [share(KW, KW), sbuf("kT_lo", [P, KW], F32R)[:]]
        v = [share(2 * KW, VW).rearrange("p (b a n) -> p b a n", a=2, n=P), sbuf("v", [P, VT, 2, P], F32R)[:]]
        qT_hi = [share(2 * KW + VW, QW).rearrange("p (c n) -> p c n", n=P), sbuf("qT_hi", [P, NC, P], F32R)[:]]
        qT_lo = [sbuf(f"qT_lo{b}", [P, NC, P], F32R)[:] for b in range(2)]
        raw = t["staging"][:].rearrange("p (s i n) -> p s i n", s=RAW, n=P)
        lam = t["lam"]
        z_arena = sbuf("z", [P, Z_WIDTH])
        w_arena = sbuf("w", [P, W_WIDTH])
        aT_hi = sbuf("aT_hi", [P, TURNED, 4, P], F32R)
        aT_lo = sbuf("aT_lo", [P, TURNED, 4, P], F32R)
        bias = w_arena[:, 0:LIVE]
        early = w_arena[:, LIVE:LIVE + 7 * 64].rearrange("p (j n) -> p j n", n=64)
        lambdas, lam_prod, mask = early[:, 0:4], early[:, 4:6], early[:, 6]
        mask_r = sbuf("mask_r", [P, 2 * WIDE - CHUNK], F32R)
        ident_r = sbuf("ident_r", [P, P], F32R)
        seg_max = sbuf("seg_max", [P, STATS, 8])
        neg_max = sbuf("neg_max", [P, STATS])
        row_sum = sbuf("row_sum", [P, STATS])
        inv_sum = sbuf("inv_sum", [P, STATS])
        o_sb = sbuf("o_sb", [P, 4, P])
        ps_prep = psum("ps_prep", [P, 2, 4, P])
        ps_z = psum("ps_z", [P, 2, BANK])
        ps_aT = psum("ps_aT", [P, 2, 4, P])
        ps_o = psum("ps_o", [P, 2, BANK])
        raw_loaded = [sem(f"raw_loaded{i}") for i in range(RAW)]
        wo_hi_done = sem("wo_hi_done")
        wo_lo_done = sem("wo_lo_done")
        small_loaded = sem("small_loaded")
        lam_dve = sem("lam_dve")
        lam_act = sem("lam_act")
        zeroed = sem("zeroed")
        tables = sem("tables")
        mask_ready = sem("mask_ready")
        bias_done = sem("bias_done")
        prep_turned = sem("prep_turned")
        prep_hi = sem("prep_hi")
        prep_lo = sem("prep_lo")
        v_hi = sem("v_hi")
        v_lo = sem("v_lo")
        scored = sem("scored")
        biased = sem("biased")
        copied = sem("copied")
        max_step = sem("max_step")
        max_ready = sem("max_ready")
        clamped = sem("clamped")
        exp_done = sem("exp_done")
        kept = sem("kept")
        summed = sem("summed")
        exponents = sem("exponents")
        low_exponents = sem("low_exponents")
        weights = sem("weights")
        inv_done = sem("inv_done")
        a_turned = sem("a_turned")
        a_hi = sem("a_hi")
        a_lo = sem("a_lo")
        a_used = sem("a_used")
        o_half = sem("o_half")
        o_done = sem("o_done")
        o_stored = [sem(f"o_stored{i}") for i in range(4)]
        block = ctx.enter_context(nc.Block())

        def summed_before(s):
            return 2 * (s - SB0) + 2 * (s // NC - ND)

        def cut(s):
            return keys(s) // 2 if s % NC == NC - 1 else 0

        def is_diff(s):
            return s < SB0

        def is_sb(s):
            return SB0 <= s < NTASK

        def z(s, a=0, n=None):
            n = keys(s) - a if n is None else n
            return z_arena[:, z_at[s] + a:z_at[s] + a + n]

        def w(s, a=0, n=None):
            n = keys(s) - a if n is None else n
            return w_arena[:, w_at[s] + a:w_at[s] + a + n]

        def stat(tile, s):
            return tile[:, s % STATS:s % STATS + 1]

        steps = range(min(pieces_in), NTASK + 2)

        @block.sync
        def _(sp):
            def load(n):
                m = n - RAW
                if m in turn_order:
                    sp.wait_ge(prep_turned, turn_order[m] + 1)
                elif m in value_order:
                    sp.wait_ge(v_lo, value_order[m] + 1)
                elif m >= WO0:
                    sp.wait_ge(wo_lo_done, m - WO0 + 1)
                if n >= WO0:
                    k, j = divmod(n - WO0, 2)
                    sp.dma_start(raw[:, n % RAW].rearrange("p a b -> p (a b)"), w_out[:, k, j]) \
                        .then_inc(raw_loaded[n % RAW], 16)
                    return
                u, j = divmod(n, NP)
                kind, where, r, rows, _ = pieces[j]
                src = source(u, kind, where)[r:r + rows, :]
                if rows >= P:
                    src = src.rearrange("(i p) n -> p i n", p=P)
                    sp.dma_start(raw[:, n % RAW, 0:rows // P], src).then_inc(raw_loaded[n % RAW], 16)
                else:
                    sp.dma_start(raw[0:rows, n % RAW, 0], src).then_inc(raw_loaded[n % RAW], 16)

            def store(s):
                u, c = divmod(s, NC)
                tok, col = c * CHUNK, u * P
                sp.wait_ge(o_done, s + 1)
                o = o_sb[:, s % 4]
                if u < ND:
                    sp.dma_start(t["mixed"][tok:tok + CHUNK, col:col + P], o[0:CHUNK]) \
                        .then_inc(o_stored[s % 4], 16)
                    sp.dma_start(t["mixed1"][tok:tok + CHUNK, col:col + P], o[CHUNK:P]) \
                        .then_inc(o_stored[s % 4], 16)
                else:
                    for a in (0, CHUNK):
                        sp.dma_start(t["mixed"][tok:tok + CHUNK, col + a:col + a + CHUNK],
                                     o[a:a + CHUNK, a:a + CHUNK]).then_inc(o_stored[s % 4], 16)

            for n in range(RAW - 1):
                load(n)
            for j, name in enumerate(("lambda_q1", "lambda_k1", "lambda_q2", "lambda_k2")):
                sp.dma_start(lambdas[:, j], t[name].partition_broadcast(P)).then_inc(small_loaded, 16)
            ahead = RAW - 1
            for s in steps:
                for n in pieces_in.get(s, ()):
                    if n + ahead < WO0 + 2 * KD:
                        load(n + ahead)
                if 0 <= s - 3:
                    store(s - 3)
            sp.wait_ge(wo_lo_done, 2 * KD)
            for i in range(4):
                sp.wait_ge(o_stored[i], 32 * len(range(i, NC * (NU - 1) + 4, 4)))
            for i in range(2):
                load_mixed(t, sp, i)
            store(NTASK - 1)
            for i in range(4):
                sp.wait_ge(o_stored[i], 32 * len(range(i, NTASK, 4)))

        @block.gpsimd
        def _(pool):
            for a in (0, CHUNK):
                if a:
                    pool.wait_ge(tables, 1)
                nc.gpsimd.iota(w_arena[a:a + CHUNK, 0:LIVE], [[-1, LIVE]], base=past, channel_multiplier=1,
                               allow_small_or_imprecise_dtypes=True).then_inc(tables, 1)

            def make_tables():
                made = DISTANCES
                for q in (qT_hi[1], qT_lo[1]):
                    for a in (0, CHUNK):
                        off = q[a:a + CHUNK, :, CHUNK - a:P - a].bitcast(mybir.dt.uint32)
                        pool.wait_ge(tables, made)
                        nc.gpsimd.memset(off, 0).then_inc(tables, 1)
                        made += 1
                pool.wait_ge(tables, made)
                nc.gpsimd.memset(mask, 0.0).then_inc(tables, 1)
                made += 1
                pool.wait_ge(tables, made)
                nc.gpsimd.memset(mask_r[:].bitcast(mybir.dt.uint32), 0).then_inc(tables, 1)
                made += 1
                for a in (0, CHUNK):
                    pool.wait_ge(tables, made)
                    nc.gpsimd.affine_select(out=mask[a:a + CHUNK], in_=mask[a:a + CHUNK], compare_op=ALU.is_gt,
                                            fill=NEG_INF, base=0, pattern=[[-1, CHUNK]],
                                            channel_multiplier=1).then_inc(tables, 1)
                    made += 1
                pool.wait_ge(tables, made)
                nc.gpsimd.tensor_copy(ident_r[:], t["ident"][:]).then_inc(tables, 1)
                made += 1
                assert made == TABLES
                pool.wait_ge(tables, made)
                nc.gpsimd.tensor_copy(mask_r[:, MASK0:MASK0 + CHUNK], mask).then_inc(mask_ready, 1)

            def split_values(n):
                u, j = divmod(n, NP)
                _, _, _, rows, place = pieces[j]
                k, m = max(1, rows // P), min(P, rows)
                pool.wait_ge(v_hi, value_order[n] + 1)
                nc.gpsimd.tensor_tensor(v[u % 2][0:m, place:place + k, 1, :], raw[0:m, n % RAW, 0:k],
                                        v[u % 2][0:m, place:place + k, 0, :].bitcast(F32),
                                        ALU.subtract).then_inc(v_lo, 1)

            def split_w_out(i):
                k, j = divmod(i, 2)
                part = (slice(None), k, slice(j * BANK, (j + 1) * BANK))
                pool.wait_ge(wo_hi_done, i + 1)
                nc.gpsimd.tensor_tensor(t["wo_lo"][part], raw[:, (WO0 + i) % RAW].rearrange("p a b -> p (a b)"),
                                        t["wo_hi"][part].bitcast(F32), ALU.subtract).then_inc(wo_lo_done, 1)

            def exponent(s):
                pool.wait_ge(summed, summed_before(s) + 2)
                nc.gpsimd.tensor_tensor(z(s, cut(s)), z(s, cut(s)), w(s, cut(s)), ALU.subtract) \
                    .then_inc(exponents, 1)

            def maximum(s):
                nb = len(segments(s))
                pool.wait_ge(biased, seg0[s + 1])
                if s >= STATS:
                    pool.wait_ge(weights, s - STATS + 1)
                sm = seg_max[:, s % STATS]
                for b in range(1, nb - 1):
                    nc.gpsimd.tensor_scalar(sm[:, b:b + 1], sm[:, b:b + 1], sm[:, b - 1:b], None,
                                            ALU.max).then_inc(max_step, 1)
                    pool.wait_ge(max_step, (nb - 2) * (s // NC) + b)
                last = sm[:, nb - 1:nb]
                if nb > 1:
                    nc.gpsimd.tensor_scalar(stat(neg_max, s), last, sm[:, nb - 2:nb - 1], -1.0, ALU.max,
                                            ALU.mult).then_inc(max_ready, 1)
                else:
                    nc.gpsimd.tensor_scalar(stat(neg_max, s), last, -1.0, None, ALU.mult).then_inc(max_ready, 1)

            pool.wait_ge(tables, DISTANCES)
            for s in steps:
                if s == 0:
                    pool.wait_ge(max_ready, 3)
                    make_tables()
                    pool.wait_ge(mask_ready, 1)
                for n in pieces_in.get(s, ()):
                    if n in value_order:
                        split_values(n)
                    elif n >= WO0:
                        split_w_out(n - WO0)
                if is_sb(s + 2):
                    exponent(s + 2)
                if 0 <= s + 3 and is_diff(s + 3):
                    maximum(s + 3)

        @block.scalar
        def _(act):
            nc.scalar.preload_act_table_set("natural_log_exp_and_others")

            def prepare(n):
                u, j = divmod(n, NP)
                kind, _, _, rows, place = pieces[j]
                k, m = max(1, rows // P), min(P, rows)
                if u == 1:
                    act.wait_ge(tables, TABLES)
                if u >= 2:
                    act.wait_ge(a_used, grp0[NC * (u - 1)])
                if kind == "v":
                    act.wait_ge(raw_loaded[n % RAW], 16 * (n // RAW + 1))
                    nc.scalar.copy(v[u % 2][0:m, place:place + k, 0, :], raw[0:m, n % RAW, 0:k]).then_inc(v_hi, 1)
                    return
                e = turn_order[n]
                act.wait_ge(prep_turned, e + 1)
                src = ps_prep[:, e % 2].rearrange("p a b -> p (a b)")
                if kind == "k":
                    nc.scalar.copy(kT_hi[u % 2][:, place:place + rows], src[:, 0:rows]).then_inc(prep_hi, 1)
                else:
                    ch = rows // CHUNK
                    srcq = src[:, 0:rows].rearrange("p (c q) -> p c q", q=CHUNK)
                    for a in (0, CHUNK):
                        last = nc.scalar.activation(qT_hi[u % 2][a:a + CHUNK, place:place + ch, a:a + CHUNK],
                                                    srcq[a:a + CHUNK], ACT.Copy, scale=QSCALE)
                    last.then_inc(prep_hi, 1)

            def copy_scores(s):
                if z_over[s] >= 0:
                    act.wait_ge(a_turned, grp0[z_over[s] + 1])
                for b, (a, n) in enumerate(segments(s)):
                    e = seg0[s] + b
                    act.wait_ge(scored, e + 1)
                    nc.scalar.copy(z(s, a, n), ps_z[:, e % 2, 0:n]).then_inc(copied, 1)

            def begin(s):
                if is_diff(s):
                    act.wait_ge(max_ready, s + 1)
                    if s >= STATS:
                        act.wait_ge(inv_done, s - STATS + 1)
                    nc.scalar.activation(z(s), z(s), ACT.Exp, bias=stat(neg_max, s),
                                         accum_out=stat(row_sum, s)).then_inc(weights, 1)
                else:
                    act.wait_ge(clamped, s - SB0 + 1)
                    nc.scalar.activation(w(s), w(s), ACT.Exp).then_inc(exp_done, 1)
                    act.wait_ge(exp_done, s - SB0 + 1)
                    nc.scalar.activation(w(s), w(s), ACT.Ln, bias=1.0).then_inc(kept, 1)

            def finish(s):
                act.wait_ge(exponents, s - SB0 + 1)
                if cut(s):
                    nc.scalar.activation(z(s, cut(s)), z(s, cut(s)), ACT.Exp)
                    act.wait_ge(low_exponents, s // NC - ND + 1)
                    nc.scalar.activation(z(s, 0, cut(s)), z(s, 0, cut(s)), ACT.Exp).then_inc(weights, 1)
                else:
                    nc.scalar.activation(z(s), z(s), ACT.Exp).then_inc(weights, 1)

            def split(s):
                for g, bl in enumerate(groups(s)):
                    e = grp0[s] + g
                    act.wait_ge(a_turned, e + 1)
                    if e >= TURNED:
                        act.wait_ge(a_used, e - TURNED + 1)
                    f = sum(m == P for _, m in bl)
                    if f:
                        last = nc.scalar.copy(aT_hi[:, e % TURNED, 0:f], ps_aT[:, e % 2, 0:f])
                    if f < len(bl):
                        m = bl[f][1]
                        last = nc.scalar.copy(aT_hi[0:m, e % TURNED, f], ps_aT[0:m, e % 2, f])
                    last.then_inc(a_hi, 1)

            def left(s):
                act.wait_ge(a_used, grp0[s + 1])
                if s >= 4:
                    act.wait_ge(o_stored[s % 4], 32 * (s // 4))
                act.wait_ge(inv_done, s + 1)
                nc.scalar.activation(o_sb[:, s % 4], ps_o[:, s % 2, 0:P], ACT.Copy,
                                     scale=stat(inv_sum, s)).then_inc(o_half, 1)

            act.wait_ge(zeroed, 4)
            for s in steps:
                for n in pieces_in.get(s, ()):
                    if n < WO0:
                        prepare(n)
                if s == 2:
                    act.wait_ge(lam_dve, 2)
                    nc.scalar.activation(lam[:, 2:4], lam[:, 0:2], ACT.Exp).then_inc(lam_act, 1)
                if 0 <= s + 2 < NTASK:
                    begin(s + 2)
                if 0 <= s < NTASK:
                    split(s)
                if is_sb(s + 3):
                    copy_scores(s + 3)
                if is_sb(s + 1):
                    finish(s + 1)
                if 0 <= s - 2 and is_diff(s - 2):
                    left(s - 2)

        @block.vector
        def _(dve):
            def prepare(n):
                u, j = divmod(n, NP)
                kind, _, _, rows, place = pieces[j]
                e = turn_order[n]
                dve.wait_ge(prep_hi, e + 1)
                src = ps_prep[:, e % 2].rearrange("p a b -> p (a b)")
                if kind == "k":
                    nc.vector.tensor_tensor(kT_lo[u % 2][:, place:place + rows], src[:, 0:rows],
                                            kT_hi[u % 2][:, place:place + rows].bitcast(F32),
                                            ALU.subtract).then_inc(prep_lo, 1)
                else:
                    ch = rows // CHUNK
                    srcq = src[:, 0:rows].rearrange("p (c q) -> p c q", q=CHUNK)
                    for a in (0, CHUNK):
                        part = (slice(a, a + CHUNK), slice(place, place + ch), slice(a, a + CHUNK))
                        last = nc.vector.scalar_tensor_tensor(qT_lo[u % 2][part], srcq[a:a + CHUNK], QSCALE,
                                                              qT_hi[u % 2][part].bitcast(F32), ALU.mult,
                                                              ALU.subtract)
                    last.then_inc(prep_lo, 1)

            def sum_softplus(s):
                q = summed_before(s)
                dve.wait_ge(kept, s - SB0 + 1)
                later = 0.0
                for a, n in ((cut(s), None), (0, cut(s)))[:2 if cut(s) else 1]:
                    nc.vector.tensor_tensor(w(s, a, n), z(s, a, n), w(s, a, n), ALU.max).then_inc(summed, 1)
                    q += 1
                    dve.wait_ge(summed, q)
                    back = w(s, a, n)[:, ::-1]
                    nc.vector.tensor_tensor_scan(back, back, back, later, ALU.add, ALU.bypass).then_inc(summed, 1)
                    q += 1
                    later = w(s, a, 1)
                if cut(s):
                    dve.wait_ge(summed, q)
                    nc.vector.tensor_tensor(z(s, 0, cut(s)), z(s, 0, cut(s)), w(s, 0, cut(s)),
                                            ALU.subtract).then_inc(low_exponents, 1)

            def read_scores(s):
                n = keys(s)
                if is_diff(s):
                    if s % NC == 0:
                        u = s // NC
                        if u == 0:
                            dve.wait_ge(tables, DISTANCES)
                            nc.vector.scalar_tensor_tensor(bias, bias, -1.0, bias,
                                                           ALU.mult, ALU.min).then_inc(bias_done, 1)
                            dve.wait_ge(bias_done, 1)
                        else:
                            dve.wait_ge(biased, seg0[s])
                        nc.vector.tensor_scalar(bias, bias, 0.25, None, ALU.mult).then_inc(bias_done, 1)
                        dve.wait_ge(bias_done, u + 2)
                    if z_over[s] >= 0:
                        dve.wait_ge(a_turned, grp0[z_over[s] + 1])
                    if s >= STATS:
                        dve.wait_ge(max_ready, s - STATS + 1)
                    for b, (a, m) in enumerate(segments(s)):
                        e = seg0[s] + b
                        dve.wait_ge(scored, e + 1)
                        off = LIVE - n + a
                        nc.vector.tensor_tensor_reduce(z(s, a, m), ps_z[:, e % 2, 0:m], bias[:, off:off + m],
                                                       1.0, -3e38, ALU.add, ALU.max,
                                                       seg_max[:, s % STATS, b:b + 1]).then_inc(biased, 1)
                else:
                    dve.wait_ge(copied, seg0[s + 1] - seg0[SB0])
                    if w_over[s] >= SB0:
                        dve.wait_ge(exponents, w_over[s] - SB0 + 1)
                        if w_over[s] // NC > ND:
                            dve.wait_ge(low_exponents, w_over[s] // NC - ND)
                    else:
                        dve.wait_ge(biased, seg0[SB0])
                    nc.vector.tensor_scalar(w(s), z(s), SOFTPLUS_LINEAR, None, ALU.min).then_inc(clamped, 1)

            def split(s):
                for g, bl in enumerate(groups(s)):
                    e = grp0[s] + g
                    dve.wait_ge(a_hi, e + 1)
                    f = sum(m == P for _, m in bl)
                    if f:
                        last = nc.vector.tensor_tensor(aT_lo[:, e % TURNED, 0:f], ps_aT[:, e % 2, 0:f],
                                                       aT_hi[:, e % TURNED, 0:f].bitcast(F32), ALU.subtract)
                    if f < len(bl):
                        m = bl[f][1]
                        last = nc.vector.tensor_tensor(aT_lo[0:m, e % TURNED, f], ps_aT[0:m, e % 2, f],
                                                       aT_hi[0:m, e % TURNED, f].bitcast(F32), ALU.subtract)
                    last.then_inc(a_lo, 1)
                if is_diff(s):
                    dve.wait_ge(weights, s + 1)
                    nc.vector.reciprocal(stat(inv_sum, s), stat(row_sum, s)).then_inc(inv_done, 1)

            def output(s):
                o, half = o_sb[:, s % 4], ps_o[:, s % 2, P:2 * P]
                if is_diff(s):
                    dve.wait_ge(o_half, s + 1)
                    nc.vector.scalar_tensor_tensor(o, half, stat(inv_sum, s), o, ALU.mult,
                                                   ALU.add).then_inc(o_done, 1)
                else:
                    dve.wait_ge(a_used, grp0[s + 1])
                    dve.wait_ge(o_stored[s % 4], 32 * (s // 4))
                    halves = ps_o[:, s % 2, 0:2 * P].rearrange("p (a n) -> p n a", a=2)
                    nc.vector.tensor_reduce(o, halves, AX.X, ALU.add).then_inc(o_done, 1)

            def split_w_out(i):
                k, j = divmod(i, 2)
                n = WO0 + i
                dve.wait_ge(raw_loaded[n % RAW], 16 * (n // RAW + 1))
                if i == 0:
                    dve.wait_ge(a_used, grp0[NC * (NU - 1)])
                nc.vector.tensor_copy(t["wo_hi"][:, k, j * BANK:(j + 1) * BANK],
                                      raw[:, n % RAW].rearrange("p a b -> p (a b)")).then_inc(wo_hi_done, 1)

            def lambda_products():
                dve.wait_ge(small_loaded, 64)
                for j in range(2):
                    nc.vector.tensor_tensor_reduce(lam_prod[:, j], lambdas[:, 2 * j], lambdas[:, 2 * j + 1], 1.0,
                                                   0.0, ALU.mult, ALU.add, lam[:, j:j + 1]).then_inc(lam_dve, 1)

            def negative_lambda():
                dve.wait_ge(lam_act, 1)
                nc.vector.tensor_tensor(lam[:, 4:5], lam[:, 3:4], lam[:, 2:3], ALU.subtract).then_inc(lam_dve, 1)
                dve.wait_ge(lam_dve, 3)
                nc.vector.tensor_scalar(lam[:, 5:6], lam[:, 4:5], -LAM_INIT, None, ALU.add).then_inc(lam_dve, 1)

            for q in (qT_hi[0], qT_lo[0]):
                for a in (0, CHUNK):
                    off = q[a:a + CHUNK, :, CHUNK - a:P - a].bitcast(mybir.dt.uint32)
                    nc.vector.memset(off, 0).then_inc(zeroed, 1)
            for s in steps:
                for n in pieces_in.get(s, ()):
                    if n in turn_order:
                        prepare(n)
                    elif n >= WO0:
                        split_w_out(n - WO0)
                if s == 1:
                    lambda_products()
                if s == 3:
                    negative_lambda()
                if 0 <= s + 3 and is_diff(s + 3):
                    read_scores(s + 3)
                if 0 <= s < NTASK:
                    split(s)
                if 0 <= s - 2:
                    output(s - 2)
                if is_sb(s + 3):
                    read_scores(s + 3)
                if is_sb(s + 2):
                    sum_softplus(s + 2)

        @block.tensor
        def _(pe):
            def prepare(n):
                rows = pieces[n % NP][3]
                e = turn_order[n]
                pe.wait_ge(raw_loaded[n % RAW], 16 * (n // RAW + 1))
                if e >= 2:
                    pe.wait_ge(prep_lo, e - 1)
                for i in range(max(1, rows // P)):
                    m = min(P, rows)
                    last = nc.tensor.transpose(ps_prep[:, e % 2, i, 0:m], raw[0:m, n % RAW, i], t["ident"][0:m, 0:m])
                last.then_inc(prep_turned, 1)

            def pieces_end(s):
                u, c = divmod(s, NC)
                if c == NC - 1:
                    return NP * (u + 1)
                return 0 if c * CHUNK % PP else NP * u + 3 * (c * CHUNK // PP + 1)

            def score(s, first, last):
                u, c = divmod(s, NC)
                if first == 0 and pieces_end(s):
                    pe.wait_ge(prep_lo, sum(n < pieces_end(s) for n in turn_order))
                if s == SB0 and first == 0:
                    pe.wait_ge(mask_ready, 1)
                q_hi, q_lo = qT_hi[u % 2][:, c], qT_lo[u % 2][:, c]
                for b, (a, n) in list(enumerate(segments(s)))[first:last]:
                    e = seg0[s] + b
                    if e >= 2:
                        if e - 2 < seg0[SB0]:
                            pe.wait_ge(biased, e - 1)
                        else:
                            pe.wait_ge(copied, e - 1 - seg0[SB0])
                    m = max(n, WIDE)
                    out = ps_z[:, e % 2, 0:m]
                    k0 = key_base(s) + a
                    k_hi, k_lo = kT_hi[u % 2][:, k0:k0 + m], kT_lo[u % 2][:, k0:k0 + m]
                    nc.tensor.matmul(out, q_hi, k_hi, start=True, stop=False)
                    nc.tensor.matmul(out, q_hi, k_lo, start=False, stop=False)
                    if is_sb(s) and a + n == keys(s):
                        at = m - n
                        nc.tensor.matmul(out[:, m - WIDE:m], ident_r[:], mask_r[:, at:at + WIDE], start=False,
                                         stop=False)
                    nc.tensor.matmul(out, q_lo, k_hi, start=False, stop=True).then_inc(scored, 1)

            def turn(s, g):
                e = grp0[s] + g
                if g == 0:
                    pe.wait_ge(weights, s + 1)
                if e >= 2:
                    pe.wait_ge(a_lo, e - 1)
                for i, (b, m) in enumerate(groups(s)[g]):
                    last = nc.tensor.transpose(ps_aT[0:m, e % 2, i], z(s, b, m), t["ident"][:, :])
                last.then_inc(a_turned, 1)

            def values(s, g):
                u = s // NC
                e = grp0[s] + g
                pe.wait_ge(a_lo, e + 1)
                if g == 0 and pieces_end(s):
                    pe.wait_ge(v_lo, sum(n < pieces_end(s) for n in value_order))
                if g == 0 and s >= 2:
                    pe.wait_ge(o_done, s - 1)
                out = ps_o[:, s % 2, 0:2 * P]
                for i, (b, m) in enumerate(groups(s)[g]):
                    rhs = v[u % 2][0:m, (key_base(s) + b) // P].rearrange("p a n -> p (a n)")
                    nc.tensor.matmul(out, aT_hi[0:m, e % TURNED, i], rhs, start=(b == 0), stop=False)
                    last = nc.tensor.matmul(out, aT_lo[0:m, e % TURNED, i], rhs,
                                            start=False, stop=(b + m == keys(s)))
                last.then_inc(a_used, 1)

            for s in steps:
                for n in pieces_in.get(s, ()):
                    if n in turn_order:
                        prepare(n)
                turns = [(turn, s, g) for g in range(len(groups(s)))] if 0 <= s < NTASK else []
                uses = [(values, s - 1, g) for g in range(len(groups(s - 1)))] if 1 <= s <= NTASK else []
                for i in range(max(len(turns), len(uses))):
                    for f, x, g in turns[i:i + 1] + uses[i:i + 1]:
                        f(x, g)
                if 0 <= s + 3 < NTASK:
                    score(s + 3, 2, None)
                if 0 <= s + 4 < NTASK:
                    score(s + 4, 0, 2)


def mix(nc, t, h_all, nT_hi, nT_lo):
    tiles = token_tiles(t["seq"], t["dec"])
    NT = len(tiles)
    D = t["x_prompt"].shape[1]
    KD = D // P
    DW = t["mixed1"].shape[1]
    NH = DW // P
    wo_hi, wo_lo = t["wo_hi"], t["wo_lo"]
    lam = t["lam"]
    with ExitStack() as ctx:
        def sbuf(name, shape, dtype=F32):
            return ctx.enter_context(nc.sbuf_tensor(name, shape, dtype))

        def psum(name, shape):
            return ctx.enter_context(nc.psum_tensor(name, shape, F32))

        def sem(name):
            return ctx.enter_context(nc.semaphore(name))

        m0, m1 = t["m0"], t["m1"]
        subln = sbuf("subln", [P, P])
        head_sq = sbuf("head_sq", [P, NT, NH])
        head_ms = sbuf("head_ms", [P, NT, NH])
        head_rstd = sbuf("head_rstd", [P, NT, NH])
        mT_hi = sbuf("mT_hi", [P, 2, KD, P], F32R)
        mT_lo = sbuf("mT_lo", [P, 2, KD, P], F32R)
        xn = sbuf("xn3", [P, D])
        g_sb = sbuf("g3", [P, D])
        sumsq = sbuf("sumsq3", [P, NT])
        ms = sbuf("ms3", [P, NT])
        rstd = sbuf("rstd3", [P, NT])
        ps_m = psum("ps_m", [P, 2, 4, P])
        ps_n = psum("ps_n", [P, 2, 4, P])
        ps_h = psum("ps_h", [P, 4, BANK])
        m_loaded = t["m_loaded"]
        h_loaded = sem("h_loaded")
        g_loaded = sem("g_loaded3")
        subln_loaded = sem("subln_loaded")
        subln_scaled = sem("subln_scaled")
        combined = sem("combined")
        head_rstd_done = sem("head_rstd_done")
        turned = sem("turned3")
        m_hi = sem("m_hi")
        m_lo = sem("m_lo")
        multiplied = sem("multiplied")
        h_added = sem("h_added")
        squared = sem("squared3")
        rstd_done = sem("rstd_done3")
        normed = sem("normed3")
        n_turned = sem("n_turned3")
        n_hi = sem("n_hi3")
        n_lo = sem("n_lo3")
        block = ctx.enter_context(nc.Block())

        @block.sync
        def _(sp):
            sp.dma_start(subln[:], t["diff_subln_g"].partition_broadcast(P)).then_inc(subln_loaded, 16)
            for j in range(NT):
                m = tiles[j][1]
                sp.dma_start(h_all[0:m, j], split_rows(tiles, t["x_prompt"], t["x_sample"], j)) \
                    .then_inc(h_loaded, 16)
            sp.dma_start(g_sb[:], t["norm_ffn_g"].partition_broadcast(P)).then_inc(g_loaded, 16)
            for i in range(2, NT):
                sp.wait_ge(turned, 2 * (i - 1))
                load_mixed(t, sp, i)
            sp.wait_ge(turned, 2 * NT)
            load_gate_up(t, sp, 0)
            load_down(t, sp, 0)

        @block.gpsimd
        def _(pool):
            def head_norm(i):
                n = tiles[i][1]
                pool.wait_ge(combined, 6 * i + 3)
                rstd_pool(nc, pool, head_ms[0:n, i], head_sq[0:n, i], head_rstd[0:n, i],
                          t["neg_half"][0:n, 0:NH], P, head_rstd_done, i)

            def row_norm(i):
                n = tiles[i][1]
                pool.wait_ge(squared, i + 1)
                rstd_pool(nc, pool, ms[0:n, i:i + 1], sumsq[0:n, i:i + 1], rstd[0:n, i:i + 1],
                          t["neg_half"][0:n, 0:1], D, rstd_done, i)

            head_norm(0)
            head_norm(1)
            for i in range(NT + 1):
                if i >= 1:
                    row_norm(i - 1)
                if i + 2 < NT:
                    head_norm(i + 2)

        @block.scalar
        def _(act):
            def split_m(i):
                n = tiles[i][1]
                for j in range(2):
                    act.wait_ge(turned, 2 * i + j + 1)
                    if i >= 2:
                        act.wait_ge(multiplied, 2 * (i - 1))
                    nc.scalar.copy(mT_hi[:, i % 2, 4 * j:4 * j + 4, 0:n], ps_m[:, j, :, 0:n]).then_inc(m_hi, 1)

            split_m(0)
            for i in range(NT + 1):
                if i + 1 < NT:
                    split_m(i + 1)
                if i >= 1:
                    t0, n = tiles[i - 1]
                    act.wait_ge(h_added, 2 * i)
                    if i >= 2:
                        act.wait_ge(n_turned, 2 * (i - 1))
                    nc.scalar.activation(xn[0:n], h_all[0:n, i - 1], ACT.Square,
                                         accum_out=sumsq[0:n, i - 1:i]).then_inc(squared, 1)
                    for j in range(2):
                        act.wait_ge(n_turned, 2 * (i - 1) + j + 1)
                        nc.scalar.copy(nT_hi[:, 4 * j:4 * j + 4, t0:t0 + n], ps_n[:, j, :, 0:n]).then_inc(n_hi, 1)

        @block.vector
        def _(dve):
            def combine(i):
                n = tiles[i][1]
                d = m0[0:n, i % 2, 0:DW]
                dh = d.rearrange("p (h v) -> p h v", h=NH)
                squares = m1[0:n, i % 2]
                dve.wait_ge(m_loaded[i % 2], 32 * (i // 2 + 1))
                nc.vector.scalar_tensor_tensor(d, m1[0:n, i % 2], lam[0:n, 5:6], d, ALU.mult,
                                               ALU.add).then_inc(combined, 1)
                dve.wait_ge(combined, 6 * i + 1)
                nc.vector.tensor_tensor(squares, d, d, ALU.mult).then_inc(combined, 1)
                dve.wait_ge(combined, 6 * i + 2)
                nc.vector.tensor_reduce(head_sq[0:n, i], squares.rearrange("p (h v) -> p h v", h=NH),
                                        AX.X, ALU.add).then_inc(combined, 1)
                if i == 0:
                    dve.wait_ge(subln_loaded, 16)
                    nc.vector.tensor_scalar(subln[:], subln[:], 1.0 - LAM_INIT, None,
                                            ALU.mult).then_inc(subln_scaled, 1)
                    dve.wait_ge(subln_scaled, 1)
                nc.vector.tensor_tensor(dh, dh, subln[0:n].unsqueeze(1).to_broadcast([n, NH, P]),
                                        ALU.mult).then_inc(combined, 1)
                dve.wait_ge(combined, 6 * i + 4)
                dve.wait_ge(head_rstd_done, 2 * (i + 1))
                nc.vector.tensor_tensor(dh, dh, head_rstd[0:n, i].unsqueeze(2).to_broadcast([n, NH, P]),
                                        ALU.mult).then_inc(combined, 2)

            def split_m(i):
                n = tiles[i][1]
                for j in range(2):
                    dve.wait_ge(m_hi, 2 * i + j + 1)
                    nc.vector.tensor_tensor(mT_lo[:, i % 2, 4 * j:4 * j + 4, 0:n], ps_m[:, j, :, 0:n],
                                            mT_hi[:, i % 2, 4 * j:4 * j + 4, 0:n].bitcast(F32),
                                            ALU.subtract).then_inc(m_lo, 1)

            def add(i):
                n = tiles[i][1]
                for j in range(2):
                    m = 2 * i + j
                    dve.wait_ge(multiplied, m + 1)
                    hh = h_all[0:n, i, j * BANK:(j + 1) * BANK]
                    nc.vector.tensor_tensor(hh, ps_h[0:n, m % 4], hh, ALU.add).then_inc(h_added, 1)

            def norm(i):
                n = tiles[i][1]
                dve.wait_ge(rstd_done, 2 * (i + 1))
                nc.vector.scalar_tensor_tensor(xn[0:n], h_all[0:n, i], rstd[0:n, i:i + 1], g_sb[0:n],
                                               ALU.mult, ALU.mult).then_inc(normed, 1)

            def split_n(i):
                t0, n = tiles[i]
                for j in range(2):
                    dve.wait_ge(n_hi, 2 * i + j + 1)
                    nc.vector.tensor_tensor(nT_lo[:, 4 * j:4 * j + 4, t0:t0 + n], ps_n[:, j, :, 0:n],
                                            nT_hi[:, 4 * j:4 * j + 4, t0:t0 + n].bitcast(F32),
                                            ALU.subtract).then_inc(n_lo, 1)

            combine(0)
            split_m(0)
            combine(1)
            dve.wait_ge(h_loaded, 16 * NT)
            dve.wait_ge(g_loaded, 16)
            for i in range(NT + 1):
                if i >= 1:
                    add(i - 1)
                if i + 1 < NT:
                    split_m(i + 1)
                if i >= 1:
                    norm(i - 1)
                if i + 2 < NT:
                    combine(i + 2)
                if i >= 1:
                    split_n(i - 1)

        @block.tensor
        def _(pe):
            def turn_m(i):
                n = tiles[i][1]
                pe.wait_ge(combined, 6 * i + 6)
                for j in range(2):
                    if i >= 1:
                        pe.wait_ge(m_lo, 2 * (i - 1) + j + 1)
                    for k in range(4):
                        c = (4 * j + k) * P
                        last = nc.tensor.transpose(ps_m[:, j, k, 0:n], m0[0:n, i % 2, c:c + P],
                                                   t["ident"][0:n, 0:n])
                    last.then_inc(turned, 1)

            def turn_n(i):
                n = tiles[i][1]
                pe.wait_ge(normed, i + 1)
                for j in range(2):
                    if i >= 1:
                        pe.wait_ge(n_lo, 2 * (i - 1) + j + 1)
                    for k in range(4):
                        c = (4 * j + k) * P
                        last = nc.tensor.transpose(ps_n[:, j, k, 0:n], xn[0:n, c:c + P], t["ident"][0:n, 0:n])
                    last.then_inc(n_turned, 1)

            turn_m(0)
            for i in range(NT):
                n = tiles[i][1]
                if 1 < i + 1 < NT:
                    turn_m(i + 1)
                pe.wait_ge(m_lo, 2 * (i + 1))
                for j in range(2):
                    m = 2 * i + j
                    if m >= 4:
                        pe.wait_ge(h_added, m - 3)
                    for k in range(KD):
                        out = ps_h[0:n, m % 4]
                        b_hi, b_lo = (x[:, k, j * BANK:(j + 1) * BANK] for x in (wo_hi, wo_lo))
                        nc.tensor.matmul(out, mT_hi[:, i % 2, k, 0:n], b_hi, start=(k == 0), stop=False)
                        nc.tensor.matmul(out, mT_hi[:, i % 2, k, 0:n], b_lo, start=False, stop=False)
                        last = nc.tensor.matmul(out, mT_lo[:, i % 2, k, 0:n], b_hi, start=False, stop=(k == KD - 1))
                    last.then_inc(multiplied, 1)
                    if j == 0 and i == 0:
                        turn_m(1)
                    if j == 0 and i >= 1:
                        turn_n(i - 1)
            turn_n(NT - 1)


def load_gate_up(t, sp, f):
    for i, name in enumerate(("w_gate", "w_up")):
        w = t[name].rearrange("(k p) n -> p k n", p=P)
        sp.dma_start(t["gu_raw"][:, :, i], w[:, :, f * P:(f + 1) * P]).then_inc(t["gu_loaded"], 16)


def load_down(t, sp, f):
    sp.dma_start(t["wd_raw"], t["w_down"][f * P:(f + 1) * P, :]).then_inc(t["wd_loaded"], 16)


def feed(nc, t, h_all, nT_hi, nT_lo):
    tiles = token_tiles(t["seq"], t["dec"])
    NT, T = len(tiles), t["seq"] + t["dec"]
    D = h_all.shape[2]
    KD = D // P
    NF = t["w_gate"].shape[1] // P
    parts = 3
    width = -(-T // parts // 2) * 2
    chunks = [(a, min(width, T - a)) for a in range(0, T, width)]
    G = NF // 2
    HALF = KD // 2
    NY = 2 * NT
    with ExitStack() as ctx:
        def sbuf(name, shape, dtype=F32):
            return ctx.enter_context(nc.sbuf_tensor(name, shape, dtype))

        def psum(name, shape):
            return ctx.enter_context(nc.psum_tensor(name, shape, F32))

        def sem(name):
            return ctx.enter_context(nc.semaphore(name))

        GU, WD = 2 * D, 3 * D
        assert 4 * GU + 2 * WD + T <= t["shared"].shape[1]

        def share(a, n):
            return t["shared"][:, a:a + n]

        gu_hi, gu_lo = (share(a, 2 * GU).rearrange("p (f k w n) -> p f k w n", f=2, w=2, n=P)
                        for a in (0, 2 * GU))
        wd_hi, wd_lo = (share(a, WD).rearrange("p (f n) -> p f n", n=D) for a in (4 * GU, 4 * GU + WD))
        gu_raw, wd_raw = t["gu_raw"], t["wd_raw"]
        squares, g_sb = t["staging"][:, 0:D], t["staging"][:, D:2 * D]
        sumsq = sbuf("sumsq4", [P, NT])
        ms = sbuf("ms4", [P, NT])
        rstd = sbuf("rstd4", [P, NT])
        gate = sbuf("gate", [P, 2, width])
        hidden = sbuf("hidden", [P, 2, width])
        hT_hi = sbuf("hT_hi", [P, 3, T], F32R)
        hT_lo = [share(4 * GU + 2 * WD, T)] + [sbuf(f"hT_lo{i}", [P, T], F32R)[:] for i in (1, 2)]
        ps_g = psum("ps_g", [P, 2, BANK])
        ps_u = psum("ps_u", [P, 2, BANK])
        ps_y = psum("ps_y", [P, 4, BANK])
        gu_loaded, wd_loaded = t["gu_loaded"], t["wd_loaded"]
        gu_hi_first = sem("gu_hi_first")
        gu_lo_first = sem("gu_lo_first")
        gu_hi_done = sem("gu_hi_done")
        gu_lo_done = sem("gu_lo_done")
        wd_hi_done = sem("wd_hi_done")
        wd_lo_done = sem("wd_lo_done")
        gu_done = sem("gu_done")
        silu_done = sem("silu_done")
        hidden_done = sem("hidden_done")
        hid_hi = sem("hid_hi")
        hid_lo = sem("hid_lo")
        y_done = sem("y_done")
        y_added = sem("y_added")
        g_loaded = sem("g_loaded4")
        squared = sem("squared4")
        rstd_done = sem("rstd_done4")
        y_normed = sem("y_normed")
        y_stored = sem("y_stored")
        block = ctx.enter_context(nc.Block())
        C = len(chunks)

        @block.sync
        def _(sp):
            sp.wait_ge(gu_lo_first, 1)
            for f in range(1, NF):
                sp.wait_ge(gu_lo_done, f)
                load_gate_up(t, sp, f)
                sp.wait_ge(wd_lo_done, f)
                load_down(t, sp, f)
            sp.wait_ge(gu_lo_done, NF)
            sp.dma_start(g_sb, t["norm_final_g"].partition_broadcast(P)).then_inc(g_loaded, 16)
            for i in range(NT):
                n = tiles[i][1]
                sp.wait_ge(y_normed, i + 1)
                sp.dma_start(split_rows(tiles, t["y_prompt"], t["y_sample"], i), h_all[0:n, i]) \
                    .then_inc(y_stored, 16)
            sp.wait_ge(y_stored, 16 * NT)

        @block.gpsimd
        def _(pool):
            def split_gu(f):
                pool.wait_ge(gu_hi_done, f + 1)
                nc.gpsimd.tensor_tensor(gu_lo[:, f % 2].rearrange("p k w n -> p (k w n)"),
                                        gu_raw.rearrange("p k w n -> p (k w n)"),
                                        gu_hi[:, f % 2].bitcast(F32).rearrange("p k w n -> p (k w n)"),
                                        ALU.subtract).then_inc(gu_lo_done, 1)

            def split_wd(f):
                pool.wait_ge(wd_hi_done, f + 1)
                nc.gpsimd.tensor_tensor(wd_lo[:, f % 3], wd_raw, wd_hi[:, f % 3].bitcast(F32),
                                        ALU.subtract).then_inc(wd_lo_done, 1)

            pool.wait_ge(gu_hi_done, 1)
            nc.gpsimd.tensor_tensor(gu_lo[:, 0, HALF:], gu_raw[:, HALF:], gu_hi[:, 0, HALF:].bitcast(F32),
                                    ALU.subtract).then_inc(gu_lo_done, 1)
            split_wd(0)
            split_gu(1)
            for f in range(NF):
                for c, (a, n) in enumerate(chunks):
                    q = C * f + c
                    pool.wait_ge(hid_hi, q + 1)
                    nc.gpsimd.tensor_tensor(hT_lo[f % 3][:, a:a + n], hidden[:, q % 2, 0:n],
                                            hT_hi[:, f % 3, a:a + n].bitcast(F32), ALU.subtract).then_inc(hid_lo, 1)
                if f + 2 < NF:
                    split_gu(f + 2)
                if f + 1 < NF:
                    split_wd(f + 1)
            for i in range(NT):
                n = tiles[i][1]
                pool.wait_ge(squared, i + 1)
                rstd_pool(nc, pool, ms[0:n, i:i + 1], sumsq[0:n, i:i + 1], rstd[0:n, i:i + 1],
                          t["neg_half"][0:n, 0:1], D, rstd_done, i)

        @block.scalar
        def _(act):
            for q in range(C * NF):
                f, c = divmod(q, C)
                a, n = chunks[c]
                act.wait_ge(gu_done, q + 1)
                if q >= 2:
                    act.wait_ge(hidden_done, q - 1)
                nc.scalar.activation(gate[:, q % 2, 0:n], ps_g[:, q % 2, 0:n], ACT.Silu).then_inc(silu_done, 1)
                act.wait_ge(hidden_done, q + 1)
                if f >= 3 and c == 0:
                    act.wait_ge(y_done, NY * ((f - 3) // 2 + 1))
                nc.scalar.copy(hT_hi[:, f % 3, a:a + n], hidden[:, q % 2, 0:n]).then_inc(hid_hi, 1)
            act.wait_ge(gu_lo_done, NF)
            for i in range(NT):
                n = tiles[i][1]
                act.wait_ge(y_added, NY * (G - 1) + 2 * (i + 1))
                norm_rows_act(nc, act, h_all[0:n, i], squares[0:n], sumsq[0:n, i:i + 1], squared, i)

        @block.vector
        def _(dve):
            def split_gu(f):
                dve.wait_ge(gu_loaded, 32 * (f + 1))
                if f >= 2:
                    dve.wait_ge(gu_done, C * (f - 1))
                nc.vector.tensor_copy(gu_hi[:, f % 2].rearrange("p k w n -> p (k w n)"),
                                      gu_raw.rearrange("p k w n -> p (k w n)")).then_inc(gu_hi_done, 1)

            def split_wd(f):
                dve.wait_ge(wd_loaded, 16 * (f + 1))
                if f >= 3:
                    dve.wait_ge(y_done, NY * ((f - 3) // 2 + 1))
                nc.vector.tensor_copy(wd_hi[:, f % 3], wd_raw).then_inc(wd_hi_done, 1)

            def add_tile(g, i):
                n = tiles[i][1]
                for j in range(2):
                    y = NY * g + 2 * i + j
                    dve.wait_ge(y_done, y + 1)
                    hh = h_all[0:n, i, j * BANK:(j + 1) * BANK]
                    nc.vector.tensor_tensor(hh, ps_y[0:n, y % 4], hh, ALU.add).then_inc(y_added, 1)

            def final_norm(i):
                n = tiles[i][1]
                dve.wait_ge(rstd_done, 2 * (i + 1))
                nc.vector.scalar_tensor_tensor(h_all[0:n, i], h_all[0:n, i], rstd[0:n, i:i + 1], g_sb[0:n],
                                               ALU.mult, ALU.mult).then_inc(y_normed, 1)

            dve.wait_ge(gu_loaded, 32)
            nc.vector.tensor_copy(gu_hi[:, 0, 0:HALF], gu_raw[:, 0:HALF]).then_inc(gu_hi_first, 1)
            nc.vector.tensor_copy(gu_hi[:, 0, HALF:], gu_raw[:, HALF:]).then_inc(gu_hi_done, 1)
            dve.wait_ge(gu_hi_first, 1)
            nc.vector.tensor_tensor(gu_lo[:, 0, 0:HALF], gu_raw[:, 0:HALF], gu_hi[:, 0, 0:HALF].bitcast(F32),
                                    ALU.subtract).then_inc(gu_lo_first, 1)
            split_wd(0)
            split_gu(1)
            for f in range(NF):
                for c, (a, n) in enumerate(chunks):
                    q = C * f + c
                    dve.wait_ge(silu_done, q + 1)
                    if q >= 2:
                        dve.wait_ge(hid_lo, q - 1)
                    nc.vector.tensor_tensor(hidden[:, q % 2, 0:n], ps_u[:, q % 2, 0:n], gate[:, q % 2, 0:n],
                                            ALU.mult).then_inc(hidden_done, 1)
                if f % 2 == 0 and f >= 2:
                    for i in range(NT):
                        add_tile(f // 2 - 1, i)
                if f + 2 < NF:
                    split_gu(f + 2)
                if f + 1 < NF:
                    split_wd(f + 1)
            dve.wait_ge(g_loaded, 16)
            for i in range(NT):
                add_tile(G - 1, i)
                if i >= 1:
                    final_norm(i - 1)
            final_norm(NT - 1)

        @block.tensor
        def _(pe):
            def up(f):
                if f == 0:
                    pe.wait_ge(gu_lo_first, 1)
                else:
                    pe.wait_ge(gu_lo_done, f + 1)
                for c, (a, n) in enumerate(chunks):
                    q = C * f + c
                    if q >= 2:
                        pe.wait_ge(hidden_done, q - 1)
                    for w, ps in ((0, ps_g), (1, ps_u)):
                        out = ps[:, q % 2, 0:n]
                        for k in range(KD):
                            if f == 0 and c == 0 and w == 0 and k == HALF:
                                pe.wait_ge(gu_lo_done, 1)
                            w_h, w_l = gu_hi[:, f % 2, k, w], gu_lo[:, f % 2, k, w]
                            x_h, x_l = nT_hi[:, k, a:a + n], nT_lo[:, k, a:a + n]
                            nc.tensor.matmul(out, w_h, x_h, start=(k == 0), stop=False)
                            nc.tensor.matmul(out, w_h, x_l, start=False, stop=False)
                            last = nc.tensor.matmul(out, w_l, x_h, start=False, stop=(k == KD - 1))
                    last.then_inc(gu_done, 1)

            def down(g):
                pe.wait_ge(hid_lo, C * (2 * g + 2))
                pe.wait_ge(wd_lo_done, 2 * g + 2)
                for i in range(NT):
                    t0, n = tiles[i]
                    for j in range(2):
                        y = NY * g + 2 * i + j
                        if y >= 4:
                            pe.wait_ge(y_added, y - 3)
                        out = ps_y[0:n, y % 4]
                        for f in (2 * g, 2 * g + 1):
                            h_h, h_l = hT_hi[:, f % 3, t0:t0 + n], hT_lo[f % 3][:, t0:t0 + n]
                            b_h, b_l = (x[:, f % 3, j * BANK:(j + 1) * BANK] for x in (wd_hi, wd_lo))
                            nc.tensor.matmul(out, h_h, b_h, start=(f == 2 * g), stop=False)
                            nc.tensor.matmul(out, h_h, b_l, start=False, stop=False)
                            last = nc.tensor.matmul(out, h_l, b_h, start=False, stop=(f == 2 * g + 1))
                        last.then_inc(y_done, 1)

            for f in range(NF):
                up(f)
                if f % 2 == 0 and f >= 2:
                    down(f // 2 - 1)
            down(G - 1)


def encoder_step(nc, t):
    D = t["x_prompt"].shape[1]
    tiles = token_tiles(t["seq"], t["dec"])
    T = t["seq"] + t["dec"]
    with (
        nc.sbuf_tensor("ident", [P, P], F32) as ident,
        nc.sbuf_tensor("neg_half", [P, 4], F32) as neg_half,
        nc.sbuf_tensor("lam", [P, 8], F32) as lam,
        nc.sbuf_tensor("staging", [P, 3 * D], F32) as staging,
        nc.sbuf_tensor("shared", [P, 2 * D * D // P], F32R) as shared,
        nc.semaphore("m_loaded0") as m_loaded0,
        nc.semaphore("m_loaded1") as m_loaded1,
        nc.semaphore("gu_loaded") as gu_loaded,
        nc.semaphore("wd_loaded") as wd_loaded,
    ):
        t.update(ident=ident, neg_half=neg_half, lam=lam, staging=staging, shared=shared)
        half = D // 2
        t["m0"] = staging[:, 0:2 * D].rearrange("p (s n) -> p s n", s=2)
        t["m1"] = staging[:, 2 * D:2 * D + 2 * half].rearrange("p (s n) -> p s n", s=2)
        t["gu_raw"] = staging[:, 0:2 * D].rearrange("p (k w n) -> p k w n", w=2, n=P)
        t["wd_raw"] = staging[:, 2 * D:3 * D]
        t["m_loaded"] = [m_loaded0, m_loaded1]
        t["gu_loaded"], t["wd_loaded"] = gu_loaded, wd_loaded
        t["wo_hi"], t["wo_lo"] = (shared[:, a:a + D * D // P].rearrange("p (k n) -> p k n", n=D)
                                  for a in (0, D * D // P))
        with nc.semaphore("cleared") as cleared, nc.Block() as block:
            @block.gpsimd
            def _(pool):
                nc.gpsimd.memset(ident[:], 0.0).then_inc(cleared, 1)
                nc.gpsimd.memset(neg_half[:], -0.5).then_inc(cleared, 1)
                pool.wait_ge(cleared, 2)
                nc.gpsimd.affine_select(out=ident[:], in_=ident[:], compare_op=ALU.not_equal, fill=1.0, base=0,
                                        pattern=[[-1, P]], channel_multiplier=1).then_inc(cleared, 1)
                pool.wait_ge(cleared, 3)
        project(nc, t)
        attend(nc, t)
        with (
            nc.sbuf_tensor("h_all", [P, len(tiles), D], F32) as h_all,
            nc.sbuf_tensor("n2T_hi", [P, D // P, T], F32R) as nT_hi,
            nc.sbuf_tensor("n2T_lo", [P, D // P, T], F32R) as nT_lo,
        ):
            mix(nc, t, h_all, nT_hi, nT_lo)
            feed(nc, t, h_all, nT_hi, nT_lo)


_INS = ['x_prompt', 'x_sample', 'cache_diff_k', 'cache_diff_v', 'cache_sb_k', 'cache_sb_v', 'norm_attn_g', 'w_in',
        'lambda_q1', 'lambda_k1', 'lambda_q2', 'lambda_k2', 'diff_subln_g', 'w_out', 'norm_ffn_g', 'w_gate', 'w_up',
        'w_down', 'norm_final_g']
_OUTS = ['y_prompt', 'y_sample', 'prompt_diff_k', 'prompt_diff_v', 'prompt_sb_k', 'prompt_sb_v',
         'sample_diff_k', 'sample_diff_v', 'sample_sb_k', 'sample_sb_v']


def kernel(**inputs):
    import numpy as np
    import concourse.bacc as bacc
    from concourse.bass_utils import run_bass_kernel_spmd

    nc = bacc.Bacc("TRN2", target_bir_lowering=False, num_devices=1)
    xp, xs, ck = inputs["x_prompt"], inputs["x_sample"], inputs["cache_diff_k"]
    seq, dec, past, D = xp.shape[1], xs.shape[1], ck.shape[2], xp.shape[2]
    half = D // 2
    two_d = {"x_prompt": (seq, D), "x_sample": (dec, D), "w_in": inputs["w_in"].shape[1:],
             "w_out": inputs["w_out"].shape[1:], "w_gate": inputs["w_gate"].shape[1:],
             "w_up": inputs["w_up"].shape[1:], "w_down": inputs["w_down"].shape[1:]}
    for name in ("cache_diff_k", "cache_diff_v", "cache_sb_k", "cache_sb_v"):
        two_d[name] = (past, half)
    arrays, t = {}, {"seq": seq, "dec": dec, "past": past}
    for name in _INS:
        a = np.ascontiguousarray(np.asarray(inputs[name]))
        a = a.reshape(two_d.get(name, (a.size,)))
        arrays[f"in_{name}"] = a
        t[name] = nc.dram_tensor(f"in_{name}", a.shape, mybir.dt.from_np(a.dtype), kind="ExternalInput").ap()
    out_shapes = {"y_prompt": (seq, D), "y_sample": (dec, D)}
    for name in _OUTS:
        rows = seq if "prompt" in name else dec
        shape = out_shapes.get(name, (rows, half))
        t[name] = nc.dram_tensor(f"out_{name}", shape, F32, kind="ExternalOutput").ap()
    q_d = nc.dram_tensor("q_diff", (seq + dec, half), F32, kind="Internal").ap()
    q_s = nc.dram_tensor("q_sb", (seq + dec, half), F32, kind="Internal").ap()
    t["mixed"] = nc.dram_tensor("mixed", (seq + dec, D), F32, kind="Internal").ap()
    t["mixed1"] = nc.dram_tensor("mixed1", (seq + dec, half), F32, kind="Internal").ap()
    t["new_dq"], t["sample_dq"] = q_d[0:seq, :], q_d[seq:seq + dec, :]
    t["new_sq"], t["sample_sq"] = q_s[0:seq, :], q_s[seq:seq + dec, :]
    for side, name in (("d", "diff"), ("s", "sb")):
        for kind in "kv":
            t[f"new_{side}{kind}"] = t[f"prompt_{name}_{kind}"]
            t[f"sample_{side}{kind}"] = t[f"sample_{name}_{kind}"]
            t[f"cache_{side}{kind}"] = t[f"cache_{name}_{kind}"]
    t["proj_out"] = [(t[f"new_{side}{kind}"], t[f"sample_{side}{kind}"]) for side in "ds" for kind in "qkv"]
    encoder_step(nc, t)
    r = run_bass_kernel_spmd(nc, [arrays], core_ids=[0]).results[0]
    shapes = {"y_prompt": xp.shape, "y_sample": xs.shape}
    out = []
    for name in _OUTS:
        a = r[f"out_{name}"]
        if name not in shapes:
            heads = inputs["cache_diff_k" if "diff" in name else "cache_sb_k"].shape[3:]
            a = a.reshape((1, 1, a.shape[0]) + tuple(heads))
        else:
            a = a.reshape(shapes[name])
        out.append(a)
    return tuple(out)
```
